# Optimizing a Trainium2 kernel written in Bass

```python
import math
import jax
import jax.numpy as jnp
from jax import lax
import numpy as np

D_MODEL = 1024
BATCH = 1
SEQ = 256
DEPTH = 2

N_META = 16
LRU_WIDTH = D_MODEL
LRU_HEADS = 4
LRU_BLOCK = LRU_WIDTH // LRU_HEADS
LRU_C = 8.0
CONV_WIDTH = 4
GDN_HEADS = 8
GDN_HEAD_DIM = 128
GDN_WIDTH = GDN_HEADS * GDN_HEAD_DIM
GDN_CHUNK = 64
AB_SPLITS = (LRU_WIDTH, 2 * LRU_WIDTH, 2 * LRU_WIDTH + 3 * GDN_WIDTH,
             2 * LRU_WIDTH + 4 * GDN_WIDTH, 2 * LRU_WIDTH + 4 * GDN_WIDTH + GDN_HEADS)
AB_IN_COLS = 2 * LRU_WIDTH + 4 * GDN_WIDTH + 2 * GDN_HEADS
AB_MIX_WIDTH = LRU_WIDTH + GDN_WIDTH
S5_GROUP = 16
S5_STATE = 64
S5_GROUPS = D_MODEL // S5_GROUP
N_EXPERTS = 64
TOP_K = 8
N_GROUPS = 8
TOPK_GROUPS = 4
EXPERT_FF = 256
SHARED_FF = 256
ROUTED_SCALE = 2.5
ALPHA = (2.0 * DEPTH) ** 0.25
BETA = (8.0 * DEPTH) ** -0.25
N_EVEN = (DEPTH + 1) // 2
N_ODD = DEPTH // 2
LN_EPS = 1e-5
NORM_EPS = 1e-6

kernel_name = 'hybrid_rglru_gdn_s5_moe_deepnorm'

def _layer_norm(x, g, b):
    x32 = x.astype(jnp.float32)
    mu = jnp.mean(x32, axis=-1, keepdims=True)
    var = jnp.mean(jnp.square(x32 - mu), axis=-1, keepdims=True)
    return ((x32 - mu) * lax.rsqrt(var + LN_EPS) * g.astype(jnp.float32) + b.astype(jnp.float32)).astype(x.dtype)

def _causal_dwconv(x, w):
    k, c = w.shape
    return lax.conv_general_dilated(
        x, w[:, None, :].astype(x.dtype), window_strides=(1,), padding=[(k - 1, 0)],
        dimension_numbers=('NWC', 'WIO', 'NWC'), feature_group_count=c)

def _real_combine(e1, e2):
    a1, b1 = e1
    a2, b2 = e2
    return (a1 * a2, a2 * b1 + b2)

def _complex_combine(e1, e2):
    a1r, a1i, b1r, b1i = e1
    a2r, a2i, b2r, b2i = e2
    return (a1r * a2r - a1i * a2i, a1r * a2i + a1i * a2r,
            a2r * b1r - a2i * b1i + b2r, a2r * b1i + a2i * b1r + b2i)

def _l2norm(t):
    return t * lax.rsqrt(jnp.sum(t * t, axis=-1, keepdims=True) + NORM_EPS)

def _rglru(x, w_r, b_r, w_i, b_i, lam):
    f32 = jnp.float32
    bsz, seq, width = x.shape
    x32 = x.astype(f32)
    xh = x32.reshape(bsz, seq, LRU_HEADS, LRU_BLOCK)
    r = jax.nn.sigmoid(jnp.einsum('blhi,hij->blhj', xh, w_r.astype(f32)).reshape(bsz, seq, width) + b_r.astype(f32))
    i = jax.nn.sigmoid(jnp.einsum('blhi,hij->blhj', xh, w_i.astype(f32)).reshape(bsz, seq, width) + b_i.astype(f32))
    log_a = -LRU_C * r * jax.nn.softplus(-lam.astype(f32))
    a = jnp.exp(log_a)
    b = jnp.sqrt(-jnp.expm1(2.0 * log_a)) * (i * x32)
    _, h = lax.associative_scan(_real_combine, (a, b), axis=1)
    return h.astype(x.dtype)

def _to_chunks(t, n_chunks):
    bsz, _, nh = t.shape[:3]
    t = t.reshape((bsz, n_chunks, GDN_CHUNK, nh) + t.shape[3:])
    return t.transpose((1, 0, 3, 2) + tuple(range(4, t.ndim)))

def _gated_delta_chunked(q, k, v, g, beta):
    bsz, seq, nh, dk = q.shape
    dv = v.shape[-1]
    c = GDN_CHUNK
    front = (-N_META) % c
    back = (-(front + seq)) % c
    pad = lambda t: jnp.pad(t, ((0, 0), (front, back)) + ((0, 0),) * (t.ndim - 2))
    n_chunks = (front + seq + back) // c
    q = _to_chunks(pad(q * dk ** -0.5), n_chunks)
    k = _to_chunks(pad(k), n_chunks)
    v = _to_chunks(pad(v), n_chunks)
    beta = _to_chunks(pad(beta), n_chunks)
    g = jnp.cumsum(_to_chunks(pad(g), n_chunks), axis=-1)
    causal = jnp.tril(jnp.ones((c, c), dtype=bool))
    strict = jnp.tril(jnp.ones((c, c), dtype=bool), -1)
    decay = jnp.exp(jnp.where(causal, g[..., :, None] - g[..., None, :], -jnp.inf))
    kb = k * beta[..., None]
    vb = v * beta[..., None]
    kk = jnp.einsum('nbhcd,nbhsd->nbhcs', kb, k) * decay
    tmat = jnp.where(strict, kk, 0.0) + jnp.eye(c, dtype=q.dtype)
    rhs = jnp.concatenate([vb, kb * jnp.exp(g)[..., None]], axis=-1)
    sol = lax.linalg.triangular_solve(tmat, rhs, left_side=True, lower=True, unit_diagonal=True)
    u, w = sol[..., :dv], sol[..., dv:]
    qk = jnp.einsum('nbhcd,nbhsd->nbhcs', q, k) * decay

    def step(s, xs):
        q_c, k_c, u_c, w_c, g_c, qk_c = xs
        v_new = u_c - jnp.einsum('bhcd,bhde->bhce', w_c, s)
        o = (jnp.einsum('bhcd,bhde->bhce', q_c * jnp.exp(g_c)[..., None], s)
             + jnp.einsum('bhcs,bhse->bhce', qk_c, v_new))
        g_last = g_c[..., -1:]
        s = (s * jnp.exp(g_last)[..., None]
             + jnp.einsum('bhcd,bhce->bhde', k_c * jnp.exp(g_last - g_c)[..., None], v_new))
        return s, o

    s0 = jnp.zeros((bsz, nh, dk, dv), q.dtype)
    _, o = lax.scan(step, s0, (q, k, u, w, g, qk))
    o = o.transpose(1, 0, 3, 2, 4).reshape(bsz, n_chunks * c, nh, dv)
    return o[:, front:front + seq]

def _ab_mixer(h, w_in, conv_w, conv_b, lru_w_r, lru_b_r, lru_w_i, lru_b_i, lru_lambda,
              gdn_conv_w, gdn_a_log, gdn_dt_bias, gdn_norm_w, w_out):
    f32 = jnp.float32
    bsz, seq, _ = h.shape
    proj = jnp.einsum('bld,dc->blc', h, w_in)
    gate_a, x_a, qkv, z, beta_logit, decay_logit = jnp.split(proj, AB_SPLITS, axis=-1)
    xa = _causal_dwconv(x_a, conv_w) + conv_b.astype(x_a.dtype)
    y_a = jax.nn.gelu(gate_a) * _rglru(xa, lru_w_r, lru_b_r, lru_w_i, lru_b_i, lru_lambda)
    qkv = jax.nn.silu(_causal_dwconv(qkv, gdn_conv_w)).astype(f32).reshape(bsz, seq, 3, GDN_HEADS, GDN_HEAD_DIM)
    q = _l2norm(qkv[:, :, 0])
    k = _l2norm(qkv[:, :, 1])
    v = qkv[:, :, 2]
    beta = jax.nn.sigmoid(beta_logit.astype(f32))
    g = -jnp.exp(gdn_a_log.astype(f32)) * jax.nn.softplus(decay_logit.astype(f32) + gdn_dt_bias.astype(f32))
    o = _gated_delta_chunked(q, k, v, g, beta)
    zg = jax.nn.silu(z.astype(f32).reshape(bsz, seq, GDN_HEADS, GDN_HEAD_DIM))
    o = o * lax.rsqrt(jnp.mean(o * o, axis=-1, keepdims=True) + NORM_EPS) * gdn_norm_w.astype(f32) * zg
    y_b = o.reshape(bsz, seq, GDN_WIDTH).astype(h.dtype)
    return jnp.einsum('blc,cd->bld', jnp.concatenate([y_a, y_b], axis=-1), w_out)

def _s5_mixer(h, lam_re, lam_im, log_dt, b_re, b_im, c_re, c_im, d_skip, w_out):
    f32 = jnp.float32
    bsz, seq, dm = h.shape
    u = h.astype(f32).reshape(bsz, seq, S5_GROUPS, S5_GROUP)
    lr = jnp.minimum(lam_re.astype(f32), -1e-4)
    li = lam_im.astype(f32)
    dt = jnp.exp(log_dt.astype(f32))[:, None]
    mag = jnp.exp(lr * dt)
    ab_re = mag * jnp.cos(li * dt)
    ab_im = mag * jnp.sin(li * dt)
    den = lr * lr + li * li
    nr = ab_re - 1.0
    cf_re = (nr * lr + ab_im * li) / den
    cf_im = (ab_im * lr - nr * li) / den
    br = b_re.astype(f32)
    bi = b_im.astype(f32)
    bb_re = cf_re[..., None] * br - cf_im[..., None] * bi
    bb_im = cf_re[..., None] * bi + cf_im[..., None] * br
    bu_re = jnp.einsum('blgj,gpj->blgp', u, bb_re)
    bu_im = jnp.einsum('blgj,gpj->blgp', u, bb_im)
    a_re = jnp.broadcast_to(ab_re, (1, seq, S5_GROUPS, S5_STATE))
    a_im = jnp.broadcast_to(ab_im, (1, seq, S5_GROUPS, S5_STATE))
    _, _, s_re, s_im = lax.associative_scan(_complex_combine, (a_re, a_im, bu_re, bu_im), axis=1)
    y = (jnp.einsum('blgp,gjp->blgj', s_re, c_re.astype(f32))
         - jnp.einsum('blgp,gjp->blgj', s_im, c_im.astype(f32)))
    y = y.reshape(bsz, seq, dm) + d_skip.astype(f32) * h.astype(f32)
    y = jax.nn.gelu(y).astype(h.dtype)
    val, gate = jnp.split(jnp.einsum('bld,dc->blc', y, w_out), 2, axis=-1)
    return val * jax.nn.sigmoid(gate)

def _moe_ffn(h, w_router, router_bias, w_gate, w_up, w_down, sh_gate, sh_up, sh_down):
    f32 = jnp.float32
    bsz, seq, _ = h.shape
    scores = jax.nn.sigmoid(jnp.einsum('bld,de->ble', h, w_router).astype(f32))
    biased = scores + router_bias.astype(f32)
    grouped = biased.reshape(bsz, seq, N_GROUPS, N_EXPERTS // N_GROUPS)
    group_score = jnp.sum(lax.top_k(grouped, 2)[0], axis=-1)
    _, group_idx = lax.top_k(group_score, TOPK_GROUPS)
    group_mask = jnp.sum(jax.nn.one_hot(group_idx, N_GROUPS, dtype=f32), axis=-2)
    expert_mask = jnp.repeat(group_mask, N_EXPERTS // N_GROUPS, axis=-1) > 0
    _, idx = lax.top_k(jnp.where(expert_mask, biased, -jnp.inf), TOP_K)
    w = jnp.take_along_axis(scores, idx, axis=-1)
    w = ROUTED_SCALE * w / jnp.sum(w, axis=-1, keepdims=True)
    gates = jnp.einsum('blk,blke->ble', w, jax.nn.one_hot(idx, N_EXPERTS, dtype=f32)).astype(h.dtype)

    def routed_row(args):
        hr, gr = args
        act = jax.nn.silu(jnp.einsum('ld,edf->lef', hr, w_gate)) * jnp.einsum('ld,edf->lef', hr, w_up)
        return jnp.einsum('lef,efd->ld', act * gr[..., None], w_down)

    routed = lax.map(routed_row, (h, gates))
    shared = jnp.einsum('blf,fd->bld', jax.nn.silu(h @ sh_gate) * (h @ sh_up), sh_down)
    return routed + shared

def setup_inputs(seed: int = 0) -> dict:
    key = jax.random.key(seed)
    ks = list(jax.random.split(key, 36))
    f32 = jnp.float32
    D = D_MODEL
    ne, no = N_EVEN, N_ODD
    nrm = lambda k, shape, std: jax.random.normal(k, shape, f32) * std
    x = nrm(ks[0], (BATCH, SEQ, D), 1.0)
    meta_tokens = nrm(ks[1], (N_META, D), 1.0)
    col_scale = jnp.concatenate([
        jnp.ones((LRU_WIDTH,), f32), jnp.full((LRU_WIDTH,), BETA, f32),
        jnp.ones((2 * GDN_WIDTH,), f32), jnp.full((GDN_WIDTH,), BETA, f32),
        jnp.ones((GDN_WIDTH + 2 * GDN_HEADS,), f32)])
    ab_w_in = nrm(ks[2], (ne, D, AB_IN_COLS), D ** -0.5) * col_scale
    ab_conv_w = nrm(ks[3], (ne, CONV_WIDTH, LRU_WIDTH), CONV_WIDTH ** -0.5)
    ab_conv_b = nrm(ks[4], (ne, LRU_WIDTH), 0.01)
    lru_w_r = nrm(ks[5], (ne, LRU_HEADS, LRU_BLOCK, LRU_BLOCK), LRU_BLOCK ** -0.5)
    lru_b_r = nrm(ks[6], (ne, LRU_WIDTH), 0.1)
    lru_w_i = nrm(ks[7], (ne, LRU_HEADS, LRU_BLOCK, LRU_BLOCK), LRU_BLOCK ** -0.5)
    lru_b_i = nrm(ks[8], (ne, LRU_WIDTH), 0.1)
    a_root = jax.random.uniform(ks[9], (ne, LRU_WIDTH), f32, 0.9, 0.999) ** (1.0 / LRU_C)
    lru_lambda = jnp.log(a_root) - jnp.log1p(-a_root)
    gdn_conv_w = nrm(ks[10], (ne, CONV_WIDTH, 3 * GDN_WIDTH), CONV_WIDTH ** -0.5)
    gdn_a_log = jnp.log(jax.random.uniform(ks[11], (ne, GDN_HEADS), f32, 1.0, 16.0))
    dt0 = jnp.exp(jax.random.uniform(ks[12], (ne, GDN_HEADS), f32, math.log(1e-3), math.log(1e-1)))
    gdn_dt_bias = dt0 + jnp.log(-jnp.expm1(-dt0))
    gdn_norm_w = 1.0 + nrm(ks[13], (ne, GDN_HEAD_DIM), 0.05)
    ab_w_out = nrm(ks[14], (ne, AB_MIX_WIDTH, D), AB_MIX_WIDTH ** -0.5 * BETA)
    s5_lambda_re = -0.5 * jnp.exp(nrm(ks[15], (no, S5_GROUPS, S5_STATE), 0.05))
    s5_lambda_im = math.pi * jnp.arange(S5_STATE, dtype=f32) + nrm(ks[16], (no, S5_GROUPS, S5_STATE), 0.05)
    s5_log_dt = jax.random.uniform(ks[17], (no, S5_GROUPS), f32, math.log(1e-3), math.log(1e-1))
    s5_b_re = nrm(ks[18], (no, S5_GROUPS, S5_STATE, S5_GROUP), (2 * S5_GROUP) ** -0.5)
    s5_b_im = nrm(ks[19], (no, S5_GROUPS, S5_STATE, S5_GROUP), (2 * S5_GROUP) ** -0.5)
    s5_c_re = nrm(ks[20], (no, S5_GROUPS, S5_GROUP, S5_STATE), S5_STATE ** -0.5)
    s5_c_im = nrm(ks[21], (no, S5_GROUPS, S5_GROUP, S5_STATE), S5_STATE ** -0.5)
    s5_d = nrm(ks[22], (no, D), 0.5)
    out_scale = jnp.concatenate([jnp.full((D,), BETA, f32), jnp.ones((D,), f32)])
    s5_w_out = nrm(ks[23], (no, D, 2 * D), D ** -0.5) * out_scale
    moe_w_router = nrm(ks[24], (DEPTH, D, N_EXPERTS), D ** -0.5)
    moe_router_bias = nrm(ks[25], (DEPTH, N_EXPERTS), 0.01)
    moe_w_gate = nrm(ks[26], (DEPTH, N_EXPERTS, D, EXPERT_FF), D ** -0.5)
    moe_w_up = nrm(ks[27], (DEPTH, N_EXPERTS, D, EXPERT_FF), D ** -0.5)
    moe_w_down = nrm(ks[28], (DEPTH, N_EXPERTS, EXPERT_FF, D), EXPERT_FF ** -0.5 * BETA)
    moe_shared_w_gate = nrm(ks[29], (DEPTH, D, SHARED_FF), D ** -0.5)
    moe_shared_w_up = nrm(ks[30], (DEPTH, D, SHARED_FF), D ** -0.5)
    moe_shared_w_down = nrm(ks[31], (DEPTH, SHARED_FF, D), SHARED_FF ** -0.5 * BETA)
    ln_mix_g = 1.0 + nrm(ks[32], (DEPTH, D), 0.02)
    ln_mix_b = nrm(ks[33], (DEPTH, D), 0.02)
    ln_ffn_g = 1.0 + nrm(ks[34], (DEPTH, D), 0.02)
    ln_ffn_b = nrm(ks[35], (DEPTH, D), 0.02)
    return {
        'x': x, 'meta_tokens': meta_tokens,
        'ab_w_in': ab_w_in, 'ab_conv_w': ab_conv_w, 'ab_conv_b': ab_conv_b,
        'lru_w_r': lru_w_r, 'lru_b_r': lru_b_r, 'lru_w_i': lru_w_i, 'lru_b_i': lru_b_i,
        'lru_lambda': lru_lambda, 'gdn_conv_w': gdn_conv_w, 'gdn_a_log': gdn_a_log,
        'gdn_dt_bias': gdn_dt_bias, 'gdn_norm_w': gdn_norm_w, 'ab_w_out': ab_w_out,
        's5_lambda_re': s5_lambda_re, 's5_lambda_im': s5_lambda_im, 's5_log_dt': s5_log_dt,
        's5_b_re': s5_b_re, 's5_b_im': s5_b_im, 's5_c_re': s5_c_re, 's5_c_im': s5_c_im,
        's5_d': s5_d, 's5_w_out': s5_w_out,
        'moe_w_router': moe_w_router, 'moe_router_bias': moe_router_bias,
        'moe_w_gate': moe_w_gate, 'moe_w_up': moe_w_up, 'moe_w_down': moe_w_down,
        'moe_shared_w_gate': moe_shared_w_gate, 'moe_shared_w_up': moe_shared_w_up,
        'moe_shared_w_down': moe_shared_w_down,
        'ln_mix_g': ln_mix_g, 'ln_mix_b': ln_mix_b, 'ln_ffn_g': ln_ffn_g, 'ln_ffn_b': ln_ffn_b,
    }

def reference(x, meta_tokens, ab_w_in, ab_conv_w, ab_conv_b, lru_w_r, lru_b_r, lru_w_i, lru_b_i,
              lru_lambda, gdn_conv_w, gdn_a_log, gdn_dt_bias, gdn_norm_w, ab_w_out,
              s5_lambda_re, s5_lambda_im, s5_log_dt, s5_b_re, s5_b_im, s5_c_re, s5_c_im, s5_d, s5_w_out,
              moe_w_router, moe_router_bias, moe_w_gate, moe_w_up, moe_w_down,
              moe_shared_w_gate, moe_shared_w_up, moe_shared_w_down,
              ln_mix_g, ln_mix_b, ln_ffn_g, ln_ffn_b):
    bsz = x.shape[0]
    meta = jnp.broadcast_to(meta_tokens.astype(x.dtype)[None], (bsz, N_META, D_MODEL))
    h = jnp.concatenate([meta, x], axis=1)
    for layer in range(DEPTH):
        j = layer // 2
        if layer % 2 == 0:
            mix = _ab_mixer(h, ab_w_in[j], ab_conv_w[j], ab_conv_b[j], lru_w_r[j], lru_b_r[j],
                            lru_w_i[j], lru_b_i[j], lru_lambda[j], gdn_conv_w[j], gdn_a_log[j],
                            gdn_dt_bias[j], gdn_norm_w[j], ab_w_out[j])
        else:
            mix = _s5_mixer(h, s5_lambda_re[j], s5_lambda_im[j], s5_log_dt[j], s5_b_re[j], s5_b_im[j],
                            s5_c_re[j], s5_c_im[j], s5_d[j], s5_w_out[j])
        h = _layer_norm(ALPHA * h + mix, ln_mix_g[layer], ln_mix_b[layer])
        ffn = _moe_ffn(h, moe_w_router[layer], moe_router_bias[layer], moe_w_gate[layer], moe_w_up[layer],
                       moe_w_down[layer], moe_shared_w_gate[layer], moe_shared_w_up[layer],
                       moe_shared_w_down[layer])
        h = _layer_norm(ALPHA * h + ffn, ln_ffn_g[layer], ln_ffn_b[layer])
    return h[:, N_META:]


_drawn_inputs = setup_inputs


def setup_inputs(seed=0):
    import zlib

    import numpy as np

    out = dict(_drawn_inputs(seed))
    spreads = {}
    factors = {'lru_b_r': 8.0,
     'lru_b_i': 6.6,
     's5_lambda_re': 64.0,
     's5_log_dt': 14.766,
     's5_b_im': 12.143,
     's5_c_re': 23.925,
     's5_c_im': 22.253,
     's5_lambda_im': 7.873,
     's5_b_re': 8.0}
    for name, (base, spread) in spreads.items():
        noise = np.random.default_rng([zlib.crc32(name.encode()), seed]).standard_normal(out[name].shape)
        drawn = base * np.exp(spread * noise) if base else spread * noise
        out[name] = jnp.asarray(drawn.astype(out[name].dtype))
    for name, factor in factors.items():
        out[name] = (out[name] * factor).astype(out[name].dtype)
    return out
```

```python
import math
from contextlib import ExitStack

import numpy as np

import concourse.bass as bass
from concourse import mybir

ALU = mybir.AluOpType
ACT = mybir.ActivationFunctionType
AX_X = mybir.AxisListType.X
F32 = mybir.dt.float32
I32 = mybir.dt.int32
U32 = mybir.dt.uint32

P = 128
D = 1024
META = 16
SEQ = 256
T = META + SEQ
DC = D // P
DEPTH = 2
ALPHA = (2.0 * DEPTH) ** 0.25
LN_EPS = 1e-5
NORM_EPS = 1e-6

HEADS = 8
CONV = 4
IN_COLS = 6 * D + 2 * HEADS
CHUNKS = ((0, META), (META, P), (META + P, P))
LEVELS = 7

STATES = 64
S5_TILES = 32

E = 64
PAIRS = E // 2
FF = 256
FC = FF // P
SLOTS = 64
TOP = 8
GROUPS = 8
TOP_GROUPS = 4
SCALE = 2.5
TILES = ((0, P), (P, P), (2 * P, META))
BLOCK = 512
LOG1P_TERMS = 9


class Chain:

    def __init__(self, eng, sem):
        self.eng, self.sem, self.n = eng, sem, 0

    def done(self, ins):
        ins.then_inc(self.sem, 1)
        self.n += 1
        self.eng.wait_ge(self.sem, self.n)


class Signals:

    def __init__(self, nc, prefix=""):
        self.nc, self.prefix, self.held = nc, prefix, []

    def __enter__(self):
        return self

    def __call__(self, name):
        self.held.append(self.nc.alloc_semaphore(self.prefix + name))
        return self.held[-1]

    def __exit__(self, *failed):
        if not failed[0]:
            self.nc.clear_and_free_semaphores(self.held)
            self.nc.all_engine_barrier()


def log1p_steps(v, link, out, e, z, z2):
    link(v.tensor_scalar_add(z, e, 2.0))
    link(v.reciprocal(z, z))
    link(v.tensor_tensor(z, z, e, ALU.mult))
    link(v.tensor_tensor(z2, z, z, ALU.mult))
    link(v.memset(out, 1.0 / (2 * LOG1P_TERMS + 1)))
    for k in range(LOG1P_TERMS - 1, -1, -1):
        link(v.tensor_tensor(out, out, z2, ALU.mult))
        link(v.tensor_scalar_add(out, out, 1.0 / (2 * k + 1)))
    link(v.scalar_tensor_tensor(out=out, in0=out, scalar=2.0, in1=z, op0=ALU.mult, op1=ALU.mult))


def in_projection(nc, k, ctx, mem):
    cols = [3 * D, 3 * D + BLOCK, 2 * D, 2 * D + BLOCK, 4 * D, 4 * D + BLOCK, 5 * D, 5 * D + BLOCK,
            D, D + BLOCK, 0, BLOCK]
    per = BLOCK // P
    N_CONV = 32
    conv_of = {n: n for n in range(24)} | {n: n - 8 for n in range(32, 40)}
    conv_w, conv_b, w_bd = mem["conv_w"], mem["conv_b"], mem["w_bd"]
    qkv, xa, y, bd = mem["qkv"], mem["xa"], mem["y"], mem["bd"]
    hT, ring = mem["hT"], mem["dense"]
    with ExitStack() as inner:
        sem = inner.enter_context(Signals(nc))
        cin = inner.enter_context(nc.sbuf_tensor("cin", [P, 4, T + CONV - 1], F32))
        ps = [inner.enter_context(nc.psum_tensor(f"proj{b}", [P, BLOCK], F32)) for b in range(4)]
        loaded = sem("inproj_loaded")
        w_ready = [sem("w_in_even_ready"), sem("w_in_odd_ready")]
        proj_done, evacuated, pads_zero = sem("proj_done"), sem("proj_evacuated"), sem("pads_zero")
        conv_done, conv_step, silu_done = sem("conv_done"), sem("conv_step"), sem("silu_done")
        w_in = k["w_in"].rearrange("(c p) n -> p c n", p=P)
        with nc.Block(no_gpsimd_drain=True) as block:

            @block.sync
            def _(sp):
                sp.dma_start(hT[:], k["h0T"]).then_inc(loaded, 16)
                sp.dma_start(w_bd[:], w_in[:, :, 6 * D:]).then_inc(loaded, 16)
                for b, c0 in enumerate(cols):
                    if b >= 2:
                        sp.wait_ge(proj_done, 2 + per * (b - 1))
                    sp.dma_start(ring[:, b % 2], w_in[:, :, c0:c0 + BLOCK]).then_inc(w_ready[b % 2], 16)
                    if b == 0:
                        sp.dma_start(conv_w[:], k["conv_w"]).then_inc(loaded, 16)
                        sp.dma_start(conv_b[:], k["conv_b"]).then_inc(loaded, 16)
                        for name in ("ident", "offmask", "causal", "sel8", "lru_b", "lru_lam", "head_par", "norm_w",
                                     "ln_par", "eps"):
                            sp.dma_start(mem[name][:], k[name]).then_inc(mem["consts_loaded"], 16)

            @block.tensor
            def _(pe):
                pe.wait_ge(loaded, 32 + 32)
                for g in range(2):
                    for c in range(DC):
                        mm = pe.matmul(ps[g][0:HEADS, 0:T], w_bd[:, c, HEADS * g:HEADS * (g + 1)], hT[:, c, :],
                                       start=(c == 0), stop=(c == DC - 1))
                    mm.then_inc(proj_done, 1)
                for n in range(per * len(cols)):
                    g, b = n + 2, n // per
                    if n % per == 0:
                        pe.wait_ge(w_ready[b % 2], 16 * (b // 2 + 1))
                    if g >= 4:
                        pe.wait_ge(evacuated, g - 3)
                    j = n % per
                    for c in range(DC):
                        mm = pe.matmul(ps[g % 4][:, 0:T], ring[:, b % 2, c, j * P:(j + 1) * P], hT[:, c, :],
                                       start=(c == 0), stop=(c == DC - 1))
                    mm.then_inc(proj_done, 1)

            @block.scalar
            def _(act):
                def silu(n):
                    act.wait_ge(conv_done, n + 1)
                    act.activation(qkv[:, n, :], qkv[:, n, :], ACT.Silu).then_inc(silu_done, 1)

                for g in range(2):
                    act.wait_ge(proj_done, g + 1)
                    act.copy(bd[:, g, :], ps[g][0:HEADS, 0:T]).then_inc(evacuated, 1)
                act.wait_ge(pads_zero, 1)
                for n in range(per * len(cols)):
                    src = ps[(n + 2) % 4][:, 0:T]
                    act.wait_ge(proj_done, n + 3)
                    if n in conv_of:
                        cs = conv_of[n]
                        if cs >= 4:
                            act.wait_ge(conv_done, cs - 3)
                        act.copy(cin[:, cs % 4, CONV - 1:], src).then_inc(evacuated, 1)
                    elif n < 32:
                        act.activation(y[:, n - 24 + DC, :], src, ACT.Silu).then_inc(evacuated, 1)
                    else:
                        act.activation(y[:, n - 40, :], src, ACT.Gelu_apprx_tanh).then_inc(evacuated, 1)
                    if 2 <= n < 26:
                        silu(n - 2)

            @block.vector
            def _(dve):
                step = Chain(dve, conv_step)
                dve.memset(cin[:, :, 0:CONV - 1], 0.0).then_inc(pads_zero, 1)
                dve.wait_ge(pads_zero, 1)
                dve.wait_ge(loaded, 64)
                for n, cs in conv_of.items():
                    dve.wait_ge(evacuated, n + 3)
                    src, dst = cin[:, cs % 4, :], qkv[:, n, :] if n < 24 else xa[:, n - 32, :]
                    w = lambda j: conv_w[:, cs, j:j + 1]
                    if n < 24:
                        step.done(dve.tensor_scalar(dst, src[:, 0:T], w(0), None, ALU.mult))
                    else:
                        step.done(dve.tensor_scalar(dst, src[:, 0:T], w(0), conv_b[:, n - 32:n - 31],
                                                    ALU.mult, ALU.add))
                    for j in (1, 2):
                        step.done(dve.scalar_tensor_tensor(out=dst, in0=src[:, j:j + T], scalar=w(j), in1=dst,
                                                           op0=ALU.mult, op1=ALU.add))
                    dve.scalar_tensor_tensor(out=dst, in0=src[:, 3:3 + T], scalar=w(3), in1=dst,
                                             op0=ALU.mult, op1=ALU.add).then_inc(conv_done, 1)


def group_mixers(nc, k, ctx, mem):
    qkv, xa, y, bd, ring = mem["qkv"], mem["xa"], mem["y"], mem["bd"], mem["dense"]
    ident, offmask, causal, sel8, ones = mem["ident"], mem["offmask"], mem["causal"], mem["sel8"], mem["ones"]
    keys, queries, values = qkv[:, 0:8, :], qkv[:, 8:16, :], qkv[:, 16:24, :]
    NQ = 4
    SETS = [(1, 0, 4), (1, 4, 4), (2, 0, 4), (2, 4, 4), (0, 0, 8)]
    with ExitStack() as inner:
        sem = inner.enter_context(Signals(nc))
        sb = lambda name, shape: inner.enter_context(nc.sbuf_tensor(name, shape, F32))
        bank = [inner.enter_context(nc.psum_tensor(f"mix{b}", [P, BLOCK], F32)) for b in range(8)]
        gates = sb("gates", [P, 2 * DC, T])
        kdec = sb("kdec", [P, 3, HEADS * P])
        vbeta = sb("vbeta", [P, 3, HEADS * P])
        lru_t = vbeta[:].rearrange("p a b -> p (a b)")[:, 0:DC * T].rearrange("p (c t) -> p c t", c=DC)
        lru_u = kdec[:].rearrange("p a b -> p (a b)")[:, 0:DC * T].rearrange("p (c t) -> p c t", c=DC)
        gb = sb("g_rows", [P, HEADS, T])
        kb_o = sb("kb_then_o", [P, HEADS, T])
        sq = sb("squares", [P, 2, T])
        nrm = sb("norms", [P, 2, T])
        LT = sb("LT", [P, 5, 4, P])
        X = sb("X", [P, 4, 4, P])
        Y = sb("Y", [P, 4, 4, P])
        QK = sb("QK", [P, 4, 4, P])
        X0, Y0, QK0 = (sb(n, [META, HEADS, META]) for n in ("X0", "Y0", "QK0"))
        T1, LTo, r, vn = (ring[:, 1, 2 * i:2 * i + 2, :] for i in range(4))
        S = gates[:].rearrange("p c t -> p (c t)")[:, 0:HEADS * P].rearrange("p (h d) -> p h d", h=HEADS)
        colg, colb, kd, egl, nbeg = (sb(n, [P, 3, HEADS]) for n in ("colg", "colb", "kd", "egl", "nbeg"))
        bt = sb("small", [HEADS, 2, T])
        c8, l8 = sb("c8", [P, DC]), sb("l8", [P, 4, DC])
        ea = sb("ea", [HEADS, 1])
        beta, G = bt[:, 0, :], bt[:, 1, :]
        s0, s1, s2, s3 = (kb_o[0:HEADS, i, :] for i in range(4))

        lru_w_ready, w_ready = sem("lru_w_ready"), sem("spare_w")
        s_sq, s_sum, s_nrm, s_qkn = sem("squared"), sem("sums_ready"), sem("norm_ready"), sem("qk_normed")
        s_lg, s_gate = sem("lru_gates_ready"), sem("gates_done")
        act_step, dve_step, pool_step = sem("act_step"), sem("dve_step"), sem("pool_step")
        s_beta, s_x, s_exp, s_ea, s_G = sem("beta_done"), sem("decay_abs"), sem("decay_exp"), sem("ea"), sem("G_done")
        s_lame, s_c8 = sem("lam_exp"), sem("c8_done")
        s_th, s_m, s_sqrt, s_u, s_b, s_scan, s_y = (sem(n) for n in ("tanh_a", "lru_m", "lru_sqrt", "lru_ix",
                                                                     "lru_b_done", "lru_scan", "lru_y"))
        s_bc, s_gb, s_eg, s_kb, s_qg = (sem(n) for n in ("bcast_ready", "g_rows_done", "eg_done", "kb_done", "qg_done"))
        s_col, s_colc, s_kdx, s_kde, s_nb = (sem(n) for n in ("cols_ready", "cols_done", "kd_diff", "kd_exp", "nbeg"))
        s_tt, s_tok = sem("tok_ready"), sem("tok_done")
        s_diff, s_dexp, s_mask, s_kk, s_lt = (sem(n) for n in ("diff", "decay_mat", "decay_masked", "kk_ready", "lt_done"))
        s_lto, s_t1, s_t1c, s_pq, s_x2 = (sem(n) for n in ("lt_off", "t1_ready", "t1_done", "pq_ready", "xy_done"))
        s_init = sem("xy_init")
        s_ks, s_r, s_vn, s_vnc, s_o, s_oc, s_s, s_sc = (sem(n) for n in (
            "ks_ready", "rhs_done", "vnew_ready", "vnew_done", "o_ready", "o_done", "s_ready", "s_done"))
        s_osq, s_osum, s_on, s_of = (sem(n) for n in ("o_squared", "o_sums", "o_norm", "o_final"))
        lru_w = ring[:, 0].rearrange("p c n -> p (c n)").rearrange("p (g h q n) -> p g h q n", g=2, h=4, q=2)

        n_lv = lambda s: LEVELS if s < 4 else 4
        work = [(lv, s) for lv in range(LEVELS) for s in range(5) if lv < n_lv(s)]
        place = {w: i for i, w in enumerate(work)}
        rec = [(cc, half) for cc in range(3) for half in range(2)]

        with nc.Block(no_gpsimd_drain=True) as block:

            @block.sync
            def _(sp):
                sp.dma_start(ring[:, 0], k["lru_w"]).then_inc(lru_w_ready, 16)

            @block.tensor
            def _(pe):
                for i in range(16):
                    pe.wait_ge(s_sq, i + 1)
                    if i >= 2:
                        pe.wait_ge(s_nrm, i - 1)
                    pe.matmul(bank[i % 2][:, 0:T], ones[:], sq[:, i % 2, :], start=True, stop=True).then_inc(s_sum, 1)
                pe.wait_ge(lru_w_ready, 16)
                for i in range(16):
                    g, m = i // 8, i % 8
                    if i >= 2:
                        pe.wait_ge(s_gate, i - 1)
                    for q in range(2):
                        mm = pe.matmul(bank[2 + i % 2][:, 0:T], lru_w[:, g, m // 2, q, (m % 2) * P:(m % 2 + 1) * P],
                                       xa[:, 2 * (m // 2) + q, :], start=(q == 0), stop=(q == 1))
                    mm.then_inc(s_lg, 1)
                pe.wait_ge(s_G, 1)
                pe.wait_ge(s_beta, 1)
                for h in range(HEADS):
                    if h >= 2:
                        pe.wait_ge(s_gb, h - 1)
                        pe.wait_ge(s_kb, h - 1)
                    o = 4 + 2 * (h % 2)
                    pe.matmul(bank[o][:, 0:T], sel8[:, h, :], G, start=True, stop=True).then_inc(s_bc, 1)
                    pe.matmul(bank[o + 1][:, 0:T], sel8[:, h, :], beta, start=True, stop=True).then_inc(s_bc, 1)
                pe.wait_ge(s_nrm, 16)
                for cc, (t0, n) in enumerate(CHUNKS):
                    for q, row in enumerate((G, beta)):
                        mm = pe.transpose(bank[0][0:n, (2 * cc + q) * HEADS:(2 * cc + q + 1) * HEADS],
                                          row[:, t0:t0 + n], ident[0:HEADS, 0:HEADS])
                mm.then_inc(s_col, 1)
                pe.wait_ge(s_gate, 16)
                pe.wait_ge(s_colc, 2)
                pe.wait_ge(s_qkn, 16)
                for i in range(12):
                    cc, q, half = i // 4, i // 2 % 2, i % 2
                    t0, n = CHUNKS[cc]
                    if i >= 4:
                        pe.wait_ge(s_tok, i - 3)
                    for h in range(4):
                        src = (keys, values)[q]
                        mm = pe.transpose(bank[i % 4][0:n, h * P:(h + 1) * P], src[:, 4 * half + h, t0:t0 + n], ident[:])
                    mm.then_inc(s_tt, 1)
                pe.wait_ge(s_kb, HEADS)
                pe.wait_ge(s_gb, HEADS)
                for s, (cc, h0, nh) in enumerate(SETS):
                    t0, n = CHUNKS[cc]
                    if s >= 2:
                        pe.wait_ge(s_lt, 2 * (s - 1))
                    o = 4 + 2 * (s % 2)
                    for q, rhs in enumerate((kb_o, queries)):
                        for h in range(nh):
                            mm = pe.matmul(bank[o + q][0:n, h * n:(h + 1) * n], keys[:, h0 + h, t0:t0 + n],
                                           rhs[:, h0 + h, t0:t0 + n], start=True, stop=True)
                        mm.then_inc(s_kk, 1)
                pe.wait_ge(s_tok, 12)
                pe.wait_ge(s_lt, 10)

                def off_times_x(i):
                    lv, s = work[i]
                    cc, h0, nh = SETS[s]
                    n = CHUNKS[cc][1]
                    pe.wait_ge(s_lto, i + 1)
                    if lv > 0:
                        pe.wait_ge(s_x2, 2 * (place[(lv - 1, s)] + 1))
                    if i >= 2:
                        pe.wait_ge(s_t1c, i - 1)
                    for h in range(nh):
                        lto = LTo[0:n, i % 2, h * n:(h + 1) * n]
                        rhs = ident[0:n, 0:n] if lv == 0 else (X[:, s, h, :] if s < 4 else X0[:, h, :])
                        mm = pe.matmul(bank[i % 2][0:n, h * n:(h + 1) * n], lto, rhs, start=True, stop=True)
                    mm.then_inc(s_t1, 1)

                def products(i):
                    lv, s = work[i]
                    if lv == 0:
                        return
                    cc, h0, nh = SETS[s]
                    n = CHUNKS[cc][1]
                    pe.wait_ge(s_t1c, i + 1)
                    if i >= 2:
                        pe.wait_ge(s_x2, 2 * (i - 1))
                    o = 2 + 2 * (i % 2)
                    for q in range(2):
                        for h in range(nh):
                            t1 = T1[0:n, i % 2, h * n:(h + 1) * n]
                            yy = Y[:, s, h, :] if s < 4 else Y0[:, h, :]
                            a, b = (yy, t1) if q == 0 else (t1, yy)
                            mm = pe.matmul(bank[o + q][0:n, h * n:(h + 1) * n], a, b, start=True, stop=True)
                        mm.then_inc(s_pq, 1)

                for i in range(len(work) + 1):
                    if i < len(work):
                        off_times_x(i)
                    if i >= 1:
                        products(i - 1)
                pe.wait_ge(s_x2, 2 * len(work))
                pe.wait_ge(s_qg, 1)
                pe.wait_ge(s_nb, 1)

                def solve_rhs(i):
                    cc, half = rec[i]
                    t0, n = CHUNKS[cc]
                    if cc > 0:
                        pe.wait_ge(s_sc, i - 1)
                        for h in range(4):
                            mm = pe.matmul(bank[half][:, h * P:(h + 1) * P], keys[:, 4 * half + h, t0:t0 + n],
                                           S[:, 4 * half + h, :], start=True, stop=True)
                        mm.then_inc(s_ks, 1)

                def new_values(i):
                    cc, half = rec[i]
                    t0, n = CHUNKS[cc]
                    if cc > 0:
                        pe.wait_ge(s_r, i - 1)
                    if i >= 2:
                        pe.wait_ge(s_vnc, i - 1)
                    for h in range(4):
                        hh = 4 * half + h
                        if cc > 0:
                            yy, rhs = Y[:, 2 * (cc - 1) + half, h, :], r[:, half, h * P:(h + 1) * P]
                        else:
                            yy, rhs = Y0[:, hh, :], vbeta[0:n, 0, hh * P:(hh + 1) * P]
                        mm = pe.matmul(bank[2 + half][0:n, h * P:(h + 1) * P], yy, rhs, start=True, stop=True)
                    mm.then_inc(s_vn, 1)

                def outputs(i):
                    cc, half = rec[i]
                    t0, n = CHUNKS[cc]
                    pe.wait_ge(s_vnc, i + 1)
                    if i >= 2:
                        pe.wait_ge(s_oc, i - 1)
                    for h in range(4):
                        hh = 4 * half + h
                        out = bank[4 + half][:, h * n:(h + 1) * n]
                        v = vn[0:n, half, h * P:(h + 1) * P]
                        qk = QK[:, 2 * (cc - 1) + half, h, :] if cc > 0 else QK0[:, hh, :]
                        if cc > 0:
                            pe.matmul(out, S[:, hh, :], queries[:, hh, t0:t0 + n], start=True, stop=False)
                        mm = pe.matmul(out, v, qk, start=(cc == 0), stop=True)
                    mm.then_inc(s_o, 1)
                    if cc < 2:
                        if i >= 2:
                            pe.wait_ge(s_sc, i - 1)
                        for h in range(4):
                            hh = 4 * half + h
                            mm = pe.matmul(bank[6 + half][:, h * P:(h + 1) * P], kdec[0:n, cc, hh * P:(hh + 1) * P],
                                           vn[0:n, half, h * P:(h + 1) * P], start=True, stop=True)
                        mm.then_inc(s_s, 1)

                for cc in range(3):
                    for f in (solve_rhs, new_values, outputs):
                        for half in range(2):
                            f(2 * cc + half)
                for h in range(HEADS):
                    pe.wait_ge(s_osq, h + 1)
                    if h >= 2:
                        pe.wait_ge(s_on, h - 1)
                    pe.matmul(bank[h % 2][:, 0:T], ones[:], sq[:, h % 2, :], start=True, stop=True).then_inc(s_osum, 1)

            @block.scalar
            def _(act):
                eps = mem["eps"]
                step = Chain(act, act_step)
                for i in range(17):
                    if i < 16:
                        if i >= 2:
                            act.wait_ge(s_sum, i - 1)
                        act.activation(sq[:, i % 2, :], qkv[:, i, :], ACT.Square).then_inc(s_sq, 1)
                    if i >= 1:
                        j = i - 1
                        act.wait_ge(s_sum, j + 1)
                        if j >= 2:
                            act.wait_ge(s_qkn, j - 1)
                        f = float(P) if j >= 8 else 1.0
                        act.activation(nrm[:, j % 2, :], bank[j % 2][:, 0:T], ACT.Sqrt, scale=f,
                                       bias=eps[:, 0:1] if j < 8 else eps[:, 1:2]).then_inc(s_nrm, 1)
                act.activation(beta, bd[:, 0, :], ACT.Sigmoid).then_inc(s_beta, 1)
                for i in range(16):
                    act.wait_ge(s_lg, i + 1)
                    act.activation(gates[:, i, :], bank[2 + i % 2][:, 0:T], ACT.Sigmoid,
                                   bias=mem["lru_b"][:, i:i + 1]).then_inc(s_gate, 1)
                act.activation(ea[:], mem["head_par"][:, 0:1], ACT.Exp).then_inc(s_ea, 1)
                act.wait_ge(s_x, 1)
                step.done(act.activation(s1, s0, ACT.Abs))
                act.activation(s1, s1, ACT.Exp, scale=-1.0).then_inc(s_exp, 1)
                step.done(act.activation(l8[:, 1, :], mem["lru_lam"][:], ACT.Abs))
                act.activation(l8[:, 1, :], l8[:, 1, :], ACT.Exp, scale=-1.0).then_inc(s_lame, 1)
                act.wait_ge(s_c8, 1)
                act.wait_ge(s_gate, 16)
                for c in range(DC):
                    act.activation(lru_t[:, c, :], gates[:, c, :], ACT.Tanh, scale=c8[:, c:c + 1]).then_inc(s_th, 1)
                act.wait_ge(s_th, DC)
                for c in range(DC):
                    act.activation(gates[:, c, :], gates[:, c, :], ACT.Exp, scale=c8[:, c:c + 1]).then_inc(s_th, 1)
                for h in range(HEADS):
                    act.wait_ge(s_bc, 2 * h + 1)
                    src = bank[4 + 2 * (h % 2)][:, 0:T]
                    act.copy(gb[:, h, :], src).then_inc(s_gb, 1)
                act.wait_ge(s_kdx, 1)
                act.activation(kd[:], kd[:], ACT.Exp).then_inc(s_kde, 1)
                act.activation(egl[:], egl[:], ACT.Exp).then_inc(s_kde, 1)
                act.activation(nbeg[:], nbeg[:], ACT.Exp).then_inc(s_kde, 1)
                for s, (cc, h0, nh) in enumerate(SETS):
                    n = CHUNKS[cc][1]
                    act.wait_ge(s_diff, s + 1)
                    d = LT[0:n, s].rearrange("p a b -> p (a b)")[:, 0:nh * n]
                    act.activation(d, d, ACT.Exp).then_inc(s_dexp, 1)
                act.activation(gb[:], gb[:], ACT.Exp).then_inc(s_eg, 1)
                act.wait_ge(s_m, 1)
                act.activation(lru_t, lru_t, ACT.Sqrt).then_inc(s_sqrt, 1)
                for i, (lv, s) in enumerate(work):
                    cc, h0, nh = SETS[s]
                    n = CHUNKS[cc][1]
                    act.wait_ge(s_t1, i + 1)
                    if i >= 2:
                        before = sum(1 for w in work[:i - 1] if w[0] > 0)
                        if before:
                            act.wait_ge(s_pq, 2 * before)
                        if work[i - 2][0] == 0:
                            act.wait_ge(s_x2, 2 * (i - 1))
                    act.copy(T1[0:n, i % 2, 0:nh * n], bank[i % 2][0:n, 0:nh * n]).then_inc(s_t1c, 1)
                for cc in range(3):
                    t0, n = CHUNKS[cc]
                    for half in range(2):
                        i = 2 * cc + half
                        act.wait_ge(s_vn, i + 1)
                        if i >= 2:
                            act.wait_ge(s_o, i - 1)
                            act.wait_ge(s_s, i - 1)
                        act.copy(vn[0:n, half, :], bank[2 + half][0:n, :]).then_inc(s_vnc, 1)
                    for half in range(2):
                        i = 2 * cc + half
                        act.wait_ge(s_o, i + 1)
                        act.copy(kb_o[:, 4 * half:4 * half + 4, t0:t0 + n],
                                 bank[4 + half][:, 0:4 * n].rearrange("p (h t) -> p h t", h=4)).then_inc(s_oc, 1)
                act.wait_ge(s_oc, 6)
                for h in range(HEADS + 1):
                    if h < HEADS:
                        if h >= 2:
                            act.wait_ge(s_osum, h - 1)
                        act.activation(sq[:, h % 2, :], kb_o[:, h, :], ACT.Square).then_inc(s_osq, 1)
                    if h >= 1:
                        j = h - 1
                        act.wait_ge(s_osum, j + 1)
                        if j >= 2:
                            act.wait_ge(s_of, j - 1)
                        act.activation(nrm[:, j % 2, :], bank[j % 2][:, 0:T], ACT.Sqrt, scale=1.0 / P,
                                       bias=eps[:, 0:1]).then_inc(s_on, 1)

            @block.gpsimd
            def _(pool):
                step = Chain(pool, pool_step)
                pool.wait_ge(s_gate, 16)
                pool.tensor_tensor(gates[:, DC:, :], gates[:, DC:, :], xa[:], ALU.mult).then_inc(s_u, 1)
                for s, (cc, h0, nh) in enumerate(SETS):
                    n = CHUNKS[cc][1]
                    pool.wait_ge(s_dexp, s + 1)
                    d = LT[0:n, s].rearrange("p a b -> p (a b)")[:, 0:nh * n].rearrange("p (h t) -> p h t", h=nh)
                    pool.tensor_tensor(d, d, causal[0:n, 0:n].unsqueeze(1).broadcast_to([n, nh, n]),
                                       ALU.mult).then_inc(s_mask, 1)
                pool.wait_ge(s_lt, 10)
                for i, (lv, s) in enumerate(work):
                    cc, h0, nh = SETS[s]
                    n = CHUNKS[cc][1]
                    if i >= 2:
                        pool.wait_ge(s_t1, i - 1)
                        if work[i - 2][0] == 0:
                            pool.wait_ge(s_x2, 2 * (i - 1))
                    d = LT[0:n, s].rearrange("p a b -> p (a b)")[:, 0:nh * n].rearrange("p (h t) -> p h t", h=nh)
                    o = LTo[0:n, i % 2, 0:nh * n].rearrange("p (h t) -> p h t", h=nh)
                    pool.tensor_tensor(o, d, offmask[0:n, lv, 0:n].unsqueeze(1).broadcast_to([n, nh, n]),
                                       ALU.mult).then_inc(s_lto, 1)
                    if i == 14:
                        pool.wait_ge(s_scan, DC)
                        pool.tensor_tensor(y[:, 0:DC, :], y[:, 0:DC, :], xa[:], ALU.mult).then_inc(s_y, 1)

            @block.vector
            def _(dve):
                step = Chain(dve, dve_step)
                link = step.done
                link(dve.memset(colg[:], 0.0))
                link(dve.memset(colb[:], 0.0))
                hp, lam = mem["head_par"], mem["lru_lam"]
                dve.tensor_scalar(s0, bd[:, 1, :], hp[:, 1:2], None, ALU.add).then_inc(s_x, 1)
                for i in range(16):
                    dve.wait_ge(s_nrm, i + 1)
                    link(dve.reciprocal(nrm[:, i % 2, :], nrm[:, i % 2, :]))
                    dve.tensor_tensor(qkv[:, i, :], qkv[:, i, :], nrm[:, i % 2, :], ALU.mult).then_inc(s_qkn, 1)
                dve.wait_ge(s_exp, 1)
                log1p_steps(dve, link, s2, s1, s3, bd[:, 1, :])
                link(dve.scalar_tensor_tensor(out=s0, in0=s0, scalar=0.0, in1=s2, op0=ALU.max, op1=ALU.add))
                dve.wait_ge(s_ea, 1)
                link(dve.tensor_scalar(s0, s0, ea[:, 0:1], -1.0, ALU.mult, ALU.mult))
                link(dve.memset(s1, 1.0))
                for t0, n in CHUNKS:
                    dve.tensor_tensor_scan(G[:, t0:t0 + n], s1[:, t0:t0 + n], s0[:, t0:t0 + n], 0.0,
                                           ALU.mult, ALU.add).then_inc(dve_step, 1)
                    step.n += 1
                dve.wait_ge(dve_step, step.n)
                dve.memset(s1[:, 0:1], 1.0).then_inc(s_G, 1)
                dve.wait_ge(s_lame, 1)
                log1p_steps(dve, link, l8[:, 0, :], l8[:, 1, :], l8[:, 2, :], l8[:, 3, :])
                link(dve.tensor_scalar(l8[:, 2, :], lam[:], -1.0, 0.0, ALU.mult, ALU.max))
                link(dve.tensor_tensor(l8[:, 0, :], l8[:, 0, :], l8[:, 2, :], ALU.add))
                dve.tensor_scalar(c8[:], l8[:, 0, :], -8.0, None, ALU.mult).then_inc(s_c8, 1)
                for h in range(HEADS):
                    dve.wait_ge(s_bc, 2 * h + 2)
                    dve.wait_ge(s_qkn, 16)
                    dve.tensor_tensor(kb_o[:, h, :], keys[:, h, :], bank[5 + 2 * (h % 2)][:, 0:T],
                                      ALU.mult).then_inc(s_kb, 1)
                dve.wait_ge(s_col, 1)
                for q, dst in enumerate((colg, colb)):
                    src = bank[0][:, 0:6 * HEADS].rearrange("p (c q h) -> p c q h", c=3, q=2)
                    link(dve.tensor_copy(dst[0:META, 0, :], src[0:META, 0, q, :]))
                    dve.tensor_copy(dst[:, 1:3, :], src[:, 1:3, q, :]).then_inc(s_colc, 1)
                    dve.wait_ge(s_colc, q + 1)
                dve.wait_ge(s_gb, HEADS)
                for cc, (t0, n) in enumerate(CHUNKS):
                    link(dve.tensor_copy(egl[:, cc, :], gb[:, :, t0 + n - 1]))
                link(dve.tensor_copy(nbeg[:], colg[:]))
                dve.tensor_tensor(kd[:], egl[:], colg[:], ALU.subtract).then_inc(s_kdx, 1)
                for s, (cc, h0, nh) in enumerate(SETS):
                    t0, n = CHUNKS[cc]
                    d = LT[0:n, s].rearrange("p a b -> p (a b)")[:, 0:nh * n].rearrange("p (h t) -> p h t", h=nh)
                    link(dve.tensor_tensor(d, gb[0:n, h0:h0 + nh, t0:t0 + n],
                                           colg[0:n, cc, h0:h0 + nh].unsqueeze(2).broadcast_to([n, nh, n]),
                                           ALU.subtract))
                    dve.tensor_scalar(d, d, 0.0, None, ALU.min).then_inc(s_diff, 1)
                dve.wait_ge(s_th, 2 * DC)
                link(dve.tensor_scalar(lru_u, lru_t, -1.0, 1.0, ALU.mult, ALU.add))
                link(dve.reciprocal(lru_u, lru_u))
                dve.scalar_tensor_tensor(out=lru_t.rearrange("p c t -> p (c t)"),
                                         in0=lru_t.rearrange("p c t -> p (c t)"), scalar=-2.0,
                                         in1=lru_u.rearrange("p c t -> p (c t)"),
                                         op0=ALU.mult, op1=ALU.mult).then_inc(s_m, 1)
                dve.wait_ge(s_kde, 3)
                link(dve.scalar_tensor_tensor(out=nbeg[:].rearrange("p a b -> p (a b)"),
                                              in0=nbeg[:].rearrange("p a b -> p (a b)"), scalar=-1.0,
                                              in1=colb[:].rearrange("p a b -> p (a b)"), op0=ALU.mult, op1=ALU.mult))
                dve.memset(s1[:, 0:1], 1.0).then_inc(s_nb, 1)
                dve.wait_ge(s_nb, 1)
                dve.wait_ge(s_sqrt, 1)
                dve.wait_ge(s_u, 1)
                dve.tensor_tensor(gates[:, DC:, :], gates[:, DC:, :], lru_t, ALU.mult).then_inc(s_b, 1)
                dve.wait_ge(s_b, 1)
                for i in range(12):
                    cc, q, half = i // 4, i // 2 % 2, i % 2
                    t0, n = CHUNKS[cc]
                    dve.wait_ge(s_tt, i + 1)
                    dst, col = ((kdec, kd), (vbeta, colb))[q]
                    dve.tensor_tensor(
                        dst[0:n, cc, 4 * half * P:4 * (half + 1) * P].rearrange("p (h d) -> p h d", h=4),
                        bank[i % 4][0:n, :].rearrange("p (h d) -> p h d", h=4),
                        col[0:n, cc, 4 * half:4 * half + 4].unsqueeze(2).broadcast_to([n, 4, P]),
                        ALU.mult).then_inc(s_tok, 1)
                for s, (cc, h0, nh) in enumerate(SETS):
                    n = CHUNKS[cc][1]
                    o = 4 + 2 * (s % 2)
                    d = LT[0:n, s].rearrange("p a b -> p (a b)")[:, 0:nh * n]
                    qk = QK[:, s].rearrange("p a b -> p (a b)") if s < 4 else QK0[:].rearrange("p a b -> p (a b)")
                    dve.wait_ge(s_mask, s + 1)
                    dve.wait_ge(s_kk, 2 * s + 2)
                    dve.tensor_tensor(qk, d, bank[o + 1][0:n, 0:nh * n], ALU.mult).then_inc(s_lt, 1)
                    dve.wait_ge(s_lt, 2 * s + 1)
                    dve.tensor_tensor(d, d, bank[o][0:n, 0:nh * n], ALU.mult).then_inc(s_lt, 1)
                dve.wait_ge(s_kk, 10)
                dve.wait_ge(s_eg, 1)
                dve.tensor_tensor(queries, queries, gb[:], ALU.mult).then_inc(s_qg, 1)
                for i, (lv, s) in enumerate(work):
                    cc, h0, nh = SETS[s]
                    n = CHUNKS[cc][1]
                    if lv == 0:
                        idb = ident[0:n, 0:n].unsqueeze(1).broadcast_to([n, nh, n])
                        xx = X[:, s] if s < 4 else X0[:]
                        yy = Y[:, s] if s < 4 else Y0[:]
                        dve.wait_ge(s_t1c, i + 1)
                        dve.tensor_tensor(xx, idb, T1[0:n, i % 2, 0:nh * n].rearrange("p (h t) -> p h t", h=nh),
                                          ALU.subtract).then_inc(s_x2, 1)
                        dve.tensor_tensor(yy, idb, LTo[0:n, i % 2, 0:nh * n].rearrange("p (h t) -> p h t", h=nh),
                                          ALU.subtract).then_inc(s_x2, 1)
                        continue
                    o = 2 + 2 * (i % 2)
                    m = sum(1 for w in work[:i + 1] if w[0] > 0)
                    for q in range(2):
                        t = ((X, X0), (Y, Y0))[q][s == 4]
                        t = (t[:, s] if s < 4 else t[:]).rearrange("p a b -> p (a b)")
                        dve.wait_ge(s_pq, 2 * m)
                        if i >= 1:
                            dve.wait_ge(s_x2, 2 * i)
                        dve.tensor_tensor(t, t, bank[o + q][0:n, 0:nh * n], ALU.subtract).then_inc(s_x2, 1)
                    if 5 <= i < 5 + DC:
                        c = i - 5
                        dve.wait_ge(s_u, 1)
                        dve.tensor_tensor_scan(xa[:, c, :], gates[:, c, :], gates[:, DC + c, :], 0.0,
                                               ALU.mult, ALU.add).then_inc(s_scan, 1)
                for cc in range(3):
                    t0, n = CHUNKS[cc]
                    if cc > 0:
                        for half in range(2):
                            i = 2 * cc + half
                            dve.wait_ge(s_ks, i - 1)
                            rr = r[:, half, :].rearrange("p (h d) -> p h d", h=4)
                            if cc > 1:
                                dve.wait_ge(s_vn, i - 1)
                            link(dve.tensor_tensor(rr, bank[half][:].rearrange("p (h d) -> p h d", h=4),
                                                   nbeg[:, cc, 4 * half:4 * half + 4].unsqueeze(2).broadcast_to([P, 4, P]),
                                                   ALU.mult))
                            dve.tensor_tensor(r[:, half, :], r[:, half, :],
                                              vbeta[:, cc, 4 * half * P:4 * (half + 1) * P], ALU.add).then_inc(s_r, 1)
                    if cc < 2:
                        for half in range(2):
                            i = 2 * cc + half
                            sh = S[:, 4 * half:4 * half + 4, :]
                            dve.wait_ge(s_s, i + 1)
                            src = bank[6 + half][:].rearrange("p (h d) -> p h d", h=4)
                            if cc == 0:
                                dve.tensor_copy(sh, src).then_inc(s_sc, 1)
                                continue
                            link(dve.tensor_tensor(sh, sh, egl[:, cc, 4 * half:4 * half + 4].unsqueeze(2).broadcast_to(
                                [P, 4, P]), ALU.mult))
                            dve.tensor_tensor(sh, sh, src, ALU.add).then_inc(s_sc, 1)
                for h in range(HEADS):
                    dve.wait_ge(s_on, h + 1)
                    link(dve.reciprocal(nrm[:, h % 2, :], nrm[:, h % 2, :]))
                    link(dve.tensor_tensor(kb_o[:, h, :], kb_o[:, h, :], nrm[:, h % 2, :], ALU.mult))
                    dve.scalar_tensor_tensor(out=y[:, DC + h, :], in0=kb_o[:, h, :], scalar=mem["norm_w"][:, 0:1],
                                             in1=y[:, DC + h, :], op0=ALU.mult, op1=ALU.mult).then_inc(s_of, 1)
                dve.wait_ge(s_y, 1)


def layer_norm(nc, mem, which, source):
    hT, acc, ones, ln, eps = mem["hT"], mem["acc"], mem["ones"], mem["ln_par"], mem["eps"]
    with ExitStack() as inner:
        sem = inner.enter_context(Signals(nc, f"ln{which}_"))
        sb = lambda name, shape: inner.enter_context(nc.sbuf_tensor(f"ln{which}_{name}", shape, F32))
        sums = inner.enter_context(nc.psum_tensor(f"ln{which}_sums", [P, BLOCK], F32))
        sqs = inner.enter_context(nc.psum_tensor(f"ln{which}_sqs", [P, BLOCK], F32))
        sq = sb("sq", [P, DC, T])
        mean, rstd = sb("mean", [P, T]), sb("rstd", [P, T])
        added, summed, meaned, centred = sem("added"), sem("summed"), sem("meaned"), sem("centred")
        squared, sq_summed, rooted, inverted, scaled, out = (sem("squared"), sem("sq_summed"), sem("rooted"),
                                                             sem("inverted"), sem("scaled"), sem("out"))
        with nc.Block(no_gpsimd_drain=True) as block:

            @block.tensor
            def _(pe):
                for c in range(DC):
                    if source == "acc":
                        pe.wait_ge(added, c + 1)
                    mm = pe.matmul(sums[:, 0:T], ones[:], hT[:, c, :], start=(c == 0), stop=(c == DC - 1))
                mm.then_inc(summed, 1)
                for c in range(DC):
                    pe.wait_ge(squared, c + 1)
                    mm = pe.matmul(sqs[:, 0:T], ones[:], sq[:, c, :], start=(c == 0), stop=(c == DC - 1))
                mm.then_inc(sq_summed, 1)

            @block.scalar
            def _(act):
                for c in range(DC):
                    act.wait_ge(centred, c + 1)
                    act.activation(sq[:, c, :], hT[:, c, :], ACT.Square).then_inc(squared, 1)
                act.wait_ge(sq_summed, 1)
                act.activation(rstd[:], sqs[:, 0:T], ACT.Sqrt, scale=1.0 / D, bias=eps[:, 2:3]).then_inc(rooted, 1)

            @block.vector
            def _(dve):
                if source == "acc":
                    for c in range(DC):
                        dve.scalar_tensor_tensor(out=hT[:, c, :], in0=hT[:, c, :], scalar=ALPHA, in1=acc[:, c, :],
                                                 op0=ALU.mult, op1=ALU.add).then_inc(added, 1)
                dve.wait_ge(summed, 1)
                dve.tensor_scalar(mean[:], sums[:, 0:T], 1.0 / D, None, ALU.mult).then_inc(meaned, 1)
                dve.wait_ge(meaned, 1)
                for c in range(DC):
                    dve.tensor_tensor(hT[:, c, :], hT[:, c, :], mean[:], ALU.subtract).then_inc(centred, 1)
                dve.wait_ge(rooted, 1)
                dve.reciprocal(rstd[:], rstd[:]).then_inc(inverted, 1)
                dve.wait_ge(inverted, 1)
                for c in range(DC):
                    dve.tensor_tensor(hT[:, c, :], hT[:, c, :], rstd[:], ALU.mult).then_inc(scaled, 1)
                for c in range(DC):
                    dve.wait_ge(scaled, c + 1)
                    dve.tensor_scalar(hT[:, c, :], hT[:, c, :], ln[:, 2 * which * DC + c:2 * which * DC + c + 1],
                                      ln[:, (2 * which + 1) * DC + c:(2 * which + 1) * DC + c + 1],
                                      ALU.mult, ALU.add).then_inc(out, 1)


def out_projection(nc, k, mem):
    hT, y, ring = mem["hT"], mem["y"], mem["dense"]
    KC = 2 * DC
    NB, cols = 4, D // 4
    with ExitStack() as inner:
        sem = inner.enter_context(Signals(nc))
        ps = [inner.enter_context(nc.psum_tensor(f"outp{b}", [P, BLOCK], F32)) for b in range(4)]
        ready = [sem("w_out_even"), sem("w_out_odd")]
        projected, added = sem("out_projected"), sem("out_added")
        w = k["w_out"].rearrange("(c p) n -> p c n", p=P)
        with nc.Block(no_gpsimd_drain=True) as block:

            @block.sync
            def _(sp):
                for b in range(NB):
                    if b >= 2:
                        sp.wait_ge(projected, 2 * (b - 1))
                    dst = ring[:, b % 2].rearrange("p c n -> p (c n)").rearrange("p (c n) -> p c n", c=KC)
                    sp.dma_start(dst, w[:, :, b * cols:(b + 1) * cols]).then_inc(ready[b % 2], 16)

            @block.tensor
            def _(pe):
                for m in range(DC):
                    b = m // 2
                    if m % 2 == 0:
                        pe.wait_ge(ready[b % 2], 16 * (b // 2 + 1))
                    if m >= 4:
                        pe.wait_ge(added, m - 3)
                    wv = ring[:, b % 2].rearrange("p c n -> p (c n)").rearrange("p (c n) -> p c n", c=KC)
                    for c in range(KC):
                        mm = pe.matmul(ps[m % 4][:, 0:T], wv[:, c, (m % 2) * P:(m % 2 + 1) * P], y[:, c, :],
                                       start=(c == 0), stop=(c == KC - 1))
                    mm.then_inc(projected, 1)

            @block.vector
            def _(dve):
                for m in range(DC):
                    dve.wait_ge(projected, m + 1)
                    dve.scalar_tensor_tensor(out=hT[:, m, :], in0=hT[:, m, :], scalar=ALPHA, in1=ps[m % 4][:, 0:T],
                                             op0=ALU.mult, op1=ALU.add).then_inc(added, 1)


def router_and_shared(nc, k, mem, layer):
    hT, acc, ring, ident, pg = mem["hT"], mem["acc"], mem["dense"], mem["ident"], mem["pg"]
    with ExitStack() as inner:
        sem = inner.enter_context(Signals(nc, f"r{layer}_"))
        sb = lambda name, shape, dt=F32: inner.enter_context(nc.sbuf_tensor(f"r{layer}_{name}", shape, dt))
        bank = [inner.enter_context(nc.psum_tensor(f"r{layer}_b{b}", [P, BLOCK], F32)) for b in range(8)]
        rows = sb("rows", [P, 3, D])
        wr, rb = sb("wr", [P, DC, E]), sb("rb", [P, E])
        after, lower = sb("after", [P, 3, T]), sb("lower", [P, GROUPS, GROUPS])
        sc, bi, mb, mr, sel, gt = (sb(n, [P, 3, E]) for n in ("sc", "bi", "mb", "mr", "sel", "gt"))
        m8 = sb("m8", [P, 3 * GROUPS, 8])
        gs, rk, gm = (sb(n, [P, 3, GROUPS]) for n in ("gs", "rk", "gm"))
        cmp, eq = sb("cmp", [P, 3 * GROUPS, GROUPS]), sb("eq", [P, 3 * GROUPS, GROUPS])
        t8, ws = sb("t8", [P, 3, 8]), sb("ws", [P, 3])
        maskT = sb("maskT", [E, T])
        cm = sb("cm", [E, 1])
        row = sb("row", [1, 2])
        actT = sb("actT", [P, FC, T])
        silu = sb("silu", [P, FC, T])
        loaded, gu_ready, dn_ready = sem("loaded"), sem("shared_gu_ready"), sem("shared_down_ready")
        rows_t, rows_c, stored = sem("rows_turned"), sem("rows_copied"), mem["rows_stored"]
        zero, logits, scored, step_s = sem("zeroed"), sem("logits"), sem("scored"), sem("step")
        selected, gated, ranked, placed = sem("selected"), sem("gated"), sem("ranked"), sem("placed")
        counted, maxed = sem("count_turned"), mem["count_ready"]
        sh_gu, sh_act, sh_mul, sh_dn, sh_out = (sem(n) for n in ("sh_gu", "sh_silu", "sh_mul", "sh_down", "sh_out"))
        w_gu = ring[:, 0]
        w_dn = ring[:, 1].rearrange("p c n -> p (c n)")[:, 0:FC * D].rearrange("p (c n) -> p c n", c=FC)
        with nc.Block(no_gpsimd_drain=True) as block:

            @block.sync
            def _(sp):
                sp.dma_start(wr[:], k["router_w"][layer]).then_inc(loaded, 16)
                sp.dma_start(rb[:], k["router_b"][layer:layer + 1, :].broadcast_to([P, E])).then_inc(loaded, 16)
                sp.dma_start(after[:], k["after"]).then_inc(loaded, 16)
                sp.dma_start(lower[:], k["lower"]).then_inc(loaded, 16)
                for q, name in enumerate(("sh_gate", "sh_up")):
                    sp.dma_start(w_gu[:, :, q * FF:(q + 1) * FF],
                                 k[name][layer].rearrange("(c p) f -> p c f", p=P)).then_inc(gu_ready, 16)
                sp.dma_start(w_dn, k["sh_down"][layer].rearrange("(c p) d -> p c d", p=P)).then_inc(dn_ready, 16)
                for tt, (t0, n) in enumerate(TILES):
                    sp.wait_ge(rows_c, 2 * tt + 2)
                    sp.dma_start(mem["rows_dram"][t0:t0 + n, :], rows[0:n, tt, :]).then_inc(stored, 16)

            @block.tensor
            def _(pe):
                pe.wait_ge(loaded, 64)
                for tt, (t0, n) in enumerate(TILES):
                    for c in range(DC):
                        mm = pe.matmul(bank[0][0:n, tt * E:(tt + 1) * E], hT[:, c, t0:t0 + n], wr[:, c, :],
                                       start=(c == 0), stop=(c == DC - 1))
                mm.then_inc(logits, 1)
                for i in range(6):
                    tt, half = i // 2, i % 2
                    t0, n = TILES[tt]
                    if i >= 2:
                        pe.wait_ge(rows_c, i - 1)
                    for c in range(4):
                        mm = pe.transpose(bank[1 + i % 2][0:n, c * P:(c + 1) * P], hT[:, 4 * half + c, t0:t0 + n],
                                          ident[:])
                    mm.then_inc(rows_t, 1)
                pe.wait_ge(gu_ready, 32)
                for m in range(4):
                    for c in range(DC):
                        mm = pe.matmul(bank[3 + m][:, 0:T], w_gu[:, c, m * P:(m + 1) * P], hT[:, c, :],
                                       start=(c == 0), stop=(c == DC - 1))
                    mm.then_inc(sh_gu, 1)
                pe.wait_ge(dn_ready, 16)
                pe.wait_ge(sh_mul, FC)
                for m in range(DC):
                    if m >= 2:
                        pe.wait_ge(sh_out, m - 1)
                    for c in range(FC):
                        mm = pe.matmul(bank[3 + m % 2][:, 0:T], w_dn[:, c, m * P:(m + 1) * P], actT[:, c, :],
                                       start=(c == 0), stop=(c == FC - 1))
                    mm.then_inc(sh_dn, 1)
                pe.wait_ge(selected, 1)
                for tt, (t0, n) in enumerate(TILES):
                    mm = pe.matmul(bank[7][0:E, 0:T], sel[0:n, tt, :], after[0:n, tt, :], start=(tt == 0), stop=(tt == 2))
                mm.then_inc(ranked, 1)
                pe.wait_ge(gated, 1)
                pe.wait_ge(rows_c, 6)
                for q, src in enumerate((sel, gt)):
                    for tt, (t0, n) in enumerate(TILES):
                        mm = pe.transpose(bank[1 + q][0:E, t0:t0 + n], src[0:n, tt, :], ident[0:n, 0:n])
                    mm.then_inc(ranked, 1)
                pe.wait_ge(counted, 1)
                pe.transpose(bank[0][0:1, 0:E], cm[:, 0:1], ident[0:E, 0:E]).then_inc(ranked, 1)

            @block.scalar
            def _(act):
                act.wait_ge(logits, 1)
                act.wait_ge(zero, 1)
                lg = bank[0][:, 0:3 * E].rearrange("p (t e) -> p t e", t=3)
                act.activation(sc[:, 0:2, :], lg[:, 0:2, :], ACT.Sigmoid).then_inc(scored, 1)
                act.activation(sc[0:META, 2, :], lg[0:META, 2, :], ACT.Sigmoid).then_inc(scored, 1)
                for i in range(6):
                    tt, half = i // 2, i % 2
                    n = TILES[tt][1]
                    act.wait_ge(rows_t, i + 1)
                    src = bank[1 + i % 2][0:n, :].rearrange("p (c q r) -> p c q r", c=4, r=DC)
                    dst = rows[0:n, tt, :].rearrange("p (r c q) -> p c q r", r=DC, c=DC)[:, 4 * half:4 * half + 4]
                    act.copy(dst, src).then_inc(rows_c, 1)
                for m in range(FC):
                    act.wait_ge(sh_gu, m + 1)
                    act.activation(silu[:, m, :], bank[3 + m][:, 0:T], ACT.Silu).then_inc(sh_act, 1)
                for m in range(DC):
                    act.wait_ge(sh_dn, m + 1)
                    act.copy(acc[:, m, :], bank[3 + m % 2][:, 0:T]).then_inc(sh_out, 1)

            @block.vector
            def _(dve):
                step = Chain(dve, step_s)
                link = step.done
                dve.memset(sc[:], 0.5).then_inc(zero, 1)
                dve.wait_ge(loaded, 64)
                dve.wait_ge(scored, 2)
                link(dve.tensor_tensor(bi[:], sc[:], rb[:].unsqueeze(1).broadcast_to([P, 3, E]), ALU.add))
                for i in range(3 * GROUPS):
                    ins = dve.max(out=m8[:, i, :], in_=bi[:, i // GROUPS, (i % GROUPS) * 8:(i % GROUPS + 1) * 8])
                link(ins)
                gsf = gs[:].rearrange("p t g -> p (t g)")
                link(dve.tensor_tensor(gsf, m8[:, :, 0], m8[:, :, 1], ALU.add))
                for tt in range(3):
                    a = gs[:, tt, :].unsqueeze(1).broadcast_to([P, GROUPS, GROUPS])
                    b = gs[:, tt, :].unsqueeze(2).broadcast_to([P, GROUPS, GROUPS])
                    o = slice(tt * GROUPS, (tt + 1) * GROUPS)
                    link(dve.tensor_tensor(cmp[:, o, :], a, b, ALU.is_gt))
                    link(dve.tensor_tensor(eq[:, o, :], a, b, ALU.is_equal))
                    link(dve.tensor_tensor(eq[:, o, :], eq[:, o, :], lower[:], ALU.mult))
                link(dve.tensor_tensor(cmp[:], cmp[:], eq[:], ALU.add))
                link(dve.tensor_reduce(rk[:].rearrange("p t g -> p (t g)"), cmp[:], AX_X, ALU.add))
                link(dve.tensor_scalar(gm[:], rk[:], float(TOP_GROUPS), None, ALU.is_lt))
                link(dve.tensor_scalar(rk[:], gm[:], 1e30, -1e30, ALU.mult, ALU.add))
                wide = lambda t: t[:].rearrange("p t g -> p (t g)").unsqueeze(2).broadcast_to([P, 3 * GROUPS, 8])
                flat = lambda t: t[:].rearrange("p t (g i) -> p (t g) i", i=8)
                link(dve.tensor_tensor(flat(mb), flat(bi), wide(gm), ALU.mult))
                link(dve.tensor_tensor(flat(mb), flat(mb), wide(rk), ALU.add))
                for tt in range(3):
                    link(dve.max(out=t8[:, tt, :], in_=mb[:, tt, :]))
                    link(dve.match_replace(out=mr[:, tt, :], in_to_replace=t8[:, tt, :], in_values=mb[:, tt, :],
                                           imm_value=-3e30))
                dve.tensor_tensor(sel[:], mr[:], mb[:], ALU.not_equal).then_inc(selected, 1)
                dve.wait_ge(selected, 1)
                link(dve.tensor_tensor(gt[:], sc[:], sel[:], ALU.mult))
                link(dve.tensor_reduce(ws[:], gt[:], AX_X, ALU.add))
                link(dve.reciprocal(ws[:], ws[:]))
                link(dve.tensor_scalar(ws[:], ws[:], SCALE, None, ALU.mult))
                dve.tensor_tensor(gt[:], gt[:], ws[:].unsqueeze(2).broadcast_to([P, 3, E]), ALU.mult).then_inc(gated, 1)
                for m in range(FC):
                    dve.wait_ge(sh_act, m + 1)
                    dve.wait_ge(sh_gu, FC + m + 1)
                    dve.tensor_tensor(actT[:, m, :], silu[:, m, :], bank[3 + FC + m][:, 0:T],
                                      ALU.mult).then_inc(sh_mul, 1)
                dve.wait_ge(ranked, 2)
                link(dve.tensor_copy(maskT[:], bank[1][0:E, 0:T]))
                link(dve.scalar_tensor_tensor(out=pg[:, 0, :], in0=bank[7][0:E, 0:T], scalar=1.0, in1=maskT[:],
                                              op0=ALU.add, op1=ALU.mult))
                link(dve.tensor_reduce(cm[:], pg[:, 0, :], AX_X, ALU.max))
                dve.tensor_scalar_add(pg[:, 0, :], pg[:, 0, :], -1.0).then_inc(counted, 1)
                dve.wait_ge(ranked, 3)
                dve.tensor_copy(pg[:, 1, :], bank[2][0:E, 0:T]).then_inc(placed, 1)
                dve.wait_ge(ranked, 4)
                link(dve.tensor_reduce(row[:, 0:1], bank[0][0:1, 0:E], AX_X, ALU.max))
                dve.tensor_copy(mem["count"][:], row[:, 0:1]).then_inc(maxed, 1)


def experts(nc, k, mem, layer):
    acc, ident, pg, ring = mem["acc"], mem["ident"], mem["pg"], mem["experts"]
    base, slot_id, tok = mem["pair_base"], mem["slot_id"], mem["tok"]
    AHEAD = 3
    with ExitStack() as inner:
        sem = inner.enter_context(Signals(nc, f"e{layer}_"))
        sb = lambda name, shape, dt=F32: inner.enter_context(nc.sbuf_tensor(f"e{layer}_{name}", shape, dt))
        bank = [inner.enter_context(nc.psum_tensor(f"e{layer}_b{b}", [P, BLOCK], F32)) for b in range(8)]
        t0b, t1b, gub, atb, y0b, y1b = bank[:6]
        cb = bank[6:]
        xg = sb("xg", [P, 2, D])
        xgT = sb("xgT", [P, 2, DC, P])
        selw = sb("selw", [E, 2, P])
        basew = sb("basew", [E, P])
        gsb, hit = sb("gsb", [P, T]), sb("hit", [P, T])
        sg = sb("sg", [P, 4, T])
        idf, idx = sb("idf", [P, 1]), sb("idx", [P, 4, 1], I32)
        sl, ac, aT, ys = sb("sl", [P, FF]), sb("ac", [P, FF]), sb("aT", [P, FC, P]), sb("ys", [P, D])
        gu_ready = [sem("gu_even_ready"), sem("gu_odd_ready")]
        dn_ready = [sem("down_even_ready"), sem("down_odd_ready")]
        based, selw_ok, sel_mm, gate_in, sg_ok, idf_ok, idx_ok = (sem(n) for n in (
            "base_moved", "pair_selected", "rows_broadcast", "gates_in", "scatter_ready", "index_summed", "index_ready"))
        gathered = [sem("gathered_even"), sem("gathered_odd")]
        going = sem("gather_going")
        turned, ev0, ev1 = sem("turned"), sem("turned_in_a"), sem("turned_in_b")
        gu, sil, mul, at, ate = sem("gate_up"), sem("silu"), sem("gated_act"), sem("act_turned"), sem("act_in")
        dn, ye0, ye1, cmm, addd = sem("down"), sem("y_in_a"), sem("y_in_b"), sem("combined"), sem("added")
        wg = k["moe_gate"][layer].rearrange("e (p c) f -> e p c f", p=P)
        wu = k["moe_up"][layer].rearrange("e (p c) f -> e p c f", p=P)
        wd = k["moe_down"][layer].rearrange("e (c p) d -> e p c d", p=P)
        GU = DC * 2 * FF
        gu_w = lambda s: ring[:, s, 0:GU].rearrange("p (c n) -> p c n", c=DC)
        dn_w = lambda s: ring[:, s, GU:].rearrange("p (c n) -> p c n", c=FC)
        FULL = PAIRS - 4

        def load_gate_up(sp, q, u):
            for e in range(2):
                w = gu_w(2 * (u % 2) + e)
                sp.dma_start(w[:, :, 0:FF], wg[q * 2 + e]).then_inc(gu_ready[u % 2], 16)
                sp.dma_start(w[:, :, FF:], wu[q * 2 + e]).then_inc(gu_ready[u % 2], 16)

        def load_down(sp, q, u):
            for e in range(2):
                sp.dma_start(dn_w(2 * (u % 2) + e), wd[q * 2 + e]).then_inc(dn_ready[u % 2], 16)

        def in_loop(eng, body):
            with eng.Fori(0, FULL // 4) as i:
                for v in range(4):
                    body(i * 4 + (1 + v), (1 + v) % 4)

        with nc.Block(no_gpsimd_drain=True) as block:

            @block.sync
            def _(sp):
                def load(q, u):
                    sp.wait_ge(gu, q - 1)
                    load_gate_up(sp, q, u)
                    sp.wait_ge(dn, q - 1)
                    load_down(sp, q, u)

                sp.wait_ge(mem["rows_stored"], 16 * 3 * (layer + 1))
                for q in range(2):
                    load_gate_up(sp, q, q)
                    load_down(sp, q, q)
                with sp.Fori(0, FULL // 4) as i:
                    for v in range(4):
                        load(i * 4 + (2 + v), (2 + v) % 4)
                for q in range(PAIRS - 2, PAIRS):
                    load(q, q % 4)

            @block.gpsimd
            def _(pool):
                def gather(q, u):
                    pool.wait_ge(idx_ok, q + 1)
                    pool.sem_inc(going, 1)
                    pool.indirect_dma_start(
                        out=xg[:, u % 2, :], out_offset=None, in_=mem["rows_dram"],
                        in_offset=bass.IndirectOffsetOnAxis(ap=idx[:, u, :], axis=0)).then_inc(gathered[u % 2], 16)

                pool.wait_ge(mem["rows_stored"], 16 * 3 * (layer + 1))
                gather(0, 0)
                gather(1, 1)

                def next_gather(q, u):
                    pool.wait_ge(turned, q)
                    gather(q + 1, (u + 1) % 4)

                in_loop(pool, next_gather)
                for q in range(PAIRS - 3, PAIRS - 1):
                    next_gather(q, q % 4)

            @block.tensor
            def _(pe):
                def broadcast(q, u, first=False):
                    pe.wait_ge(selw_ok, q + 1)
                    if not first:
                        pe.wait_ge(ev0, q - (AHEAD - 2))
                        pe.wait_ge(ev1, q - (AHEAD - 2))
                    pe.matmul(t0b[:, 0:T], selw[:, u % 2, :], pg[:, 0, :], start=True, stop=True)
                    pe.matmul(t1b[:, 0:T], selw[:, u % 2, :], pg[:, 1, :], start=True, stop=True).then_inc(sel_mm, 1)

                def turn(q, u, known):
                    pe.wait_ge(gathered[u % 2], ((q - u % 2) // 2) * 16 + 16 if isinstance(q, int) else known[1])
                    pe.wait_ge(idf_ok, known[0])
                    pe.wait_ge(gate_in, known[0])
                    for c in range(DC):
                        mm = pe.transpose((t0b, t1b)[c // 4][:, (c % 4) * P:(c % 4 + 1) * P],
                                          xg[:, u % 2, c * P:(c + 1) * P], ident[:])
                        if c == DC - 1:
                            mm.then_inc(turned, 1)

                def gate_up(q, u, ready):
                    pe.wait_ge(gu_ready[u % 2], ready)
                    pe.wait_ge(ev0, q + 1)
                    pe.wait_ge(ev1, q + 1)
                    if not (isinstance(q, int) and q == 0):
                        pe.wait_ge(mul, q)
                    for c in range(DC):
                        for e in range(2):
                            mm = pe.matmul(gub[e * SLOTS:(e + 1) * SLOTS, :], xgT[:, u % 2, c, e * SLOTS:(e + 1) * SLOTS],
                                           gu_w(2 * (u % 2) + e)[:, c, :], start=(c == 0), stop=(c == DC - 1))
                    mm.then_inc(gu, 1)

                def combine(q, u):
                    pe.wait_ge(ye0, q + 1)
                    pe.wait_ge(ye1, q + 1)
                    for m in range(DC):
                        if m >= 2:
                            pe.wait_ge(addd, q * DC + m)
                        elif m == 0:
                            pe.wait_ge(addd, q * DC + 1)
                        pe.matmul(cb[m % 2][:, 0:T], ys[:, m * P:(m + 1) * P], sg[:, u, :],
                                  start=True, stop=True).then_inc(cmm, 1)

                def turn_act(q, u):
                    pe.wait_ge(mul, q + 1)
                    if not (isinstance(q, int) and q == 0):
                        pe.wait_ge(ate, q)
                    for f in range(FC):
                        mm = pe.transpose(atb[:, f * P:(f + 1) * P], ac[:, f * P:(f + 1) * P], ident[:])
                    mm.then_inc(at, 1)

                def down(q, u, ready):
                    pe.wait_ge(dn_ready[u % 2], ready)
                    pe.wait_ge(ate, q + 1)
                    if not (isinstance(q, int) and q == 0):
                        pe.wait_ge(ye0, q)
                        pe.wait_ge(ye1, q)
                    for h, yb in enumerate((y0b, y1b)):
                        for f in range(FC):
                            for e in range(2):
                                mm = pe.matmul(yb[e * SLOTS:(e + 1) * SLOTS, :], aT[:, f, e * SLOTS:(e + 1) * SLOTS],
                                               dn_w(2 * (u % 2) + e)[:, f, h * BLOCK:(h + 1) * BLOCK],
                                               start=(f == 0), stop=(f == FC - 1))
                    mm.then_inc(dn, 1)

                def pair(q, u, half, tail=0):
                    nxt = half + 1 if u % 2 else half
                    gate_up(q, u, half * 64 + 64)
                    if tail < 3:
                        turn(q + 1, (u + 1) % 4, (q + AHEAD if tail == 0 else PAIRS, nxt * 16 + 16))
                    if not (isinstance(q, int) and q == 0):
                        combine(q - 1, (u + 3) % 4)
                    if tail == 0:
                        broadcast(q + AHEAD, (u + AHEAD) % 4)
                    turn_act(q, u)
                    down(q, u, half * 32 + 32)

                for q in range(AHEAD):
                    if q:
                        pe.wait_ge(idf_ok, q)
                        pe.wait_ge(gate_in, q)
                    broadcast(q, q, first=True)
                turn(0, 0, (AHEAD, 16))
                pair(0, 0, 0)
                with pe.Fori(0, FULL // 4) as i:
                    for v in range(4):
                        pair(i * 4 + (1 + v), (1 + v) % 4, i * 2 + (1 + v) // 2)
                for q in range(PAIRS - 3, PAIRS):
                    pair(q, q % 4, q // 2, tail=q - (PAIRS - 4))
                combine(PAIRS - 1, 3)

            @block.scalar
            def _(act):
                def gates(q, u):
                    act.wait_ge(sel_mm, q + 1)
                    if not (isinstance(q, int) and q == 0):
                        act.wait_ge(sg_ok, q)
                    act.copy(gsb[:], t1b[:, 0:T]).then_inc(gate_in, 1)

                def turned_in(q, u, early=False):
                    act.wait_ge(turned, q + 1)
                    if not early:
                        act.wait_ge(gu, q - 1)
                    act.copy(xgT[:, u % 2, 0:4, :], t0b[:].rearrange("p (c n) -> p c n", c=4)).then_inc(ev0, 1)

                def pair(q, u, tail=0, early=False):
                    act.wait_ge(gu, q + 1)
                    if not (isinstance(q, int) and q == 0):
                        act.wait_ge(mul, q)
                    act.activation(sl[:], gub[:, 0:FF], ACT.Silu).then_inc(sil, 1)
                    if tail < 3:
                        turned_in(q + 1, (u + 1) % 4, early)
                    if tail == 0:
                        gates(q + AHEAD, (u + AHEAD) % 4)
                    act.wait_ge(at, q + 1)
                    if not (isinstance(q, int) and q == 0):
                        act.wait_ge(dn, q)
                    act.copy(aT[:], atb[:, 0:FF].rearrange("p (f n) -> p f n", f=FC)).then_inc(ate, 1)
                    act.wait_ge(dn, q + 1)
                    act.copy(ys[:, 0:BLOCK], y0b[:]).then_inc(ye0, 1)

                for q in range(AHEAD):
                    gates(q, q)
                turned_in(0, 0, True)
                pair(0, 0, early=True)
                in_loop(act, pair)
                for q in range(PAIRS - 3, PAIRS):
                    pair(q, q % 4, tail=q - (PAIRS - 4))

            @block.vector
            def _(dve):
                def select(q, u, start=False):
                    if q_ge2(q):
                        dve.wait_ge(sel_mm, q - 1)
                    dve.tensor_scalar(selw[:, u % 2, :], basew[:], 0.0, None, ALU.is_equal).then_inc(selw_ok, 1)
                    dve.wait_ge(selw_ok, q + 1)
                    dve.tensor_scalar_add(basew[:], basew[:], -2.0).then_inc(based, 1)
                    dve.wait_ge(based, q + 2)

                def q_ge2(q):
                    return not isinstance(q, int) or q >= 2

                def places(q, u):
                    dve.wait_ge(gate_in, q + 1)
                    if not (isinstance(q, int) and q < 4):
                        dve.wait_ge(cmm, q * DC - 3 * DC)
                    dve.scalar_tensor_tensor(out=sg[:, u, :], in0=t0b[:, 0:T], scalar=slot_id[:, 0:1], in1=gsb[:],
                                             op0=ALU.is_equal, op1=ALU.mult).then_inc(sg_ok, 1)
                    if not (isinstance(q, int) and q == 0):
                        dve.wait_ge(idx_ok, q)
                    dve.scalar_tensor_tensor(out=hit[:], in0=t0b[:, 0:T], scalar=slot_id[:, 0:1], in1=tok[:],
                                             op0=ALU.is_equal, op1=ALU.mult, accum_out=idf[:]).then_inc(idf_ok, 1)
                    dve.wait_ge(idf_ok, q + 1)
                    if not (isinstance(q, int) and q < 4):
                        dve.wait_ge(gathered[u % 2], gather_count(q, u))
                    dve.tensor_copy(idx[:, u, :], idf[:]).then_inc(idx_ok, 1)

                def gather_count(q, u):
                    return (q - u % 2 - 2) * 8

                def turned_in(q, u, early=False):
                    dve.wait_ge(turned, q + 1)
                    if not early:
                        dve.wait_ge(gu, q - 1)
                    dve.tensor_copy(xgT[:, u % 2, 4:8, :], t1b[:].rearrange("p (c n) -> p c n", c=4)).then_inc(ev1, 1)

                def add_up(q):
                    for m in range(DC):
                        dve.wait_ge(cmm, q * DC + (m + 1))
                        if m == 0:
                            dve.wait_ge(addd, q * DC + 1)
                        dve.tensor_tensor(acc[:, m, :], acc[:, m, :], cb[m % 2][:, 0:T], ALU.add).then_inc(addd, 1)

                def pair(q, u, tail=0, early=False):
                    dve.wait_ge(sil, q + 1)
                    if not (isinstance(q, int) and q == 0):
                        dve.wait_ge(at, q)
                    dve.tensor_tensor(ac[:], sl[:], gub[:, FF:], ALU.mult).then_inc(mul, 1)
                    if tail < 3:
                        turned_in(q + 1, (u + 1) % 4, early)
                    if not (isinstance(q, int) and q == 0):
                        add_up(q - 1)
                    if tail == 0:
                        select(q + AHEAD, (u + AHEAD) % 4)
                        places(q + AHEAD, (u + AHEAD) % 4)
                    dve.wait_ge(dn, q + 1)
                    dve.tensor_copy(ys[:, BLOCK:], y1b[:]).then_inc(ye1, 1)

                dve.tensor_copy(basew[:], base[:]).then_inc(based, 1)
                dve.memset(hit[:, 0:1], 0.0).then_inc(addd, 1)
                dve.wait_ge(based, 1)
                for q in range(AHEAD):
                    select(q, q)
                    places(q, q)
                turned_in(0, 0, True)
                pair(0, 0, early=True)
                in_loop(dve, pair)
                for q in range(PAIRS - 3, PAIRS):
                    pair(q, q % 4, tail=q - (PAIRS - 4))
                add_up(PAIRS - 1)

        more_rounds(nc, k, mem, layer, dict(
            bank=bank, xg=xg, xgT=xgT, selw=selw, basew=basew, gsb=gsb, hit=hit, sg=sg, idf=idf, idx=idx, sl=sl, ac=ac,
            aT=aT, ys=ys, gu_w=gu_w, dn_w=dn_w, wg=wg, wu=wu, wd=wd))


def more_rounds(nc, k, mem, layer, buf):
    acc, ident, pg, base, slot_id, tok = (mem[n] for n in ("acc", "ident", "pg", "pair_base", "slot_id", "tok"))
    bank, xg, xgT, selw, basew, gsb, hit, sg, idf, idx, sl, ac, aT, ys, gu_w, dn_w = (buf[n] for n in (
        "bank", "xg", "xgT", "selw", "basew", "gsb", "hit", "sg", "idf", "idx", "sl", "ac", "aT", "ys", "gu_w", "dn_w"))
    t0b, t1b, gub, atb, y0b, y1b, c0b, c1b = bank
    wg, wu, wd = buf["wg"], buf["wu"], buf["wd"]
    with Signals(nc, f"m{layer}_") as sem:
        gu_ready, dn_ready, passed = sem("gate_up_ready"), sem("down_ready"), sem("passed")
        round_set, picked, rows_bc, gate_in, placed, indexed, going, gathered = (sem(n) for n in (
            "round_set", "picked", "rows_broadcast", "gates_in", "placed", "indexed", "gather_going", "gathered"))
        turned, in_a, in_b, gu, silu, mul, at, ate = (sem(n) for n in (
            "turned", "turned_in_a", "turned_in_b", "gate_up", "silu", "gated", "act_turned", "act_in"))
        dn, y_a, y_b, combined, added = (sem(n) for n in ("down", "y_in_a", "y_in_b", "combined", "added"))

        def over_items(eng, item, new_round=None):
            longest = eng.value_load(mem["count"][0:1, 0:1], min_val=0, max_val=T)
            with eng.If(longest > SLOTS):
                with eng.Fori(1, (longest + (SLOTS - 1)) // SLOTS) as r:
                    if new_round:
                        new_round(r)
                    with eng.Fori(0, PAIRS) as p:
                        n = r * PAIRS + p - (PAIRS - 1)
                        item(p, n)
                        eng.wait_ge(added, n * DC)
                        eng.sem_inc(passed, 1)

        with nc.Block(no_gpsimd_drain=True) as block:

            @block.sync
            def _(sp):
                def item(p, n):
                    for e in range(2):
                        w = gu_w(e)
                        sp.dma_start(w[:, :, 0:FF], wg[p * 2 + e]).then_inc(gu_ready, 16)
                        sp.dma_start(w[:, :, FF:], wu[p * 2 + e]).then_inc(gu_ready, 16)
                        sp.dma_start(dn_w(e), wd[p * 2 + e]).then_inc(dn_ready, 16)

                over_items(sp, item)

            @block.gpsimd
            def _(pool):
                def item(p, n):
                    pool.wait_ge(indexed, n)
                    pool.sem_inc(going, 1)
                    pool.indirect_dma_start(
                        out=xg[:, 0, :], out_offset=None, in_=mem["rows_dram"],
                        in_offset=bass.IndirectOffsetOnAxis(ap=idx[:, 0, :], axis=0)).then_inc(gathered, 16)

                over_items(pool, item)

            @block.tensor
            def _(pe):
                def item(p, n):
                    pe.wait_ge(picked, n)
                    pe.matmul(t0b[:, 0:T], selw[:, 0, :], pg[:, 0, :], start=True, stop=True)
                    pe.matmul(t1b[:, 0:T], selw[:, 0, :], pg[:, 1, :], start=True, stop=True).then_inc(rows_bc, 1)
                    pe.wait_ge(indexed, n)
                    pe.wait_ge(gathered, n * 16)
                    for c in range(DC):
                        mm = pe.transpose((t0b, t1b)[c // 4][:, (c % 4) * P:(c % 4 + 1) * P],
                                          xg[:, 0, c * P:(c + 1) * P], ident[:])
                    mm.then_inc(turned, 1)
                    pe.wait_ge(in_a, n)
                    pe.wait_ge(in_b, n)
                    pe.wait_ge(gu_ready, n * 64)
                    for c in range(DC):
                        for e in range(2):
                            half = slice(e * SLOTS, (e + 1) * SLOTS)
                            mm = pe.matmul(gub[half, :], xgT[:, 0, c, half], gu_w(e)[:, c, :],
                                           start=(c == 0), stop=(c == DC - 1))
                    mm.then_inc(gu, 1)
                    pe.wait_ge(mul, n)
                    for f in range(FC):
                        mm = pe.transpose(atb[:, f * P:(f + 1) * P], ac[:, f * P:(f + 1) * P], ident[:])
                    mm.then_inc(at, 1)
                    pe.wait_ge(ate, n)
                    pe.wait_ge(dn_ready, n * 32)
                    for h, yb in enumerate((y0b, y1b)):
                        for f in range(FC):
                            for e in range(2):
                                half = slice(e * SLOTS, (e + 1) * SLOTS)
                                mm = pe.matmul(yb[half, :], aT[:, f, half], dn_w(e)[:, f, h * BLOCK:(h + 1) * BLOCK],
                                               start=(f == 0), stop=(f == FC - 1))
                    mm.then_inc(dn, 1)
                    pe.wait_ge(y_a, n)
                    pe.wait_ge(y_b, n)
                    for m in range(DC):
                        if m >= 2:
                            pe.wait_ge(added, n * DC - DC + m - 1)
                        pe.matmul((c0b, c1b)[m % 2][:, 0:T], ys[:, m * P:(m + 1) * P], sg[:, 0, :],
                                  start=True, stop=True).then_inc(combined, 1)

                over_items(pe, item)

            @block.scalar
            def _(act):
                def item(p, n):
                    act.wait_ge(rows_bc, n)
                    act.copy(gsb[:], t1b[:, 0:T]).then_inc(gate_in, 1)
                    act.wait_ge(turned, n)
                    act.copy(xgT[:, 0, 0:4, :], t0b[:].rearrange("p (c n) -> p c n", c=4)).then_inc(in_a, 1)
                    act.wait_ge(gu, n)
                    act.activation(sl[:], gub[:, 0:FF], ACT.Silu).then_inc(silu, 1)
                    act.wait_ge(at, n)
                    act.copy(aT[:], atb[:, 0:FF].rearrange("p (f n) -> p f n", f=FC)).then_inc(ate, 1)
                    act.wait_ge(dn, n)
                    act.copy(ys[:, 0:BLOCK], y0b[:]).then_inc(y_a, 1)

                over_items(act, item)

            @block.vector
            def _(dve):
                def new_round(r):
                    dve.tensor_scalar_add(pg[:, 0, :], pg[:, 0, :], -float(SLOTS)).then_inc(round_set, 1)
                    dve.tensor_copy(basew[:], base[:]).then_inc(round_set, 1)
                    dve.wait_ge(round_set, r * 2)
                    dve.sem_inc(passed, 1)

                def item(p, n):
                    dve.tensor_scalar(selw[:, 0, :], basew[:], 0.0, None, ALU.is_equal).then_inc(picked, 1)
                    dve.wait_ge(gate_in, n)
                    dve.tensor_scalar_add(basew[:], basew[:], -2.0).then_inc(placed, 1)
                    dve.scalar_tensor_tensor(out=sg[:, 0, :], in0=t0b[:, 0:T], scalar=slot_id[:, 0:1], in1=gsb[:],
                                             op0=ALU.is_equal, op1=ALU.mult).then_inc(placed, 1)
                    dve.scalar_tensor_tensor(out=hit[:], in0=t0b[:, 0:T], scalar=slot_id[:, 0:1], in1=tok[:],
                                             op0=ALU.is_equal, op1=ALU.mult, accum_out=idf[:]).then_inc(placed, 1)
                    dve.wait_ge(placed, n * 3)
                    dve.tensor_copy(idx[:, 0, :], idf[:]).then_inc(indexed, 1)
                    dve.wait_ge(turned, n)
                    dve.tensor_copy(xgT[:, 0, 4:8, :], t1b[:].rearrange("p (c n) -> p c n", c=4)).then_inc(in_b, 1)
                    dve.wait_ge(silu, n)
                    dve.tensor_tensor(ac[:], sl[:], gub[:, FF:], ALU.mult).then_inc(mul, 1)
                    dve.wait_ge(dn, n)
                    dve.tensor_copy(ys[:, BLOCK:], y1b[:]).then_inc(y_b, 1)
                    for m in range(DC):
                        dve.wait_ge(combined, n * DC - DC + m + 1)
                        dve.tensor_tensor(acc[:, m, :], acc[:, m, :], (c0b, c1b)[m % 2][:, 0:T],
                                          ALU.add).then_inc(added, 1)

                over_items(dve, item, new_round)


def write_out(nc, k, mem, out):
    hT, ident = mem["hT"], mem["ident"]
    with ExitStack() as inner:
        sem = lambda name: inner.enter_context(nc.semaphore(name))
        bank = [inner.enter_context(nc.psum_tensor(f"wo{b}", [P, BLOCK], F32)) for b in range(4)]
        rows = inner.enter_context(nc.sbuf_tensor("out_rows", [P, 4, BLOCK], F32))
        turned, copied, stored = sem("out_turned"), sem("out_copied"), sem("out_stored")
        with nc.Block() as block:

            @block.tensor
            def _(pe):
                for i in range(4):
                    t0 = META + (i // 2) * P
                    for c in range(4):
                        mm = pe.transpose(bank[i][:, c * P:(c + 1) * P], hT[:, 4 * (i % 2) + c, t0:t0 + P], ident[:])
                    mm.then_inc(turned, 1)

            @block.vector
            def _(dve):
                for i in range(4):
                    dve.wait_ge(turned, i + 1)
                    dve.tensor_copy(rows[:, i, :], bank[i][:]).then_inc(copied, 1)

            @block.sync
            def _(sp):
                for i in range(4):
                    sp.wait_ge(copied, i + 1)
                    sp.dma_start(out[0, (i // 2) * P:(i // 2 + 1) * P, (i % 2) * BLOCK:(i % 2 + 1) * BLOCK],
                                 rows[:, i, :]).then_inc(stored, 16)
                sp.wait_ge(stored, 64)


def s5_mixer(nc, k, mem):
    hT, ring = mem["hT"], mem["dense"]
    J, TWO_PI = S5_TILES, 2.0 * math.pi
    C1, C2 = 6.28125, 1.9350051879882812e-03
    C3 = TWO_PI - C1 - C2
    with ExitStack() as outer:
        yT = outer.enter_context(nc.sbuf_tensor("s5_y", [P, DC, T], F32))
        with ExitStack() as inner:
            sem = inner.enter_context(Signals(nc, "s5_"))
            sb = lambda name, shape, dt=F32: inner.enter_context(nc.sbuf_tensor(f"s5_{name}", shape, dt))
            bank = [inner.enter_context(nc.psum_tensor(f"s5_b{b}", [P, BLOCK], F32)) for b in range(8)]
            steps_after_tables = [0]
            lam = sb("lam", [P, 3, J])
            par = sb("par", [P, 16, J])
            ki = sb("ki", [P, J], I32)
            cosT, sinT = sb("cos", [P, J, T]), sb("sin", [P, J, T])
            c_re, c_im = sb("c_re", [P, J, 32]), sb("c_im", [P, J, 32])
            w_re, w_nre, w_nim = sb("w_re", [P, J, 32]), sb("w_nre", [P, J, 32]), sb("w_nim", [P, J, 32])
            b_re, b_im = sb("b_re", [P, DC, P]), sb("b_im", [P, DC, P])
            loaded, ph, sn, st = sem("loaded"), sem("phase"), sem("sines"), sem("step")
            lr, li, ldt = lam[:, 0, :], lam[:, 1, :], lam[:, 2, :]
            (dt, mag, th, ku, r, cs, s_, h2, abr, abi, den, nr, cfr, cfi, q1, q2) = (par[:, i, :] for i in range(16))
            with nc.Block(no_gpsimd_drain=True) as block:

                @block.sync
                def _(sp):
                    sp.dma_start(lam[:], k["s5_lam"]).then_inc(loaded, 16)
                    sp.dma_start(c_re[:], k["s5_c_re"]).then_inc(loaded, 16)
                    sp.dma_start(c_im[:], k["s5_c_im"]).then_inc(loaded, 16)
                    sp.dma_start(b_re[:], k["s5_b_re"]).then_inc(loaded, 16)
                    sp.dma_start(b_im[:], k["s5_b_im"]).then_inc(loaded, 16)
                    sp.dma_start(mem["s5_d"][:], k["s5_d"]).then_inc(loaded, 16)

                @block.scalar
                def _(act):
                    act.wait_ge(loaded, 96)
                    act.activation(dt, ldt, ACT.Exp).then_inc(sn, 1)
                    act.wait_ge(ph, 1)
                    act.activation(mag, mag, ACT.Exp).then_inc(sn, 1)
                    act.wait_ge(ph, 2)
                    act.activation(s_, r, ACT.Sin).then_inc(sn, 1)
                    act.activation(h2, r, ACT.Sin, scale=0.5).then_inc(sn, 1)

                @block.vector
                def _(dve):
                    step = Chain(dve, st)
                    link = step.done
                    dve.wait_ge(loaded, 96)
                    link(dve.tensor_scalar(lr, lr, -1e-4, None, ALU.min))
                    dve.wait_ge(sn, 1)
                    link(dve.tensor_tensor(th, li, dt, ALU.mult))
                    dve.tensor_tensor(mag, lr, dt, ALU.mult).then_inc(ph, 1)
                    link(dve.tensor_scalar(ku, th, 1.0 / TWO_PI, None, ALU.mult))
                    link(dve.tensor_copy(ki[:], ku))
                    link(dve.tensor_copy(ku, ki[:]))
                    link(dve.scalar_tensor_tensor(out=r, in0=ku, scalar=-C1, in1=th, op0=ALU.mult, op1=ALU.add))
                    link(dve.scalar_tensor_tensor(out=r, in0=ku, scalar=-C2, in1=r, op0=ALU.mult, op1=ALU.add))
                    link(dve.scalar_tensor_tensor(out=r, in0=ku, scalar=-C3, in1=r, op0=ALU.mult, op1=ALU.add))
                    dve.tensor_scalar(r, r, 3.1415925, -3.1415925, ALU.min, ALU.max).then_inc(ph, 1)
                    dve.wait_ge(sn, 4)
                    link(dve.tensor_tensor(cs, h2, h2, ALU.mult))
                    link(dve.tensor_scalar(cs, cs, -2.0, 1.0, ALU.mult, ALU.add))
                    link(dve.tensor_tensor(abr, mag, cs, ALU.mult))
                    link(dve.tensor_tensor(abi, mag, s_, ALU.mult))
                    link(dve.tensor_tensor(den, lr, lr, ALU.mult))
                    link(dve.tensor_tensor(q1, li, li, ALU.mult))
                    link(dve.tensor_tensor(den, den, q1, ALU.add))
                    link(dve.reciprocal(den, den))
                    link(dve.tensor_scalar_add(nr, abr, -1.0))
                    link(dve.tensor_tensor(q1, nr, lr, ALU.mult))
                    link(dve.tensor_tensor(q2, abi, li, ALU.mult))
                    link(dve.tensor_tensor(q1, q1, q2, ALU.add))
                    link(dve.tensor_tensor(cfr, q1, den, ALU.mult))
                    link(dve.tensor_tensor(q1, abi, lr, ALU.mult))
                    link(dve.tensor_tensor(q2, nr, li, ALU.mult))
                    link(dve.tensor_tensor(q1, q1, q2, ALU.subtract))
                    link(dve.tensor_tensor(cfi, q1, den, ALU.mult))
                    wide = lambda x: x.unsqueeze(2).broadcast_to([P, J, 32])
                    link(dve.tensor_tensor(w_re[:], c_re[:], wide(cfr), ALU.mult))
                    link(dve.tensor_tensor(w_nre[:], c_im[:], wide(cfi), ALU.mult))
                    link(dve.tensor_tensor(w_re[:], w_re[:], w_nre[:], ALU.subtract))
                    link(dve.tensor_scalar(w_nre[:], w_re[:], -1.0, None, ALU.mult))
                    link(dve.tensor_tensor(w_nim[:], c_re[:], wide(cfi), ALU.mult))
                    link(dve.tensor_tensor(c_im[:], c_im[:], wide(cfr), ALU.mult))
                    link(dve.scalar_tensor_tensor(out=w_nim[:].rearrange("p a b -> p (a b)"),
                                                  in0=w_nim[:].rearrange("p a b -> p (a b)"), scalar=-1.0,
                                                  in1=c_im[:].rearrange("p a b -> p (a b)"),
                                                  op0=ALU.mult, op1=ALU.subtract))
                    link(dve.memset(cosT[:, :, 0:1], 1.0))
                    link(dve.memset(sinT[:, :, 0:1], 0.0))
                    link(dve.tensor_copy(cosT[:, :, 1], cs))
                    link(dve.tensor_copy(sinT[:, :, 1], s_))
                    m = 1
                    while 2 * m < T:
                        cm, sm = cosT[:, :, m], sinT[:, :, m]
                        link(dve.tensor_tensor(q1, cm, cm, ALU.mult))
                        link(dve.tensor_tensor(q2, sm, sm, ALU.mult))
                        link(dve.tensor_tensor(cosT[:, :, 2 * m], q1, q2, ALU.subtract))
                        link(dve.tensor_tensor(q1, cm, sm, ALU.mult))
                        link(dve.tensor_scalar(sinT[:, :, 2 * m], q1, 2.0, None, ALU.mult))
                        m *= 2
                        n = min(m, T - m) - 1
                        ca, sa = (x[:, :, m].unsqueeze(2).broadcast_to([P, J, n]) for x in (cosT, sinT))
                        co, so = cosT[:, :, m + 1:m + 1 + n], sinT[:, :, m + 1:m + 1 + n]
                        ci, si = cosT[:, :, 1:1 + n], sinT[:, :, 1:1 + n]
                        for j0 in range(0, J, 8):
                            js = slice(j0, j0 + 8)
                            a = mem["scratch"][:, 0:8 * n].rearrange("p (j n) -> p j n", j=8)
                            link(dve.tensor_tensor(a, si[:, js], sa[:, js], ALU.mult))
                            link(dve.tensor_tensor(co[:, js], ci[:, js], ca[:, js], ALU.mult))
                            link(dve.tensor_tensor(co[:, js], co[:, js], a, ALU.subtract))
                            link(dve.tensor_tensor(a, ci[:, js], sa[:, js], ALU.mult))
                            link(dve.tensor_tensor(so[:, js], si[:, js], ca[:, js], ALU.mult))
                            link(dve.tensor_tensor(so[:, js], so[:, js], a, ALU.add))
                    steps_after_tables[0] = step.n

            b_sb = sb("b_sb", [P, 2, 2, T])
            zr, zi = sb("zr", [P, 2, T]), sb("zi", [P, 2, T])
            p4, u4 = sb("products", [P, 2, 4, T]), sb("rotated", [P, 2, 4, T])
            bu, cp, mult_a, mult_b, added = sem("bu"), sem("bu_in"), sem("rot_dve"), sem("rot_pool"), sem("rot_added")
            scanned, out_a, out_b, yy, fin, gel = (sem("scanned"), sem("back_dve"), sem("back_pool"), sem("y"),
                                                   sem("y_skip"), sem("gelu"))
            with nc.Block(no_gpsimd_drain=True) as block:

                @block.tensor
                def _(pe):
                    def inputs(j):
                        a, b = j // 4, j % 4
                        rows = slice(32 * b, 32 * b + 32)
                        if j >= 2:
                            pe.wait_ge(cp, 2 * (j - 1))
                        for q, w in enumerate((b_re, b_im)):
                            pe.matmul(bank[2 * (j % 2) + q][:, 0:T], w[rows, a, :], hT[rows, a, :],
                                      start=True, stop=True).then_inc(bu, 1)

                    def outputs(j):
                        a, b = j // 4, j % 4
                        if b == 0 and a >= 2:
                            pe.wait_ge(fin, a - 1)
                        pe.wait_ge(out_a, 2 * (j + 1))
                        pe.wait_ge(out_b, 2 * (j + 1))
                        for q, w in enumerate((w_re, w_nre, w_nim, w_nim)):
                            mm = pe.matmul(bank[4 + a % 2][32 * b:32 * b + 32, 0:T], w[:, j, :], p4[:, j % 2, q, :],
                                           start=(q == 0), stop=(q == 3))
                        mm.then_inc(yy, 1)

                    for j in range(J + 2):
                        if j < J:
                            inputs(j)
                        if j >= 2:
                            outputs(j - 2)

                @block.scalar
                def _(act):
                    for j in range(J):
                        for q in range(2):
                            act.wait_ge(bu, 2 * j + q + 1)
                            if j >= 2:
                                act.wait_ge(mult_a, 2 * (j - 1))
                                act.wait_ge(mult_b, 2 * (j - 1))
                            act.copy(b_sb[:, j % 2, q, :], bank[2 * (j % 2) + q][:, 0:T]).then_inc(cp, 1)
                    for a in range(DC):
                        act.wait_ge(fin, a + 1)
                        act.activation(yT[:, a, :], yT[:, a, :], ACT.Gelu_apprx_tanh).then_inc(gel, 1)

                @block.gpsimd
                def _(pool):
                    def forward(j):
                        c, s, u = cosT[:, j, :], sinT[:, j, :], u4[:, j % 2]
                        pool.wait_ge(cp, 2 * j + 2)
                        if j >= 2:
                            pool.wait_ge(scanned, 2 * (j - 1))
                        pool.tensor_tensor(u[:, 2, :], b_sb[:, j % 2, 1, :], c, ALU.mult).then_inc(mult_b, 1)
                        pool.tensor_tensor(u[:, 3, :], b_sb[:, j % 2, 0, :], s, ALU.mult).then_inc(mult_b, 1)
                        pool.wait_ge(mult_b, 2 * j + 2)
                        pool.tensor_tensor(u[:, 2, :], u[:, 2, :], u[:, 3, :], ALU.subtract).then_inc(added, 1)

                    def back(j):
                        c, s = cosT[:, j, :], sinT[:, j, :]
                        pool.wait_ge(scanned, 2 * j + 2)
                        if j >= 2:
                            pool.wait_ge(yy, j - 1)
                        pool.tensor_tensor(p4[:, j % 2, 2, :], zr[:, j % 2, :], s, ALU.mult).then_inc(out_b, 1)
                        pool.tensor_tensor(p4[:, j % 2, 3, :], zi[:, j % 2, :], c, ALU.mult).then_inc(out_b, 1)

                    for j in range(J + 1):
                        if j < J:
                            forward(j)
                        if j >= 1:
                            back(j - 1)

                @block.vector
                def _(dve):
                    step = Chain(dve, st)
                    step.n = steps_after_tables[0]
                    for j in range(J + 1):
                        if j < J:
                            c, s, u = cosT[:, j, :], sinT[:, j, :], u4[:, j % 2]
                            dve.wait_ge(cp, 2 * j + 2)
                            dve.tensor_tensor(u[:, 0, :], b_sb[:, j % 2, 0, :], c, ALU.mult).then_inc(mult_a, 1)
                            dve.tensor_tensor(u[:, 1, :], b_sb[:, j % 2, 1, :], s, ALU.mult).then_inc(mult_a, 1)
                            dve.wait_ge(mult_a, 2 * j + 2)
                            step.done(dve.tensor_tensor(u[:, 0, :], u[:, 0, :], u[:, 1, :], ALU.add))
                            if j >= 2:
                                dve.wait_ge(out_a, 2 * (j - 1))
                                dve.wait_ge(out_b, 2 * (j - 1))
                            rho = mag[:, j:j + 1].broadcast_to([P, T])
                            dve.tensor_tensor_scan(zr[:, j % 2, :], rho, u[:, 0, :], 0.0, ALU.mult,
                                                   ALU.add).then_inc(scanned, 1)
                            dve.wait_ge(added, j + 1)
                            dve.tensor_tensor_scan(zi[:, j % 2, :], rho, u[:, 2, :], 0.0, ALU.mult,
                                                   ALU.add).then_inc(scanned, 1)
                        if j < J:
                            dve.wait_ge(scanned, 2 * j + 2)
                            if j >= 2:
                                dve.wait_ge(yy, j - 1)
                            dve.tensor_tensor(p4[:, j % 2, 0, :], zr[:, j % 2, :], c, ALU.mult).then_inc(out_a, 1)
                            dve.tensor_tensor(p4[:, j % 2, 1, :], zi[:, j % 2, :], s, ALU.mult).then_inc(out_a, 1)
                        if j >= 4 and j % 4 == 0:
                            a = j // 4 - 1
                            dve.wait_ge(yy, 4 * (a + 1))
                            dve.scalar_tensor_tensor(out=yT[:, a, :], in0=hT[:, a, :], scalar=mem["s5_d"][:, a:a + 1],
                                                     in1=bank[4 + a % 2][:, 0:T], op0=ALU.mult,
                                                     op1=ALU.add).then_inc(fin, 1)

        with ExitStack() as inner:
            sem = inner.enter_context(Signals(nc, "glu_"))
            ps = [inner.enter_context(nc.psum_tensor(f"glu{b}", [P, BLOCK], F32)) for b in range(4)]
            val = inner.enter_context(nc.sbuf_tensor("glu_val", [P, DC, T], F32))
            sig = inner.enter_context(nc.sbuf_tensor("glu_sig", [P, 2, T], F32))
            ready = [sem("w_even"), sem("w_odd")]
            proj, taken, mul, added = sem("proj"), sem("taken"), sem("mul"), sem("added")
            w = k["s5_w_out"].rearrange("(c p) n -> p c n", p=P)
            with nc.Block(no_gpsimd_drain=True) as block:

                @block.sync
                def _(sp):
                    for b in range(4):
                        if b >= 2:
                            sp.wait_ge(proj, 4 * (b - 1))
                        sp.dma_start(ring[:, b % 2], w[:, :, b * BLOCK:(b + 1) * BLOCK]).then_inc(ready[b % 2], 16)

                @block.tensor
                def _(pe):
                    for m in range(2 * DC):
                        b = m // 4
                        if m % 4 == 0:
                            pe.wait_ge(ready[b % 2], 16 * (b // 2 + 1))
                        if m >= 4:
                            pe.wait_ge(taken, m - 3)
                        for c in range(DC):
                            mm = pe.matmul(ps[m % 4][:, 0:T], ring[:, b % 2, c, (m % 4) * P:(m % 4 + 1) * P],
                                           yT[:, c, :], start=(c == 0), stop=(c == DC - 1))
                        mm.then_inc(proj, 1)

                @block.scalar
                def _(act):
                    for m in range(2 * DC):
                        act.wait_ge(proj, m + 1)
                        if m < DC:
                            act.copy(val[:, m, :], ps[m % 4][:, 0:T]).then_inc(taken, 1)
                        else:
                            if m >= DC + 2:
                                act.wait_ge(mul, m - DC - 1)
                            act.activation(sig[:, m % 2, :], ps[m % 4][:, 0:T], ACT.Sigmoid).then_inc(taken, 1)

                @block.vector
                def _(dve):
                    for m in range(DC):
                        dve.wait_ge(taken, DC + m + 1)
                        dve.tensor_tensor(val[:, m, :], val[:, m, :], sig[:, m % 2, :], ALU.mult).then_inc(mul, 1)
                        dve.wait_ge(mul, m + 1)
                        dve.scalar_tensor_tensor(out=hT[:, m, :], in0=hT[:, m, :], scalar=ALPHA, in1=val[:, m, :],
                                                 op0=ALU.mult, op1=ALU.add).then_inc(added, 1)


def trunk(nc, k, out, phases=4):
    with ExitStack() as ctx:
        sb = lambda name, shape, dt=F32: ctx.enter_context(nc.sbuf_tensor(name, shape, dt))
        sem = lambda name: ctx.enter_context(nc.semaphore(name))
        mem = {
            "hT": sb("hT", [P, DC, T]), "dense": sb("dense_ring", [P, 2, DC, BLOCK]),
            "ident": sb("ident", [P, P]), "ones": sb("ones", [P, P]), "eps": sb("eps", [P, 3]),
            "ln_par": sb("ln_par", [P, 8 * DC]), "s5_d": sb("s5_d", [P, DC]),
            "pair_base": sb("pair_base", [E, P]), "slot_id": sb("slot_id", [P, 1]), "tok": sb("tok", [P, T]),
            "count": sb("count", [1, 1], I32),
            "consts_loaded": sem("consts_loaded"), "rows_stored": sem("rows_stored"), "count_ready": sem("count_ready"),
            "rows_dram": k["rows_dram"],
        }
        ones_set, consts2 = sem("ones_set"), sem("expert_consts_loaded")
        with nc.Block(no_gpsimd_drain=True) as block:

            @block.vector
            def _(dve):
                dve.memset(mem["ones"][:], 1.0).then_inc(ones_set, 1)

            @block.sync
            def _(sp):
                for name in ("pair_base", "slot_id", "tok"):
                    sp.dma_start(mem[name][:], k[name]).then_inc(consts2, 16)

        with ExitStack() as mix:
            msb = lambda name, shape, dt=F32: mix.enter_context(nc.sbuf_tensor(name, shape, dt))
            mem |= {
                "qkv": msb("qkv", [P, 24, T]), "xa": msb("xa", [P, DC, T]), "y": msb("y", [P, 2 * DC, T]),
                "bd": msb("bd", [HEADS, 2, T]), "conv_w": msb("conv_w", [P, 32, CONV]), "conv_b": msb("conv_b", [P, DC]),
                "w_bd": msb("w_bd", [P, DC, 2 * HEADS]), "offmask": msb("offmask", [P, LEVELS, P]),
                "causal": msb("causal", [P, P]), "sel8": msb("sel8", [HEADS, HEADS, P]), "lru_b": msb("lru_b", [P, 16]),
                "lru_lam": msb("lru_lam", [P, DC]), "head_par": msb("head_par", [HEADS, 2]),
                "norm_w": msb("norm_w", [P, 1]),
            }
            in_projection(nc, k, mix, mem)
            with nc.Block(no_gpsimd_drain=True) as block:
                for start in (block.tensor, block.scalar, block.vector, block.gpsimd):

                    @start
                    def _(eng):
                        eng.wait_ge(mem["consts_loaded"], 16 * 10)

            group_mixers(nc, k, mix, mem)
            out_projection(nc, k, mem)
        mem |= {"acc": sb("acc", [P, DC, T]), "pg": sb("places_gates", [E, 2, T])}
        layer_norm(nc, mem, 0, "hT")
        with nc.Block(no_gpsimd_drain=True) as block:
            for start in (block.tensor, block.vector):

                @start
                def _(eng):
                    eng.wait_ge(consts2, 48)

        def moe(layer):
            router_and_shared(nc, k, mem, layer)
            with ExitStack() as ex:
                mem["experts"] = ex.enter_context(nc.sbuf_tensor(f"experts{layer}", [P, 4, 3 * D * FF // P], F32))
                experts(nc, k, mem, layer)
            layer_norm(nc, mem, 2 * layer + 1, "acc")

        if phases >= 2:
            moe(0)
        if phases >= 3:
            with ExitStack() as s5:
                mem["scratch"] = s5.enter_context(nc.sbuf_tensor("s5_scratch", [P, 8 * P], F32))
                s5_mixer(nc, k, mem)
            layer_norm(nc, mem, 2, "hT")
        if phases >= 4:
            moe(1)
        write_out(nc, k, mem, out)


def constants():
    i = np.arange(P)
    f = np.float32
    offmask = np.zeros((P, LEVELS, P), f)
    for lv in range(LEVELS):
        b = 2 ** lv
        same = i[:, None] // (2 * b) == i[None, :] // (2 * b)
        offmask[:, lv, :] = same & (i[:, None] // b % 2 == 0) & (i[None, :] // b % 2 == 1)
    sel8 = np.zeros((HEADS, HEADS, P), f)
    for h in range(HEADS):
        sel8[h, h, :] = 1.0
    t = np.arange(T)
    tile_tok = i[:, None] + P * np.arange(3)[None, :]
    return {
        "ident": np.eye(P, dtype=f), "offmask": offmask,
        "causal": (i[None, :] >= i[:, None]).astype(f), "sel8": sel8,
        "eps": np.tile(np.array([[NORM_EPS, NORM_EPS * P, LN_EPS]], f), (P, 1)),
        "after": (t[None, None, :] > tile_tok[:, :, None]).astype(f),
        "lower": np.broadcast_to(np.tril(np.ones((GROUPS, GROUPS), f), -1), (P, GROUPS, GROUPS)).copy(),
        "pair_base": (np.arange(E)[:, None] - (i[None, :] >= SLOTS)).astype(f),
        "slot_id": (i % SLOTS).astype(f)[:, None],
        "tok": np.tile(t.astype(f)[None, :], (P, 1)),
    }


def layout(a):
    tile = lambda v: np.ascontiguousarray(np.asarray(v).reshape(-1, P).T)
    a = {n: np.asarray(v) for n, v in a.items()}
    r = {}
    h0 = np.concatenate([a["meta_tokens"], a["x"][0]], axis=0)
    r["h0T"] = h0.T.reshape(DC, P, T).transpose(1, 0, 2)
    r["w_in"] = a["ab_w_in"][0]
    g = a["gdn_conv_w"][0]
    conv = np.concatenate([g[:, D:2 * D], g[:, 0:D], g[:, 2 * D:], a["ab_conv_w"][0]], axis=1)
    r["conv_w"] = conv.reshape(CONV, 32, P).transpose(2, 1, 0)
    r["conv_b"] = tile(a["ab_conv_b"][0])
    w = np.stack([a["lru_w_r"][0], a["lru_w_i"][0]])
    r["lru_w"] = w.reshape(2, 4, 2, P, 2 * P).transpose(3, 0, 1, 2, 4).reshape(P, DC, BLOCK)
    r["lru_b"] = np.concatenate([tile(a["lru_b_r"][0]), tile(a["lru_b_i"][0])], axis=1)
    r["lru_lam"] = tile(a["lru_lambda"][0])
    r["head_par"] = np.stack([a["gdn_a_log"][0], a["gdn_dt_bias"][0]], axis=1)
    r["norm_w"] = a["gdn_norm_w"][0][:, None]
    r["w_out"] = a["ab_w_out"][0]
    ln = []
    for layer in range(DEPTH):
        for kind in ("mix", "ffn"):
            ln += [tile(a[f"ln_{kind}_g"][layer]), tile(a[f"ln_{kind}_b"][layer])]
    r["ln_par"] = np.concatenate(ln, axis=1)
    r["router_w"] = a["moe_w_router"].reshape(DEPTH, DC, P, E).transpose(0, 2, 1, 3)
    r["router_b"] = a["moe_router_bias"]
    r["moe_gate"], r["moe_up"], r["moe_down"] = a["moe_w_gate"], a["moe_w_up"], a["moe_w_down"]
    r["sh_gate"], r["sh_up"], r["sh_down"] = a["moe_shared_w_gate"], a["moe_shared_w_up"], a["moe_shared_w_down"]
    st = lambda v: v.reshape(S5_TILES, P).T
    dt = np.repeat(a["s5_log_dt"][0][:, None], STATES, axis=1)
    r["s5_lam"] = np.stack([st(a["s5_lambda_re"][0]), st(a["s5_lambda_im"][0]), st(dt)], axis=1)
    for name in ("re", "im"):
        b = a[f"s5_b_{name}"][0].reshape(DC, 4, 2, STATES, 16)
        wide = np.zeros((4, 2, 16, DC, 2, STATES), b.dtype)
        c = a[f"s5_c_{name}"][0].reshape(S5_TILES, 2, 16, STATES)
        cw = np.zeros((2, STATES, S5_TILES, 2, 16), c.dtype)
        for g2 in range(2):
            wide[:, g2, :, :, g2, :] = b[:, :, g2].transpose(1, 3, 0, 2)
            cw[g2, :, :, g2, :] = c[:, g2].transpose(2, 0, 1)
        r[f"s5_b_{name}"] = wide.reshape(P, DC, P)
        r[f"s5_c_{name}"] = cw.reshape(P, S5_TILES, 32)
    r["s5_d"] = tile(a["s5_d"][0])
    r["s5_w_out"] = a["s5_w_out"][0]
    return {n: np.ascontiguousarray(v) for n, v in r.items()}


def kernel(**inputs):
    import concourse.bacc as _bacc
    from concourse.bass_utils import run_bass_kernel_spmd as _run

    arrays = layout(inputs) | constants()
    nc = _bacc.Bacc("TRN2", target_bir_lowering=False, num_devices=1)
    k = {n: nc.dram_tensor(f"in_{n}", v.shape, mybir.dt.from_np(v.dtype), kind="ExternalInput").ap()
         for n, v in arrays.items()}
    k["rows_dram"] = nc.dram_tensor("rows_dram", (T, D), F32, kind="Internal").ap()
    out = nc.dram_tensor("out", (1, SEQ, D), F32, kind="ExternalOutput").ap()
    trunk(nc, k, out)
    r = _run(nc, [{f"in_{n}": v for n, v in arrays.items()}], core_ids=[0])
    return r.results[0]["out"]
```

```python
import math
from contextlib import ExitStack

import numpy as np

import concourse.bass as bass
from concourse import mybir

ALU = mybir.AluOpType
ACT = mybir.ActivationFunctionType
AX_X = mybir.AxisListType.X
F32 = mybir.dt.float32
I32 = mybir.dt.int32
U32 = mybir.dt.uint32

P = 128
D = 1024
META = 16
SEQ = 256
T = META + SEQ
DC = D // P
DEPTH = 2
ALPHA = (2.0 * DEPTH) ** 0.25
LN_EPS = 1e-5
NORM_EPS = 1e-6

HEADS = 8
CONV = 4
IN_COLS = 6 * D + 2 * HEADS
CHUNKS = ((0, META), (META, P), (META + P, P))
LEVELS = 7

STATES = 64
S5_TILES = 32
S5_SLICE = 4

E = 64
PAIRS = E // 2
FF = 256
FC = FF // P
SLOTS = 64
TOP = 8
GROUPS = 8
TOP_GROUPS = 4
SCALE = 2.5
TILES = ((0, P), (P, P), (2 * P, META))
BLOCK = 512
LOG1P_TERMS = 9


class Chain:

    def __init__(self, eng, sem):
        self.eng, self.sem, self.n = eng, sem, 0

    def done(self, ins):
        ins.then_inc(self.sem, 1)
        self.n += 1
        self.eng.wait_ge(self.sem, self.n)


class Signals:

    def __init__(self, nc, prefix=""):
        self.nc, self.prefix, self.held = nc, prefix, []

    def __enter__(self):
        return self

    def __call__(self, name):
        self.held.append(self.nc.alloc_semaphore(self.prefix + name))
        return self.held[-1]

    def __exit__(self, *failed):
        if not failed[0]:
            self.nc.clear_and_free_semaphores(self.held)
            self.nc.all_engine_barrier()


def log1p_steps(v, link, out, e, z, z2):
    link(v.tensor_scalar_add(z, e, 2.0))
    link(v.reciprocal(z, z))
    link(v.tensor_tensor(z, z, e, ALU.mult))
    link(v.tensor_tensor(z2, z, z, ALU.mult))
    link(v.memset(out, 1.0 / (2 * LOG1P_TERMS + 1)))
    for k in range(LOG1P_TERMS - 1, -1, -1):
        link(v.tensor_tensor(out, out, z2, ALU.mult))
        link(v.tensor_scalar_add(out, out, 1.0 / (2 * k + 1)))
    link(v.scalar_tensor_tensor(out=out, in0=out, scalar=2.0, in1=z, op0=ALU.mult, op1=ALU.mult))


def in_projection(nc, k, ctx, mem):
    cols = [3 * D, 3 * D + BLOCK, 2 * D, 2 * D + BLOCK, 4 * D, 4 * D + BLOCK, 5 * D, 5 * D + BLOCK,
            D, D + BLOCK, 0, BLOCK]
    per = BLOCK // P
    N_CONV = 32
    conv_of = {n: n for n in range(24)} | {n: n - 8 for n in range(32, 40)}
    conv_w, conv_b, w_bd = mem["conv_w"], mem["conv_b"], mem["w_bd"]
    qkv, xa, y, bd = mem["qkv"], mem["xa"], mem["y"], mem["bd"]
    hT, ring = mem["hT"], mem["dense"]
    with ExitStack() as inner:
        sem = inner.enter_context(Signals(nc))
        cin = inner.enter_context(nc.sbuf_tensor("cin", [P, 4, T + CONV - 1], F32))
        ps = [inner.enter_context(nc.psum_tensor(f"proj{b}", [P, BLOCK], F32)) for b in range(4)]
        loaded = sem("inproj_loaded")
        w_ready = [sem("w_in_even_ready"), sem("w_in_odd_ready")]
        proj_done, evacuated, pads_zero = sem("proj_done"), sem("proj_evacuated"), sem("pads_zero")
        conv_done, conv_step, silu_done = sem("conv_done"), sem("conv_step"), sem("silu_done")
        lam_loaded, angles, sines = sem("s5_lam_loaded"), sem("s5_angles"), sem("s5_sines")
        s5_step, table_step, sliced = sem("s5_coef_step"), sem("s5_doubling_step"), sem("s5_slice_done")
        smem = dict(mem)
        for name, shape, dt in (("lam", [P, 3, S5_TILES], F32), ("par", [P, 15, S5_TILES], F32),
                                ("int", [P, S5_TILES], I32), ("table", [P, S5_TILES, 2, T], F32),
                                ("scratch", [P, S5_TILES * 32], F32)):
            smem[f"s5_{name}"] = inner.enter_context(nc.sbuf_tensor(f"s5_{name}", shape, dt))
        w_in = k["w_in"].rearrange("(c p) n -> p c n", p=P)
        with nc.Block(no_gpsimd_drain=True) as block:

            @block.sync
            def _(sp):
                sp.dma_start(hT[:], k["h0T"]).then_inc(loaded, 16)
                sp.dma_start(smem["s5_lam"][:], k["s5_lam"]).then_inc(lam_loaded, 16)
                sp.dma_start(w_bd[:], w_in[:, :, 6 * D:]).then_inc(loaded, 16)
                for b, c0 in enumerate(cols):
                    if b >= 2:
                        sp.wait_ge(proj_done, 2 + per * (b - 1))
                    sp.dma_start(ring[:, b % 2], w_in[:, :, c0:c0 + BLOCK]).then_inc(w_ready[b % 2], 16)
                    if b == 0:
                        sp.dma_start(conv_w[:], k["conv_w"]).then_inc(loaded, 16)
                        sp.dma_start(conv_b[:], k["conv_b"]).then_inc(loaded, 16)
                        for name in ("ident", "offmask", "causal", "sel8", "lru_b", "lru_lam", "head_par", "norm_w",
                                     "ln_par", "eps"):
                            sp.dma_start(mem[name][:], k[name]).then_inc(mem["consts_loaded"], 16)
                for i in range(S5_TILES // S5_SLICE):
                    js = slice(i * S5_SLICE, (i + 1) * S5_SLICE)
                    sp.wait_ge(sliced, i + 1)
                    sp.dma_start(k["s5_table_dram"][:, js], smem["s5_table"][:, js]).then_inc(mem["tables_stored"], 16)
                sp.wait_ge(mem["tables_stored"], 16 * (S5_TILES // S5_SLICE))

            @block.tensor
            def _(pe):
                pe.wait_ge(loaded, 32 + 32)
                for g in range(2):
                    for c in range(DC):
                        mm = pe.matmul(ps[g][0:HEADS, 0:T], w_bd[:, c, HEADS * g:HEADS * (g + 1)], hT[:, c, :],
                                       start=(c == 0), stop=(c == DC - 1))
                    mm.then_inc(proj_done, 1)
                for n in range(per * len(cols)):
                    g, b = n + 2, n // per
                    if n % per == 0:
                        pe.wait_ge(w_ready[b % 2], 16 * (b // 2 + 1))
                    if g >= 4:
                        pe.wait_ge(evacuated, g - 3)
                    j = n % per
                    for c in range(DC):
                        mm = pe.matmul(ps[g % 4][:, 0:T], ring[:, b % 2, c, j * P:(j + 1) * P], hT[:, c, :],
                                       start=(c == 0), stop=(c == DC - 1))
                    mm.then_inc(proj_done, 1)

            @block.scalar
            def _(act):
                def silu(n):
                    act.wait_ge(conv_done, n + 1)
                    act.activation(qkv[:, n, :], qkv[:, n, :], ACT.Silu).then_inc(silu_done, 1)

                act.wait_ge(lam_loaded, 16)
                s5_sines(act, sines, angles, smem)
                for g in range(2):
                    act.wait_ge(proj_done, g + 1)
                    act.copy(bd[:, g, :], ps[g][0:HEADS, 0:T]).then_inc(evacuated, 1)
                act.wait_ge(pads_zero, 1)
                for n in range(per * len(cols)):
                    src = ps[(n + 2) % 4][:, 0:T]
                    act.wait_ge(proj_done, n + 3)
                    if n in conv_of:
                        cs = conv_of[n]
                        if cs >= 4:
                            act.wait_ge(conv_done, cs - 3)
                        act.copy(cin[:, cs % 4, CONV - 1:], src).then_inc(evacuated, 1)
                    elif n < 32:
                        act.activation(y[:, n - 24 + DC, :], src, ACT.Silu).then_inc(evacuated, 1)
                    else:
                        act.activation(y[:, n - 40, :], src, ACT.Gelu_apprx_tanh).then_inc(evacuated, 1)
                    if 2 <= n < 26:
                        silu(n - 2)

            @block.gpsimd
            def _(pool):
                pool.wait_ge(angles, 3)
                pool.wait_ge(sines, 4)
                s5_tables(pool, Chain(pool, table_step).done, smem, sliced)

            @block.vector
            def _(dve):
                step = Chain(dve, conv_step)
                dve.memset(cin[:, :, 0:CONV - 1], 0.0).then_inc(pads_zero, 1)
                dve.wait_ge(pads_zero, 1)
                dve.wait_ge(lam_loaded, 16)
                s5_discretise(dve, Chain(dve, s5_step).done, sines, angles, smem)
                dve.wait_ge(loaded, 64)
                for n, cs in conv_of.items():
                    dve.wait_ge(evacuated, n + 3)
                    src, dst = cin[:, cs % 4, :], qkv[:, n, :] if n < 24 else xa[:, n - 32, :]
                    w = lambda j: conv_w[:, cs, j:j + 1]
                    if n < 24:
                        step.done(dve.tensor_scalar(dst, src[:, 0:T], w(0), None, ALU.mult))
                    else:
                        step.done(dve.tensor_scalar(dst, src[:, 0:T], w(0), conv_b[:, n - 32:n - 31],
                                                    ALU.mult, ALU.add))
                    for j in (1, 2):
                        step.done(dve.scalar_tensor_tensor(out=dst, in0=src[:, j:j + T], scalar=w(j), in1=dst,
                                                           op0=ALU.mult, op1=ALU.add))
                    dve.scalar_tensor_tensor(out=dst, in0=src[:, 3:3 + T], scalar=w(3), in1=dst,
                                             op0=ALU.mult, op1=ALU.add).then_inc(conv_done, 1)


def group_mixers(nc, k, ctx, mem):
    qkv, xa, y, bd, ring = mem["qkv"], mem["xa"], mem["y"], mem["bd"], mem["dense"]
    ident, offmask, causal, sel8, ones = mem["ident"], mem["offmask"], mem["causal"], mem["sel8"], mem["ones"]
    keys, queries, values = qkv[:, 0:8, :], qkv[:, 8:16, :], qkv[:, 16:24, :]
    NQ = 4
    SETS = [(1, 0, 4), (1, 4, 4), (2, 0, 4), (2, 4, 4), (0, 0, 8)]
    with ExitStack() as inner:
        sem = inner.enter_context(Signals(nc))
        sb = lambda name, shape: inner.enter_context(nc.sbuf_tensor(name, shape, F32))
        bank = [inner.enter_context(nc.psum_tensor(f"mix{b}", [P, BLOCK], F32)) for b in range(8)]
        gates = sb("gates", [P, 2 * DC, T])
        kdec = sb("kdec", [P, 3, HEADS * P])
        vbeta = sb("vbeta", [P, 3, HEADS * P])
        lru_t = vbeta[:].rearrange("p a b -> p (a b)")[:, 0:DC * T].rearrange("p (c t) -> p c t", c=DC)
        lru_u = kdec[:].rearrange("p a b -> p (a b)")[:, 0:DC * T].rearrange("p (c t) -> p c t", c=DC)
        gb = sb("g_rows", [P, HEADS, T])
        kb_o = sb("kb_then_o", [P, HEADS, T])
        sq = sb("squares", [P, 2, T])
        nrm = sb("norms", [P, 2, T])
        LT = sb("LT", [P, 5, 4, P])
        X = sb("X", [P, 4, 4, P])
        Y = sb("Y", [P, 4, 4, P])
        QK = sb("QK", [P, 4, 4, P])
        X0, Y0, QK0 = (sb(n, [META, HEADS, META]) for n in ("X0", "Y0", "QK0"))
        T1, LTo, r, vn = (ring[:, 1, 2 * i:2 * i + 2, :] for i in range(4))
        S = gates[:].rearrange("p c t -> p (c t)")[:, 0:HEADS * P].rearrange("p (h d) -> p h d", h=HEADS)
        colg, colb, kd, egl, nbeg = (sb(n, [P, 3, HEADS]) for n in ("colg", "colb", "kd", "egl", "nbeg"))
        bt = sb("small", [HEADS, 2, T])
        c8, l8 = sb("c8", [P, DC]), sb("l8", [P, 4, DC])
        ea = sb("ea", [HEADS, 1])
        beta, G = bt[:, 0, :], bt[:, 1, :]
        s0, s1, s2, s3 = (kb_o[0:HEADS, i, :] for i in range(4))

        lru_w_ready, w_ready = sem("lru_w_ready"), sem("spare_w")
        s_sq, s_sum, s_nrm, s_qkn = sem("squared"), sem("sums_ready"), sem("norm_ready"), sem("qk_normed")
        s_lg, s_gate = sem("lru_gates_ready"), sem("gates_done")
        act_step, dve_step, pool_step = sem("act_step"), sem("dve_step"), sem("pool_step")
        s_beta, s_x, s_exp, s_ea, s_G = sem("beta_done"), sem("decay_abs"), sem("decay_exp"), sem("ea"), sem("G_done")
        s_lame, s_c8 = sem("lam_exp"), sem("c8_done")
        s_th, s_m, s_sqrt, s_u, s_b, s_scan, s_y = (sem(n) for n in ("tanh_a", "lru_m", "lru_sqrt", "lru_ix",
                                                                     "lru_b_done", "lru_scan", "lru_y"))
        s_bc, s_gb, s_eg, s_kb, s_qg = (sem(n) for n in ("bcast_ready", "g_rows_done", "eg_done", "kb_done", "qg_done"))
        s_col, s_colc, s_kdx, s_kde, s_nb = (sem(n) for n in ("cols_ready", "cols_done", "kd_diff", "kd_exp", "nbeg"))
        s_tt, s_tok = sem("tok_ready"), sem("tok_done")
        s_diff, s_dexp, s_mask, s_kk, s_lt = (sem(n) for n in ("diff", "decay_mat", "decay_masked", "kk_ready", "lt_done"))
        s_lto, s_t1, s_t1c, s_pq, s_x2 = (sem(n) for n in ("lt_off", "t1_ready", "t1_done", "pq_ready", "xy_done"))
        s_init = sem("xy_init")
        s_ks, s_r, s_vn, s_vnc, s_o, s_oc, s_s, s_sc = (sem(n) for n in (
            "ks_ready", "rhs_done", "vnew_ready", "vnew_done", "o_ready", "o_done", "s_ready", "s_done"))
        s_osq, s_osum, s_on, s_of = (sem(n) for n in ("o_squared", "o_sums", "o_norm", "o_final"))
        lru_w = ring[:, 0].rearrange("p c n -> p (c n)").rearrange("p (g h q n) -> p g h q n", g=2, h=4, q=2)

        n_lv = lambda s: LEVELS if s < 4 else 4
        work = [(lv, s) for lv in range(LEVELS) for s in range(5) if lv < n_lv(s)]
        place = {w: i for i, w in enumerate(work)}
        rec = [(cc, half) for cc in range(3) for half in range(2)]

        with nc.Block(no_gpsimd_drain=True) as block:

            @block.sync
            def _(sp):
                sp.dma_start(ring[:, 0], k["lru_w"]).then_inc(lru_w_ready, 16)

            @block.tensor
            def _(pe):
                for i in range(16):
                    pe.wait_ge(s_sq, i + 1)
                    if i >= 2:
                        pe.wait_ge(s_nrm, i - 1)
                    pe.matmul(bank[i % 2][:, 0:T], ones[:], sq[:, i % 2, :], start=True, stop=True).then_inc(s_sum, 1)
                pe.wait_ge(lru_w_ready, 16)
                for i in range(16):
                    g, m = i // 8, i % 8
                    if i >= 2:
                        pe.wait_ge(s_gate, i - 1)
                    for q in range(2):
                        mm = pe.matmul(bank[2 + i % 2][:, 0:T], lru_w[:, g, m // 2, q, (m % 2) * P:(m % 2 + 1) * P],
                                       xa[:, 2 * (m // 2) + q, :], start=(q == 0), stop=(q == 1))
                    mm.then_inc(s_lg, 1)
                pe.wait_ge(s_G, 1)
                pe.wait_ge(s_beta, 1)
                for h in range(HEADS):
                    if h >= 2:
                        pe.wait_ge(s_gb, h - 1)
                        pe.wait_ge(s_kb, h - 1)
                    o = 4 + 2 * (h % 2)
                    pe.matmul(bank[o][:, 0:T], sel8[:, h, :], G, start=True, stop=True).then_inc(s_bc, 1)
                    pe.matmul(bank[o + 1][:, 0:T], sel8[:, h, :], beta, start=True, stop=True).then_inc(s_bc, 1)
                pe.wait_ge(s_nrm, 16)
                for cc, (t0, n) in enumerate(CHUNKS):
                    for q, row in enumerate((G, beta)):
                        mm = pe.transpose(bank[0][0:n, (2 * cc + q) * HEADS:(2 * cc + q + 1) * HEADS],
                                          row[:, t0:t0 + n], ident[0:HEADS, 0:HEADS])
                mm.then_inc(s_col, 1)
                pe.wait_ge(s_gate, 16)
                pe.wait_ge(s_colc, 2)
                pe.wait_ge(s_qkn, 16)
                for i in range(12):
                    cc, q, half = i // 4, i // 2 % 2, i % 2
                    t0, n = CHUNKS[cc]
                    if i >= 4:
                        pe.wait_ge(s_tok, i - 3)
                    for h in range(4):
                        src = (keys, values)[q]
                        mm = pe.transpose(bank[i % 4][0:n, h * P:(h + 1) * P], src[:, 4 * half + h, t0:t0 + n], ident[:])
                    mm.then_inc(s_tt, 1)
                pe.wait_ge(s_kb, HEADS)
                pe.wait_ge(s_gb, HEADS)
                for s, (cc, h0, nh) in enumerate(SETS):
                    t0, n = CHUNKS[cc]
                    if s >= 2:
                        pe.wait_ge(s_lt, 2 * (s - 1))
                    o = 4 + 2 * (s % 2)
                    for q, rhs in enumerate((kb_o, queries)):
                        for h in range(nh):
                            mm = pe.matmul(bank[o + q][0:n, h * n:(h + 1) * n], keys[:, h0 + h, t0:t0 + n],
                                           rhs[:, h0 + h, t0:t0 + n], start=True, stop=True)
                        mm.then_inc(s_kk, 1)
                pe.wait_ge(s_tok, 12)
                pe.wait_ge(s_lt, 10)

                def off_times_x(i):
                    lv, s = work[i]
                    cc, h0, nh = SETS[s]
                    n = CHUNKS[cc][1]
                    pe.wait_ge(s_lto, i + 1)
                    if lv > 0:
                        pe.wait_ge(s_x2, 2 * (place[(lv - 1, s)] + 1))
                    if i >= 2:
                        pe.wait_ge(s_t1c, i - 1)
                    for h in range(nh):
                        lto = LTo[0:n, i % 2, h * n:(h + 1) * n]
                        rhs = ident[0:n, 0:n] if lv == 0 else (X[:, s, h, :] if s < 4 else X0[:, h, :])
                        mm = pe.matmul(bank[i % 2][0:n, h * n:(h + 1) * n], lto, rhs, start=True, stop=True)
                    mm.then_inc(s_t1, 1)

                def products(i):
                    lv, s = work[i]
                    if lv == 0:
                        return
                    cc, h0, nh = SETS[s]
                    n = CHUNKS[cc][1]
                    pe.wait_ge(s_t1c, i + 1)
                    if i >= 2:
                        pe.wait_ge(s_x2, 2 * (i - 1))
                    o = 2 + 2 * (i % 2)
                    for q in range(2):
                        for h in range(nh):
                            t1 = T1[0:n, i % 2, h * n:(h + 1) * n]
                            yy = Y[:, s, h, :] if s < 4 else Y0[:, h, :]
                            a, b = (yy, t1) if q == 0 else (t1, yy)
                            mm = pe.matmul(bank[o + q][0:n, h * n:(h + 1) * n], a, b, start=True, stop=True)
                        mm.then_inc(s_pq, 1)

                for i in range(len(work) + 1):
                    if i < len(work):
                        off_times_x(i)
                    if i >= 1:
                        products(i - 1)
                pe.wait_ge(s_x2, 2 * len(work))
                pe.wait_ge(s_qg, 1)
                pe.wait_ge(s_nb, 1)

                def solve_rhs(i):
                    cc, half = rec[i]
                    t0, n = CHUNKS[cc]
                    if cc > 0:
                        pe.wait_ge(s_sc, i - 1)
                        for h in range(4):
                            mm = pe.matmul(bank[half][:, h * P:(h + 1) * P], keys[:, 4 * half + h, t0:t0 + n],
                                           S[:, 4 * half + h, :], start=True, stop=True)
                        mm.then_inc(s_ks, 1)

                def new_values(i):
                    cc, half = rec[i]
                    t0, n = CHUNKS[cc]
                    if cc > 0:
                        pe.wait_ge(s_r, i - 1)
                    if i >= 2:
                        pe.wait_ge(s_vnc, i - 1)
                    for h in range(4):
                        hh = 4 * half + h
                        if cc > 0:
                            yy, rhs = Y[:, 2 * (cc - 1) + half, h, :], r[:, half, h * P:(h + 1) * P]
                        else:
                            yy, rhs = Y0[:, hh, :], vbeta[0:n, 0, hh * P:(hh + 1) * P]
                        mm = pe.matmul(bank[2 + half][0:n, h * P:(h + 1) * P], yy, rhs, start=True, stop=True)
                    mm.then_inc(s_vn, 1)

                def outputs(i):
                    cc, half = rec[i]
                    t0, n = CHUNKS[cc]
                    pe.wait_ge(s_vnc, i + 1)
                    if i >= 2:
                        pe.wait_ge(s_oc, i - 1)
                    for h in range(4):
                        hh = 4 * half + h
                        out = bank[4 + half][:, h * n:(h + 1) * n]
                        v = vn[0:n, half, h * P:(h + 1) * P]
                        qk = QK[:, 2 * (cc - 1) + half, h, :] if cc > 0 else QK0[:, hh, :]
                        if cc > 0:
                            pe.matmul(out, S[:, hh, :], queries[:, hh, t0:t0 + n], start=True, stop=False)
                        mm = pe.matmul(out, v, qk, start=(cc == 0), stop=True)
                    mm.then_inc(s_o, 1)
                    if cc < 2:
                        if i >= 2:
                            pe.wait_ge(s_sc, i - 1)
                        for h in range(4):
                            hh = 4 * half + h
                            mm = pe.matmul(bank[6 + half][:, h * P:(h + 1) * P], kdec[0:n, cc, hh * P:(hh + 1) * P],
                                           vn[0:n, half, h * P:(h + 1) * P], start=True, stop=True)
                        mm.then_inc(s_s, 1)

                for cc in range(3):
                    for f in (solve_rhs, new_values, outputs):
                        for half in range(2):
                            f(2 * cc + half)
                for h in range(HEADS):
                    pe.wait_ge(s_osq, h + 1)
                    if h >= 2:
                        pe.wait_ge(s_on, h - 1)
                    pe.matmul(bank[h % 2][:, 0:T], ones[:], sq[:, h % 2, :], start=True, stop=True).then_inc(s_osum, 1)

            @block.scalar
            def _(act):
                eps = mem["eps"]
                step = Chain(act, act_step)
                for i in range(17):
                    if i < 16:
                        if i >= 2:
                            act.wait_ge(s_sum, i - 1)
                        act.activation(sq[:, i % 2, :], qkv[:, i, :], ACT.Square).then_inc(s_sq, 1)
                    if i >= 1:
                        j = i - 1
                        act.wait_ge(s_sum, j + 1)
                        if j >= 2:
                            act.wait_ge(s_qkn, j - 1)
                        f = float(P) if j >= 8 else 1.0
                        act.activation(nrm[:, j % 2, :], bank[j % 2][:, 0:T], ACT.Sqrt, scale=f,
                                       bias=eps[:, 0:1] if j < 8 else eps[:, 1:2]).then_inc(s_nrm, 1)
                act.activation(beta, bd[:, 0, :], ACT.Sigmoid).then_inc(s_beta, 1)
                for i in range(16):
                    act.wait_ge(s_lg, i + 1)
                    act.activation(gates[:, i, :], bank[2 + i % 2][:, 0:T], ACT.Sigmoid,
                                   bias=mem["lru_b"][:, i:i + 1]).then_inc(s_gate, 1)
                act.activation(ea[:], mem["head_par"][:, 0:1], ACT.Exp).then_inc(s_ea, 1)
                act.wait_ge(s_x, 1)
                step.done(act.activation(s1, s0, ACT.Abs))
                act.activation(s1, s1, ACT.Exp, scale=-1.0).then_inc(s_exp, 1)
                step.done(act.activation(l8[:, 1, :], mem["lru_lam"][:], ACT.Abs))
                act.activation(l8[:, 1, :], l8[:, 1, :], ACT.Exp, scale=-1.0).then_inc(s_lame, 1)
                act.wait_ge(s_c8, 1)
                act.wait_ge(s_gate, 16)
                for c in range(DC):
                    act.activation(lru_t[:, c, :], gates[:, c, :], ACT.Tanh, scale=c8[:, c:c + 1]).then_inc(s_th, 1)
                act.wait_ge(s_th, DC)
                for c in range(DC):
                    act.activation(gates[:, c, :], gates[:, c, :], ACT.Exp, scale=c8[:, c:c + 1]).then_inc(s_th, 1)
                for h in range(HEADS):
                    act.wait_ge(s_bc, 2 * h + 1)
                    src = bank[4 + 2 * (h % 2)][:, 0:T]
                    act.copy(gb[:, h, :], src).then_inc(s_gb, 1)
                act.wait_ge(s_kdx, 1)
                act.activation(kd[:], kd[:], ACT.Exp).then_inc(s_kde, 1)
                act.activation(egl[:], egl[:], ACT.Exp).then_inc(s_kde, 1)
                act.activation(nbeg[:], nbeg[:], ACT.Exp).then_inc(s_kde, 1)
                for s, (cc, h0, nh) in enumerate(SETS):
                    n = CHUNKS[cc][1]
                    act.wait_ge(s_diff, s + 1)
                    d = LT[0:n, s].rearrange("p a b -> p (a b)")[:, 0:nh * n]
                    act.activation(d, d, ACT.Exp).then_inc(s_dexp, 1)
                act.activation(gb[:], gb[:], ACT.Exp).then_inc(s_eg, 1)
                act.wait_ge(s_m, 1)
                act.activation(lru_t, lru_t, ACT.Sqrt).then_inc(s_sqrt, 1)
                for i, (lv, s) in enumerate(work):
                    cc, h0, nh = SETS[s]
                    n = CHUNKS[cc][1]
                    act.wait_ge(s_t1, i + 1)
                    if i >= 2:
                        before = sum(1 for w in work[:i - 1] if w[0] > 0)
                        if before:
                            act.wait_ge(s_pq, 2 * before)
                        if work[i - 2][0] == 0:
                            act.wait_ge(s_x2, 2 * (i - 1))
                    act.copy(T1[0:n, i % 2, 0:nh * n], bank[i % 2][0:n, 0:nh * n]).then_inc(s_t1c, 1)
                for cc in range(3):
                    t0, n = CHUNKS[cc]
                    for half in range(2):
                        i = 2 * cc + half
                        act.wait_ge(s_vn, i + 1)
                        if i >= 2:
                            act.wait_ge(s_o, i - 1)
                            act.wait_ge(s_s, i - 1)
                        act.copy(vn[0:n, half, :], bank[2 + half][0:n, :]).then_inc(s_vnc, 1)
                    for half in range(2):
                        i = 2 * cc + half
                        act.wait_ge(s_o, i + 1)
                        act.copy(kb_o[:, 4 * half:4 * half + 4, t0:t0 + n],
                                 bank[4 + half][:, 0:4 * n].rearrange("p (h t) -> p h t", h=4)).then_inc(s_oc, 1)
                act.wait_ge(s_oc, 6)
                for h in range(HEADS + 1):
                    if h < HEADS:
                        if h >= 2:
                            act.wait_ge(s_osum, h - 1)
                        act.activation(sq[:, h % 2, :], kb_o[:, h, :], ACT.Square).then_inc(s_osq, 1)
                    if h >= 1:
                        j = h - 1
                        act.wait_ge(s_osum, j + 1)
                        if j >= 2:
                            act.wait_ge(s_of, j - 1)
                        act.activation(nrm[:, j % 2, :], bank[j % 2][:, 0:T], ACT.Sqrt, scale=1.0 / P,
                                       bias=eps[:, 0:1]).then_inc(s_on, 1)

            @block.gpsimd
            def _(pool):
                step = Chain(pool, pool_step)
                pool.wait_ge(s_gate, 16)
                pool.tensor_tensor(gates[:, DC:, :], gates[:, DC:, :], xa[:], ALU.mult).then_inc(s_u, 1)
                for s, (cc, h0, nh) in enumerate(SETS):
                    n = CHUNKS[cc][1]
                    pool.wait_ge(s_dexp, s + 1)
                    d = LT[0:n, s].rearrange("p a b -> p (a b)")[:, 0:nh * n].rearrange("p (h t) -> p h t", h=nh)
                    pool.tensor_tensor(d, d, causal[0:n, 0:n].unsqueeze(1).broadcast_to([n, nh, n]),
                                       ALU.mult).then_inc(s_mask, 1)
                pool.wait_ge(s_lt, 10)
                for i, (lv, s) in enumerate(work):
                    cc, h0, nh = SETS[s]
                    n = CHUNKS[cc][1]
                    if i >= 2:
                        pool.wait_ge(s_t1, i - 1)
                        if work[i - 2][0] == 0:
                            pool.wait_ge(s_x2, 2 * (i - 1))
                    d = LT[0:n, s].rearrange("p a b -> p (a b)")[:, 0:nh * n].rearrange("p (h t) -> p h t", h=nh)
                    o = LTo[0:n, i % 2, 0:nh * n].rearrange("p (h t) -> p h t", h=nh)
                    pool.tensor_tensor(o, d, offmask[0:n, lv, 0:n].unsqueeze(1).broadcast_to([n, nh, n]),
                                       ALU.mult).then_inc(s_lto, 1)
                    if i == 14:
                        pool.wait_ge(s_scan, DC)
                        pool.tensor_tensor(y[:, 0:DC, :], y[:, 0:DC, :], xa[:], ALU.mult).then_inc(s_y, 1)

            @block.vector
            def _(dve):
                step = Chain(dve, dve_step)
                link = step.done
                link(dve.memset(colg[:], 0.0))
                link(dve.memset(colb[:], 0.0))
                hp, lam = mem["head_par"], mem["lru_lam"]
                dve.tensor_scalar(s0, bd[:, 1, :], hp[:, 1:2], None, ALU.add).then_inc(s_x, 1)
                for i in range(16):
                    dve.wait_ge(s_nrm, i + 1)
                    link(dve.reciprocal(nrm[:, i % 2, :], nrm[:, i % 2, :]))
                    dve.tensor_tensor(qkv[:, i, :], qkv[:, i, :], nrm[:, i % 2, :], ALU.mult).then_inc(s_qkn, 1)
                dve.wait_ge(s_exp, 1)
                log1p_steps(dve, link, s2, s1, s3, bd[:, 1, :])
                link(dve.scalar_tensor_tensor(out=s0, in0=s0, scalar=0.0, in1=s2, op0=ALU.max, op1=ALU.add))
                dve.wait_ge(s_ea, 1)
                link(dve.tensor_scalar(s0, s0, ea[:, 0:1], -1.0, ALU.mult, ALU.mult))
                link(dve.memset(s1, 1.0))
                for t0, n in CHUNKS:
                    dve.tensor_tensor_scan(G[:, t0:t0 + n], s1[:, t0:t0 + n], s0[:, t0:t0 + n], 0.0,
                                           ALU.mult, ALU.add).then_inc(dve_step, 1)
                    step.n += 1
                dve.wait_ge(dve_step, step.n)
                dve.memset(s1[:, 0:1], 1.0).then_inc(s_G, 1)
                dve.wait_ge(s_lame, 1)
                log1p_steps(dve, link, l8[:, 0, :], l8[:, 1, :], l8[:, 2, :], l8[:, 3, :])
                link(dve.tensor_scalar(l8[:, 2, :], lam[:], -1.0, 0.0, ALU.mult, ALU.max))
                link(dve.tensor_tensor(l8[:, 0, :], l8[:, 0, :], l8[:, 2, :], ALU.add))
                dve.tensor_scalar(c8[:], l8[:, 0, :], -8.0, None, ALU.mult).then_inc(s_c8, 1)
                for h in range(HEADS):
                    dve.wait_ge(s_bc, 2 * h + 2)
                    dve.wait_ge(s_qkn, 16)
                    dve.tensor_tensor(kb_o[:, h, :], keys[:, h, :], bank[5 + 2 * (h % 2)][:, 0:T],
                                      ALU.mult).then_inc(s_kb, 1)
                dve.wait_ge(s_col, 1)
                for q, dst in enumerate((colg, colb)):
                    src = bank[0][:, 0:6 * HEADS].rearrange("p (c q h) -> p c q h", c=3, q=2)
                    link(dve.tensor_copy(dst[0:META, 0, :], src[0:META, 0, q, :]))
                    dve.tensor_copy(dst[:, 1:3, :], src[:, 1:3, q, :]).then_inc(s_colc, 1)
                    dve.wait_ge(s_colc, q + 1)
                dve.wait_ge(s_gb, HEADS)
                for cc, (t0, n) in enumerate(CHUNKS):
                    link(dve.tensor_copy(egl[:, cc, :], gb[:, :, t0 + n - 1]))
                link(dve.tensor_copy(nbeg[:], colg[:]))
                dve.tensor_tensor(kd[:], egl[:], colg[:], ALU.subtract).then_inc(s_kdx, 1)
                for s, (cc, h0, nh) in enumerate(SETS):
                    t0, n = CHUNKS[cc]
                    d = LT[0:n, s].rearrange("p a b -> p (a b)")[:, 0:nh * n].rearrange("p (h t) -> p h t", h=nh)
                    link(dve.tensor_tensor(d, gb[0:n, h0:h0 + nh, t0:t0 + n],
                                           colg[0:n, cc, h0:h0 + nh].unsqueeze(2).broadcast_to([n, nh, n]),
                                           ALU.subtract))
                    dve.tensor_scalar(d, d, 0.0, None, ALU.min).then_inc(s_diff, 1)
                dve.wait_ge(s_th, 2 * DC)
                link(dve.tensor_scalar(lru_u, lru_t, -1.0, 1.0, ALU.mult, ALU.add))
                link(dve.reciprocal(lru_u, lru_u))
                dve.scalar_tensor_tensor(out=lru_t.rearrange("p c t -> p (c t)"),
                                         in0=lru_t.rearrange("p c t -> p (c t)"), scalar=-2.0,
                                         in1=lru_u.rearrange("p c t -> p (c t)"),
                                         op0=ALU.mult, op1=ALU.mult).then_inc(s_m, 1)
                dve.wait_ge(s_kde, 3)
                link(dve.scalar_tensor_tensor(out=nbeg[:].rearrange("p a b -> p (a b)"),
                                              in0=nbeg[:].rearrange("p a b -> p (a b)"), scalar=-1.0,
                                              in1=colb[:].rearrange("p a b -> p (a b)"), op0=ALU.mult, op1=ALU.mult))
                dve.memset(s1[:, 0:1], 1.0).then_inc(s_nb, 1)
                dve.wait_ge(s_nb, 1)
                dve.wait_ge(s_sqrt, 1)
                dve.wait_ge(s_u, 1)
                dve.tensor_tensor(gates[:, DC:, :], gates[:, DC:, :], lru_t, ALU.mult).then_inc(s_b, 1)
                dve.wait_ge(s_b, 1)
                for i in range(12):
                    cc, q, half = i // 4, i // 2 % 2, i % 2
                    t0, n = CHUNKS[cc]
                    dve.wait_ge(s_tt, i + 1)
                    dst, col = ((kdec, kd), (vbeta, colb))[q]
                    dve.tensor_tensor(
                        dst[0:n, cc, 4 * half * P:4 * (half + 1) * P].rearrange("p (h d) -> p h d", h=4),
                        bank[i % 4][0:n, :].rearrange("p (h d) -> p h d", h=4),
                        col[0:n, cc, 4 * half:4 * half + 4].unsqueeze(2).broadcast_to([n, 4, P]),
                        ALU.mult).then_inc(s_tok, 1)
                for s, (cc, h0, nh) in enumerate(SETS):
                    n = CHUNKS[cc][1]
                    o = 4 + 2 * (s % 2)
                    d = LT[0:n, s].rearrange("p a b -> p (a b)")[:, 0:nh * n]
                    qk = QK[:, s].rearrange("p a b -> p (a b)") if s < 4 else QK0[:].rearrange("p a b -> p (a b)")
                    dve.wait_ge(s_mask, s + 1)
                    dve.wait_ge(s_kk, 2 * s + 2)
                    dve.tensor_tensor(qk, d, bank[o + 1][0:n, 0:nh * n], ALU.mult).then_inc(s_lt, 1)
                    dve.wait_ge(s_lt, 2 * s + 1)
                    dve.tensor_tensor(d, d, bank[o][0:n, 0:nh * n], ALU.mult).then_inc(s_lt, 1)
                dve.wait_ge(s_kk, 10)
                dve.wait_ge(s_eg, 1)
                dve.tensor_tensor(queries, queries, gb[:], ALU.mult).then_inc(s_qg, 1)
                for i, (lv, s) in enumerate(work):
                    cc, h0, nh = SETS[s]
                    n = CHUNKS[cc][1]
                    if lv == 0:
                        idb = ident[0:n, 0:n].unsqueeze(1).broadcast_to([n, nh, n])
                        xx = X[:, s] if s < 4 else X0[:]
                        yy = Y[:, s] if s < 4 else Y0[:]
                        dve.wait_ge(s_t1c, i + 1)
                        dve.tensor_tensor(xx, idb, T1[0:n, i % 2, 0:nh * n].rearrange("p (h t) -> p h t", h=nh),
                                          ALU.subtract).then_inc(s_x2, 1)
                        dve.tensor_tensor(yy, idb, LTo[0:n, i % 2, 0:nh * n].rearrange("p (h t) -> p h t", h=nh),
                                          ALU.subtract).then_inc(s_x2, 1)
                        continue
                    o = 2 + 2 * (i % 2)
                    m = sum(1 for w in work[:i + 1] if w[0] > 0)
                    for q in range(2):
                        t = ((X, X0), (Y, Y0))[q][s == 4]
                        t = (t[:, s] if s < 4 else t[:]).rearrange("p a b -> p (a b)")
                        dve.wait_ge(s_pq, 2 * m)
                        if i >= 1:
                            dve.wait_ge(s_x2, 2 * i)
                        dve.tensor_tensor(t, t, bank[o + q][0:n, 0:nh * n], ALU.subtract).then_inc(s_x2, 1)
                    if 5 <= i < 5 + DC:
                        c = i - 5
                        dve.wait_ge(s_u, 1)
                        dve.tensor_tensor_scan(xa[:, c, :], gates[:, c, :], gates[:, DC + c, :], 0.0,
                                               ALU.mult, ALU.add).then_inc(s_scan, 1)
                for cc in range(3):
                    t0, n = CHUNKS[cc]
                    if cc > 0:
                        for half in range(2):
                            i = 2 * cc + half
                            dve.wait_ge(s_ks, i - 1)
                            rr = r[:, half, :].rearrange("p (h d) -> p h d", h=4)
                            if cc > 1:
                                dve.wait_ge(s_vn, i - 1)
                            link(dve.tensor_tensor(rr, bank[half][:].rearrange("p (h d) -> p h d", h=4),
                                                   nbeg[:, cc, 4 * half:4 * half + 4].unsqueeze(2).broadcast_to([P, 4, P]),
                                                   ALU.mult))
                            dve.tensor_tensor(r[:, half, :], r[:, half, :],
                                              vbeta[:, cc, 4 * half * P:4 * (half + 1) * P], ALU.add).then_inc(s_r, 1)
                    if cc < 2:
                        for half in range(2):
                            i = 2 * cc + half
                            sh = S[:, 4 * half:4 * half + 4, :]
                            dve.wait_ge(s_s, i + 1)
                            src = bank[6 + half][:].rearrange("p (h d) -> p h d", h=4)
                            if cc == 0:
                                dve.tensor_copy(sh, src).then_inc(s_sc, 1)
                                continue
                            link(dve.tensor_tensor(sh, sh, egl[:, cc, 4 * half:4 * half + 4].unsqueeze(2).broadcast_to(
                                [P, 4, P]), ALU.mult))
                            dve.tensor_tensor(sh, sh, src, ALU.add).then_inc(s_sc, 1)
                for h in range(HEADS):
                    dve.wait_ge(s_on, h + 1)
                    link(dve.reciprocal(nrm[:, h % 2, :], nrm[:, h % 2, :]))
                    link(dve.tensor_tensor(kb_o[:, h, :], kb_o[:, h, :], nrm[:, h % 2, :], ALU.mult))
                    dve.scalar_tensor_tensor(out=y[:, DC + h, :], in0=kb_o[:, h, :], scalar=mem["norm_w"][:, 0:1],
                                             in1=y[:, DC + h, :], op0=ALU.mult, op1=ALU.mult).then_inc(s_of, 1)
                dve.wait_ge(s_y, 1)


def gate_up_weights(mem, s):
    return mem["experts"][:, s, 0:2 * D * FF // P].rearrange("p (c n) -> p c n", c=DC)


def down_weights(mem, s):
    return mem["experts"][:, s, 2 * D * FF // P:].rearrange("p (c n) -> p c n", c=FC)


def load_gate_up(sp, k, mem, layer, q, u):
    for e in range(2):
        w = gate_up_weights(mem, 2 * (u % 2) + e)
        for name, cols in (("moe_gate", slice(0, FF)), ("moe_up", slice(FF, 2 * FF))):
            src = k[name][layer].rearrange("e (p c) f -> e p c f", p=P)[q * 2 + e]
            sp.dma_start(w[:, :, cols], src).then_inc(mem["gate_up_ready"][layer][u % 2], 16)


def load_down(sp, k, mem, layer, q, u):
    for e in range(2):
        src = k["moe_down"][layer].rearrange("e (c p) d -> e p c d", p=P)[q * 2 + e]
        sp.dma_start(down_weights(mem, 2 * (u % 2) + e), src).then_inc(mem["down_ready"][layer][u % 2], 16)


def layer_norm(nc, k, mem, which, source, next_experts=None):
    hT, acc, ones, ln, eps = mem["hT"], mem["acc"], mem["ones"], mem["ln_par"], mem["eps"]
    with ExitStack() as inner:
        sem = inner.enter_context(Signals(nc, f"ln{which}_"))
        sb = lambda name, shape: inner.enter_context(nc.sbuf_tensor(f"ln{which}_{name}", shape, F32))
        sums = inner.enter_context(nc.psum_tensor(f"ln{which}_sums", [P, BLOCK], F32))
        sqs = inner.enter_context(nc.psum_tensor(f"ln{which}_sqs", [P, BLOCK], F32))
        sq = sb("sq", [P, DC, T])
        mean, rstd = sb("mean", [P, T]), sb("rstd", [P, T])
        added, summed, meaned, centred = sem("added"), sem("summed"), sem("meaned"), sem("centred")
        squared, sq_summed, rooted, inverted, scaled, out = (sem("squared"), sem("sq_summed"), sem("rooted"),
                                                             sem("inverted"), sem("scaled"), sem("out"))
        with nc.Block(no_gpsimd_drain=True) as block:
            if next_experts is not None:

                @block.sync
                def _(sp):
                    for q in range(2):
                        load_gate_up(sp, k, mem, next_experts, q, q)
                        load_down(sp, k, mem, next_experts, q, q)

            @block.tensor
            def _(pe):
                for c in range(DC):
                    if source == "acc":
                        pe.wait_ge(added, c + 1)
                    mm = pe.matmul(sums[:, 0:T], ones[:], hT[:, c, :], start=(c == 0), stop=(c == DC - 1))
                mm.then_inc(summed, 1)
                for c in range(DC):
                    pe.wait_ge(squared, c + 1)
                    mm = pe.matmul(sqs[:, 0:T], ones[:], sq[:, c, :], start=(c == 0), stop=(c == DC - 1))
                mm.then_inc(sq_summed, 1)

            @block.scalar
            def _(act):
                for c in range(DC):
                    act.wait_ge(centred, c + 1)
                    act.activation(sq[:, c, :], hT[:, c, :], ACT.Square).then_inc(squared, 1)
                act.wait_ge(sq_summed, 1)
                act.activation(rstd[:], sqs[:, 0:T], ACT.Sqrt, scale=1.0 / D, bias=eps[:, 2:3]).then_inc(rooted, 1)

            @block.vector
            def _(dve):
                if source == "acc":
                    for c in range(DC):
                        dve.scalar_tensor_tensor(out=hT[:, c, :], in0=hT[:, c, :], scalar=ALPHA, in1=acc[:, c, :],
                                                 op0=ALU.mult, op1=ALU.add).then_inc(added, 1)
                dve.wait_ge(summed, 1)
                dve.tensor_scalar(mean[:], sums[:, 0:T], 1.0 / D, None, ALU.mult).then_inc(meaned, 1)
                dve.wait_ge(meaned, 1)
                for c in range(DC):
                    dve.tensor_tensor(hT[:, c, :], hT[:, c, :], mean[:], ALU.subtract).then_inc(centred, 1)
                dve.wait_ge(rooted, 1)
                dve.reciprocal(rstd[:], rstd[:]).then_inc(inverted, 1)
                dve.wait_ge(inverted, 1)
                for c in range(DC):
                    dve.tensor_tensor(hT[:, c, :], hT[:, c, :], rstd[:], ALU.mult).then_inc(scaled, 1)
                for c in range(DC):
                    dve.wait_ge(scaled, c + 1)
                    dve.tensor_scalar(hT[:, c, :], hT[:, c, :], ln[:, 2 * which * DC + c:2 * which * DC + c + 1],
                                      ln[:, (2 * which + 1) * DC + c:(2 * which + 1) * DC + c + 1],
                                      ALU.mult, ALU.add).then_inc(out, 1)


def out_projection(nc, k, mem):
    hT, y, ring = mem["hT"], mem["y"], mem["dense"]
    KC = 2 * DC
    NB, cols = 4, D // 4
    with ExitStack() as inner:
        sem = inner.enter_context(Signals(nc))
        ps = [inner.enter_context(nc.psum_tensor(f"outp{b}", [P, BLOCK], F32)) for b in range(4)]
        ready = [sem("w_out_even"), sem("w_out_odd")]
        projected, added = sem("out_projected"), sem("out_added")
        w = k["w_out"].rearrange("(c p) n -> p c n", p=P)
        with nc.Block(no_gpsimd_drain=True) as block:

            @block.sync
            def _(sp):
                for b in range(NB):
                    if b >= 2:
                        sp.wait_ge(projected, 2 * (b - 1))
                    dst = ring[:, b % 2].rearrange("p c n -> p (c n)").rearrange("p (c n) -> p c n", c=KC)
                    sp.dma_start(dst, w[:, :, b * cols:(b + 1) * cols]).then_inc(ready[b % 2], 16)

            @block.tensor
            def _(pe):
                for m in range(DC):
                    b = m // 2
                    if m % 2 == 0:
                        pe.wait_ge(ready[b % 2], 16 * (b // 2 + 1))
                    if m >= 4:
                        pe.wait_ge(added, m - 3)
                    wv = ring[:, b % 2].rearrange("p c n -> p (c n)").rearrange("p (c n) -> p c n", c=KC)
                    for c in range(KC):
                        mm = pe.matmul(ps[m % 4][:, 0:T], wv[:, c, (m % 2) * P:(m % 2 + 1) * P], y[:, c, :],
                                       start=(c == 0), stop=(c == KC - 1))
                    mm.then_inc(projected, 1)

            @block.vector
            def _(dve):
                for m in range(DC):
                    dve.wait_ge(projected, m + 1)
                    dve.scalar_tensor_tensor(out=hT[:, m, :], in0=hT[:, m, :], scalar=ALPHA, in1=ps[m % 4][:, 0:T],
                                             op0=ALU.mult, op1=ALU.add).then_inc(added, 1)


def router_and_shared(nc, k, mem, layer):
    hT, acc, ring, ident, pg = mem["hT"], mem["acc"], mem["dense"], mem["ident"], mem["pg"]
    with ExitStack() as inner:
        sem = inner.enter_context(Signals(nc, f"r{layer}_"))
        sb = lambda name, shape, dt=F32: inner.enter_context(nc.sbuf_tensor(f"r{layer}_{name}", shape, dt))
        bank = [inner.enter_context(nc.psum_tensor(f"r{layer}_b{b}", [P, BLOCK], F32)) for b in range(8)]
        rows = sb("rows", [P, 3, D])
        wr, rb = sb("wr", [P, DC, E]), sb("rb", [P, E])
        after, lower = sb("after", [P, 3, T]), sb("lower", [P, GROUPS, GROUPS])
        sc, bi, mb, mr, sel, gt = (sb(n, [P, 3, E]) for n in ("sc", "bi", "mb", "mr", "sel", "gt"))
        m8 = sb("m8", [P, 3 * GROUPS, 8])
        gs, rk, gm = (sb(n, [P, 3, GROUPS]) for n in ("gs", "rk", "gm"))
        cmp, eq = sb("cmp", [P, 3 * GROUPS, GROUPS]), sb("eq", [P, 3 * GROUPS, GROUPS])
        t8, ws = sb("t8", [P, 3, 8]), sb("ws", [P, 3])
        maskT = sb("maskT", [E, T])
        cm = sb("cm", [E, 1])
        row = sb("row", [1, 2])
        actT = sb("actT", [P, FC, T])
        silu = sb("silu", [P, FC, T])
        loaded, gu_ready, dn_ready = sem("loaded"), sem("shared_gu_ready"), sem("shared_down_ready")
        rows_t, rows_c, stored = sem("rows_turned"), sem("rows_copied"), mem["rows_stored"]
        zero, logits, scored, step_s = sem("zeroed"), sem("logits"), sem("scored"), sem("step")
        selected, gated, ranked, placed = sem("selected"), sem("gated"), sem("ranked"), sem("placed")
        counted, maxed = sem("count_turned"), mem["count_ready"]
        sh_gu, sh_act, sh_mul, sh_dn, sh_out = (sem(n) for n in ("sh_gu", "sh_silu", "sh_mul", "sh_down", "sh_out"))
        w_gu = ring[:, 0]
        w_dn = ring[:, 1].rearrange("p c n -> p (c n)")[:, 0:FC * D].rearrange("p (c n) -> p c n", c=FC)
        with nc.Block(no_gpsimd_drain=True) as block:

            @block.sync
            def _(sp):
                sp.dma_start(wr[:], k["router_w"][layer]).then_inc(loaded, 16)
                sp.dma_start(rb[:], k["router_b"][layer:layer + 1, :].broadcast_to([P, E])).then_inc(loaded, 16)
                sp.dma_start(after[:], k["after"]).then_inc(loaded, 16)
                sp.dma_start(lower[:], k["lower"]).then_inc(loaded, 16)
                for q, name in enumerate(("sh_gate", "sh_up")):
                    sp.dma_start(w_gu[:, :, q * FF:(q + 1) * FF],
                                 k[name][layer].rearrange("(c p) f -> p c f", p=P)).then_inc(gu_ready, 16)
                sp.dma_start(w_dn, k["sh_down"][layer].rearrange("(c p) d -> p c d", p=P)).then_inc(dn_ready, 16)
                for tt, (t0, n) in enumerate(TILES):
                    sp.wait_ge(rows_c, 2 * tt + 2)
                    sp.dma_start(mem["rows_dram"][t0:t0 + n, :], rows[0:n, tt, :]).then_inc(stored, 16)

            @block.tensor
            def _(pe):
                pe.wait_ge(loaded, 64)
                for tt, (t0, n) in enumerate(TILES):
                    for c in range(DC):
                        mm = pe.matmul(bank[0][0:n, tt * E:(tt + 1) * E], hT[:, c, t0:t0 + n], wr[:, c, :],
                                       start=(c == 0), stop=(c == DC - 1))
                mm.then_inc(logits, 1)
                for i in range(6):
                    tt, half = i // 2, i % 2
                    t0, n = TILES[tt]
                    if i >= 2:
                        pe.wait_ge(rows_c, i - 1)
                    for c in range(4):
                        mm = pe.transpose(bank[1 + i % 2][0:n, c * P:(c + 1) * P], hT[:, 4 * half + c, t0:t0 + n],
                                          ident[:])
                    mm.then_inc(rows_t, 1)
                pe.wait_ge(gu_ready, 32)
                for m in range(4):
                    for c in range(DC):
                        mm = pe.matmul(bank[3 + m][:, 0:T], w_gu[:, c, m * P:(m + 1) * P], hT[:, c, :],
                                       start=(c == 0), stop=(c == DC - 1))
                    mm.then_inc(sh_gu, 1)
                pe.wait_ge(dn_ready, 16)
                pe.wait_ge(sh_mul, FC)
                for m in range(DC):
                    if m >= 2:
                        pe.wait_ge(sh_out, m - 1)
                    for c in range(FC):
                        mm = pe.matmul(bank[3 + m % 2][:, 0:T], w_dn[:, c, m * P:(m + 1) * P], actT[:, c, :],
                                       start=(c == 0), stop=(c == FC - 1))
                    mm.then_inc(sh_dn, 1)
                pe.wait_ge(selected, 1)
                for tt, (t0, n) in enumerate(TILES):
                    mm = pe.matmul(bank[7][0:E, 0:T], sel[0:n, tt, :], after[0:n, tt, :], start=(tt == 0), stop=(tt == 2))
                mm.then_inc(ranked, 1)
                pe.wait_ge(gated, 1)
                pe.wait_ge(rows_c, 6)
                for q, src in enumerate((sel, gt)):
                    for tt, (t0, n) in enumerate(TILES):
                        mm = pe.transpose(bank[1 + q][0:E, t0:t0 + n], src[0:n, tt, :], ident[0:n, 0:n])
                    mm.then_inc(ranked, 1)
                pe.wait_ge(counted, 1)
                pe.transpose(bank[0][0:1, 0:E], cm[:, 0:1], ident[0:E, 0:E]).then_inc(ranked, 1)

            @block.scalar
            def _(act):
                act.wait_ge(logits, 1)
                act.wait_ge(zero, 1)
                lg = bank[0][:, 0:3 * E].rearrange("p (t e) -> p t e", t=3)
                act.activation(sc[:, 0:2, :], lg[:, 0:2, :], ACT.Sigmoid).then_inc(scored, 1)
                act.activation(sc[0:META, 2, :], lg[0:META, 2, :], ACT.Sigmoid).then_inc(scored, 1)
                for i in range(6):
                    tt, half = i // 2, i % 2
                    n = TILES[tt][1]
                    act.wait_ge(rows_t, i + 1)
                    src = bank[1 + i % 2][0:n, :].rearrange("p (c q r) -> p c q r", c=4, r=DC)
                    dst = rows[0:n, tt, :].rearrange("p (r c q) -> p c q r", r=DC, c=DC)[:, 4 * half:4 * half + 4]
                    act.copy(dst, src).then_inc(rows_c, 1)
                for m in range(FC):
                    act.wait_ge(sh_gu, m + 1)
                    act.activation(silu[:, m, :], bank[3 + m][:, 0:T], ACT.Silu).then_inc(sh_act, 1)
                for m in range(DC):
                    act.wait_ge(sh_dn, m + 1)
                    act.copy(acc[:, m, :], bank[3 + m % 2][:, 0:T]).then_inc(sh_out, 1)

            @block.vector
            def _(dve):
                step = Chain(dve, step_s)
                link = step.done
                dve.memset(sc[:], 0.5).then_inc(zero, 1)
                dve.wait_ge(loaded, 64)
                dve.wait_ge(scored, 2)
                link(dve.tensor_tensor(bi[:], sc[:], rb[:].unsqueeze(1).broadcast_to([P, 3, E]), ALU.add))
                for i in range(3 * GROUPS):
                    ins = dve.max(out=m8[:, i, :], in_=bi[:, i // GROUPS, (i % GROUPS) * 8:(i % GROUPS + 1) * 8])
                link(ins)
                gsf = gs[:].rearrange("p t g -> p (t g)")
                link(dve.tensor_tensor(gsf, m8[:, :, 0], m8[:, :, 1], ALU.add))
                for tt in range(3):
                    a = gs[:, tt, :].unsqueeze(1).broadcast_to([P, GROUPS, GROUPS])
                    b = gs[:, tt, :].unsqueeze(2).broadcast_to([P, GROUPS, GROUPS])
                    o = slice(tt * GROUPS, (tt + 1) * GROUPS)
                    link(dve.tensor_tensor(cmp[:, o, :], a, b, ALU.is_gt))
                    link(dve.tensor_tensor(eq[:, o, :], a, b, ALU.is_equal))
                    link(dve.tensor_tensor(eq[:, o, :], eq[:, o, :], lower[:], ALU.mult))
                link(dve.tensor_tensor(cmp[:], cmp[:], eq[:], ALU.add))
                link(dve.tensor_reduce(rk[:].rearrange("p t g -> p (t g)"), cmp[:], AX_X, ALU.add))
                link(dve.tensor_scalar(gm[:], rk[:], float(TOP_GROUPS), None, ALU.is_lt))
                link(dve.tensor_scalar(rk[:], gm[:], 1e30, -1e30, ALU.mult, ALU.add))
                wide = lambda t: t[:].rearrange("p t g -> p (t g)").unsqueeze(2).broadcast_to([P, 3 * GROUPS, 8])
                flat = lambda t: t[:].rearrange("p t (g i) -> p (t g) i", i=8)
                link(dve.tensor_tensor(flat(mb), flat(bi), wide(gm), ALU.mult))
                link(dve.tensor_tensor(flat(mb), flat(mb), wide(rk), ALU.add))
                for tt in range(3):
                    link(dve.max(out=t8[:, tt, :], in_=mb[:, tt, :]))
                    link(dve.match_replace(out=mr[:, tt, :], in_to_replace=t8[:, tt, :], in_values=mb[:, tt, :],
                                           imm_value=-3e30))
                dve.tensor_tensor(sel[:], mr[:], mb[:], ALU.not_equal).then_inc(selected, 1)
                dve.wait_ge(selected, 1)
                link(dve.tensor_tensor(gt[:], sc[:], sel[:], ALU.mult))
                link(dve.tensor_reduce(ws[:], gt[:], AX_X, ALU.add))
                link(dve.reciprocal(ws[:], ws[:]))
                link(dve.tensor_scalar(ws[:], ws[:], SCALE, None, ALU.mult))
                dve.tensor_tensor(gt[:], gt[:], ws[:].unsqueeze(2).broadcast_to([P, 3, E]), ALU.mult).then_inc(gated, 1)
                for m in range(FC):
                    dve.wait_ge(sh_act, m + 1)
                    dve.wait_ge(sh_gu, FC + m + 1)
                    dve.tensor_tensor(actT[:, m, :], silu[:, m, :], bank[3 + FC + m][:, 0:T],
                                      ALU.mult).then_inc(sh_mul, 1)
                dve.wait_ge(ranked, 2)
                link(dve.tensor_copy(maskT[:], bank[1][0:E, 0:T]))
                link(dve.scalar_tensor_tensor(out=pg[:, 0, :], in0=bank[7][0:E, 0:T], scalar=1.0, in1=maskT[:],
                                              op0=ALU.add, op1=ALU.mult))
                link(dve.tensor_reduce(cm[:], pg[:, 0, :], AX_X, ALU.max))
                dve.tensor_scalar_add(pg[:, 0, :], pg[:, 0, :], -1.0).then_inc(counted, 1)
                dve.wait_ge(ranked, 3)
                dve.tensor_copy(pg[:, 1, :], bank[2][0:E, 0:T]).then_inc(placed, 1)
                dve.wait_ge(ranked, 4)
                link(dve.tensor_reduce(row[:, 0:1], bank[0][0:1, 0:E], AX_X, ALU.max))
                dve.tensor_copy(mem["count"][:], row[:, 0:1]).then_inc(maxed, 1)


def experts(nc, k, mem, layer):
    acc, ident, pg = mem["acc"], mem["ident"], mem["pg"]
    base, slot_id, tok = mem["pair_base"], mem["slot_id"], mem["tok"]
    AHEAD = 3
    with ExitStack() as inner:
        sem = inner.enter_context(Signals(nc, f"e{layer}_"))
        sb = lambda name, shape, dt=F32: inner.enter_context(nc.sbuf_tensor(f"e{layer}_{name}", shape, dt))
        bank = [inner.enter_context(nc.psum_tensor(f"e{layer}_b{b}", [P, BLOCK], F32)) for b in range(8)]
        t0b, t1b, gub, atb, y0b, y1b = bank[:6]
        cb = bank[6:]
        xg = sb("xg", [P, 2, D])
        xgT = sb("xgT", [P, 2, DC, P])
        selw = sb("selw", [E, 2, P])
        basew = sb("basew", [E, P])
        gsb, hit = sb("gsb", [P, T]), sb("hit", [P, T])
        sg = sb("sg", [P, 4, T])
        idf, idx = sb("idf", [P, 1]), sb("idx", [P, 4, 1], I32)
        sl, ac, aT, ys = sb("sl", [P, FF]), sb("ac", [P, FF]), sb("aT", [P, FC, P]), sb("ys", [P, D])
        gu_ready, dn_ready = mem["gate_up_ready"][layer], mem["down_ready"][layer]
        based, selw_ok, sel_mm, gate_in, sg_ok, idf_ok, idx_ok = (sem(n) for n in (
            "base_moved", "pair_selected", "rows_broadcast", "gates_in", "scatter_ready", "index_summed", "index_ready"))
        gathered = [sem("gathered_even"), sem("gathered_odd")]
        going = sem("gather_going")
        turned, ev0, ev1 = sem("turned"), sem("turned_in_a"), sem("turned_in_b")
        gu, sil, mul, at, ate = sem("gate_up"), sem("silu"), sem("gated_act"), sem("act_turned"), sem("act_in")
        dn, ye0, ye1, cmm, addd = sem("down"), sem("y_in_a"), sem("y_in_b"), sem("combined"), sem("added")
        wg = k["moe_gate"][layer].rearrange("e (p c) f -> e p c f", p=P)
        wu = k["moe_up"][layer].rearrange("e (p c) f -> e p c f", p=P)
        wd = k["moe_down"][layer].rearrange("e (c p) d -> e p c d", p=P)
        gu_w = lambda s: gate_up_weights(mem, s)
        dn_w = lambda s: down_weights(mem, s)
        FULL = PAIRS - 4

        def in_loop(eng, body):
            with eng.Fori(0, FULL // 4) as i:
                for v in range(4):
                    body(i * 4 + (1 + v), (1 + v) % 4)

        with nc.Block(no_gpsimd_drain=True) as block:

            @block.sync
            def _(sp):
                def load(q, u):
                    sp.wait_ge(gu, q - 1)
                    load_gate_up(sp, k, mem, layer, q, u)
                    sp.wait_ge(dn, q - 1)
                    load_down(sp, k, mem, layer, q, u)

                with sp.Fori(0, FULL // 4) as i:
                    for v in range(4):
                        load(i * 4 + (2 + v), (2 + v) % 4)
                for q in range(PAIRS - 2, PAIRS):
                    load(q, q % 4)

            @block.gpsimd
            def _(pool):
                def gather(q, u):
                    pool.wait_ge(idx_ok, q + 1)
                    pool.sem_inc(going, 1)
                    pool.indirect_dma_start(
                        out=xg[:, u % 2, :], out_offset=None, in_=mem["rows_dram"],
                        in_offset=bass.IndirectOffsetOnAxis(ap=idx[:, u, :], axis=0)).then_inc(gathered[u % 2], 16)

                pool.wait_ge(mem["rows_stored"], 16 * 3 * (layer + 1))
                gather(0, 0)
                gather(1, 1)

                def next_gather(q, u):
                    pool.wait_ge(turned, q)
                    gather(q + 1, (u + 1) % 4)

                in_loop(pool, next_gather)
                for q in range(PAIRS - 3, PAIRS - 1):
                    next_gather(q, q % 4)

            @block.tensor
            def _(pe):
                def broadcast(q, u, first=False):
                    pe.wait_ge(selw_ok, q + 1)
                    if not first:
                        pe.wait_ge(ev0, q - (AHEAD - 2))
                        pe.wait_ge(ev1, q - (AHEAD - 2))
                    pe.matmul(t0b[:, 0:T], selw[:, u % 2, :], pg[:, 0, :], start=True, stop=True)
                    pe.matmul(t1b[:, 0:T], selw[:, u % 2, :], pg[:, 1, :], start=True, stop=True).then_inc(sel_mm, 1)

                def turn(q, u, known):
                    pe.wait_ge(gathered[u % 2], ((q - u % 2) // 2) * 16 + 16 if isinstance(q, int) else known[1])
                    pe.wait_ge(idf_ok, known[0])
                    pe.wait_ge(gate_in, known[0])
                    for c in range(DC):
                        mm = pe.transpose((t0b, t1b)[c // 4][:, (c % 4) * P:(c % 4 + 1) * P],
                                          xg[:, u % 2, c * P:(c + 1) * P], ident[:])
                        if c == DC - 1:
                            mm.then_inc(turned, 1)

                def gate_up(q, u, ready):
                    pe.wait_ge(gu_ready[u % 2], ready)
                    pe.wait_ge(ev0, q + 1)
                    pe.wait_ge(ev1, q + 1)
                    if not (isinstance(q, int) and q == 0):
                        pe.wait_ge(mul, q)
                    for c in range(DC):
                        for e in range(2):
                            mm = pe.matmul(gub[e * SLOTS:(e + 1) * SLOTS, :], xgT[:, u % 2, c, e * SLOTS:(e + 1) * SLOTS],
                                           gu_w(2 * (u % 2) + e)[:, c, :], start=(c == 0), stop=(c == DC - 1))
                    mm.then_inc(gu, 1)

                def combine(q, u):
                    pe.wait_ge(ye0, q + 1)
                    pe.wait_ge(ye1, q + 1)
                    for m in range(DC):
                        if m >= 2:
                            pe.wait_ge(addd, q * DC + m)
                        elif m == 0:
                            pe.wait_ge(addd, q * DC + 1)
                        pe.matmul(cb[m % 2][:, 0:T], ys[:, m * P:(m + 1) * P], sg[:, u, :],
                                  start=True, stop=True).then_inc(cmm, 1)

                def turn_act(q, u):
                    pe.wait_ge(mul, q + 1)
                    if not (isinstance(q, int) and q == 0):
                        pe.wait_ge(ate, q)
                    for f in range(FC):
                        mm = pe.transpose(atb[:, f * P:(f + 1) * P], ac[:, f * P:(f + 1) * P], ident[:])
                    mm.then_inc(at, 1)

                def down(q, u, ready):
                    pe.wait_ge(dn_ready[u % 2], ready)
                    pe.wait_ge(ate, q + 1)
                    if not (isinstance(q, int) and q == 0):
                        pe.wait_ge(ye0, q)
                        pe.wait_ge(ye1, q)
                    for h, yb in enumerate((y0b, y1b)):
                        for f in range(FC):
                            for e in range(2):
                                mm = pe.matmul(yb[e * SLOTS:(e + 1) * SLOTS, :], aT[:, f, e * SLOTS:(e + 1) * SLOTS],
                                               dn_w(2 * (u % 2) + e)[:, f, h * BLOCK:(h + 1) * BLOCK],
                                               start=(f == 0), stop=(f == FC - 1))
                    mm.then_inc(dn, 1)

                def pair(q, u, half, tail=0):
                    nxt = half + 1 if u % 2 else half
                    gate_up(q, u, half * 64 + 64)
                    if tail < 3:
                        turn(q + 1, (u + 1) % 4, (q + AHEAD if tail == 0 else PAIRS, nxt * 16 + 16))
                    if not (isinstance(q, int) and q == 0):
                        combine(q - 1, (u + 3) % 4)
                    if tail == 0:
                        broadcast(q + AHEAD, (u + AHEAD) % 4)
                    turn_act(q, u)
                    down(q, u, half * 32 + 32)

                for q in range(AHEAD):
                    if q:
                        pe.wait_ge(idf_ok, q)
                        pe.wait_ge(gate_in, q)
                    broadcast(q, q, first=True)
                turn(0, 0, (AHEAD, 16))
                pair(0, 0, 0)
                with pe.Fori(0, FULL // 4) as i:
                    for v in range(4):
                        pair(i * 4 + (1 + v), (1 + v) % 4, i * 2 + (1 + v) // 2)
                for q in range(PAIRS - 3, PAIRS):
                    pair(q, q % 4, q // 2, tail=q - (PAIRS - 4))
                combine(PAIRS - 1, 3)

            @block.scalar
            def _(act):
                def gates(q, u):
                    act.wait_ge(sel_mm, q + 1)
                    if not (isinstance(q, int) and q == 0):
                        act.wait_ge(sg_ok, q)
                    act.copy(gsb[:], t1b[:, 0:T]).then_inc(gate_in, 1)

                def turned_in(q, u, early=False):
                    act.wait_ge(turned, q + 1)
                    if not early:
                        act.wait_ge(gu, q - 1)
                    act.copy(xgT[:, u % 2, 0:4, :], t0b[:].rearrange("p (c n) -> p c n", c=4)).then_inc(ev0, 1)

                def pair(q, u, tail=0, early=False):
                    act.wait_ge(gu, q + 1)
                    if not (isinstance(q, int) and q == 0):
                        act.wait_ge(mul, q)
                    act.activation(sl[:], gub[:, 0:FF], ACT.Silu).then_inc(sil, 1)
                    if tail < 3:
                        turned_in(q + 1, (u + 1) % 4, early)
                    if tail == 0:
                        gates(q + AHEAD, (u + AHEAD) % 4)
                    act.wait_ge(at, q + 1)
                    if not (isinstance(q, int) and q == 0):
                        act.wait_ge(dn, q)
                    act.copy(aT[:], atb[:, 0:FF].rearrange("p (f n) -> p f n", f=FC)).then_inc(ate, 1)
                    act.wait_ge(dn, q + 1)
                    act.copy(ys[:, 0:BLOCK], y0b[:]).then_inc(ye0, 1)

                for q in range(AHEAD):
                    gates(q, q)
                turned_in(0, 0, True)
                pair(0, 0, early=True)
                in_loop(act, pair)
                for q in range(PAIRS - 3, PAIRS):
                    pair(q, q % 4, tail=q - (PAIRS - 4))

            @block.vector
            def _(dve):
                def select(q, u, start=False):
                    if q_ge2(q):
                        dve.wait_ge(sel_mm, q - 1)
                    dve.tensor_scalar(selw[:, u % 2, :], basew[:], 0.0, None, ALU.is_equal).then_inc(selw_ok, 1)
                    dve.wait_ge(selw_ok, q + 1)
                    dve.tensor_scalar_add(basew[:], basew[:], -2.0).then_inc(based, 1)
                    dve.wait_ge(based, q + 2)

                def q_ge2(q):
                    return not isinstance(q, int) or q >= 2

                def places(q, u):
                    dve.wait_ge(gate_in, q + 1)
                    if not (isinstance(q, int) and q < 4):
                        dve.wait_ge(cmm, q * DC - 3 * DC)
                    dve.scalar_tensor_tensor(out=sg[:, u, :], in0=t0b[:, 0:T], scalar=slot_id[:, 0:1], in1=gsb[:],
                                             op0=ALU.is_equal, op1=ALU.mult).then_inc(sg_ok, 1)
                    if not (isinstance(q, int) and q == 0):
                        dve.wait_ge(idx_ok, q)
                    dve.scalar_tensor_tensor(out=hit[:], in0=t0b[:, 0:T], scalar=slot_id[:, 0:1], in1=tok[:],
                                             op0=ALU.is_equal, op1=ALU.mult, accum_out=idf[:]).then_inc(idf_ok, 1)
                    dve.wait_ge(idf_ok, q + 1)
                    if not (isinstance(q, int) and q < 4):
                        dve.wait_ge(gathered[u % 2], gather_count(q, u))
                    dve.tensor_copy(idx[:, u, :], idf[:]).then_inc(idx_ok, 1)

                def gather_count(q, u):
                    return (q - u % 2 - 2) * 8

                def turned_in(q, u, early=False):
                    dve.wait_ge(turned, q + 1)
                    if not early:
                        dve.wait_ge(gu, q - 1)
                    dve.tensor_copy(xgT[:, u % 2, 4:8, :], t1b[:].rearrange("p (c n) -> p c n", c=4)).then_inc(ev1, 1)

                def add_up(q):
                    for m in range(DC):
                        dve.wait_ge(cmm, q * DC + (m + 1))
                        if m == 0:
                            dve.wait_ge(addd, q * DC + 1)
                        dve.tensor_tensor(acc[:, m, :], acc[:, m, :], cb[m % 2][:, 0:T], ALU.add).then_inc(addd, 1)

                def pair(q, u, tail=0, early=False):
                    dve.wait_ge(sil, q + 1)
                    if not (isinstance(q, int) and q == 0):
                        dve.wait_ge(at, q)
                    dve.tensor_tensor(ac[:], sl[:], gub[:, FF:], ALU.mult).then_inc(mul, 1)
                    if tail < 3:
                        turned_in(q + 1, (u + 1) % 4, early)
                    if not (isinstance(q, int) and q == 0):
                        add_up(q - 1)
                    if tail == 0:
                        select(q + AHEAD, (u + AHEAD) % 4)
                        places(q + AHEAD, (u + AHEAD) % 4)
                    dve.wait_ge(dn, q + 1)
                    dve.tensor_copy(ys[:, BLOCK:], y1b[:]).then_inc(ye1, 1)

                dve.tensor_copy(basew[:], base[:]).then_inc(based, 1)
                dve.memset(hit[:, 0:1], 0.0).then_inc(addd, 1)
                dve.wait_ge(based, 1)
                for q in range(AHEAD):
                    select(q, q)
                    places(q, q)
                turned_in(0, 0, True)
                pair(0, 0, early=True)
                in_loop(dve, pair)
                for q in range(PAIRS - 3, PAIRS):
                    pair(q, q % 4, tail=q - (PAIRS - 4))
                add_up(PAIRS - 1)

        more_rounds(nc, k, mem, layer, dict(
            bank=bank, xg=xg, xgT=xgT, selw=selw, basew=basew, gsb=gsb, hit=hit, sg=sg, idf=idf, idx=idx, sl=sl, ac=ac,
            aT=aT, ys=ys, gu_w=gu_w, dn_w=dn_w, wg=wg, wu=wu, wd=wd))


def more_rounds(nc, k, mem, layer, buf):
    acc, ident, pg, base, slot_id, tok = (mem[n] for n in ("acc", "ident", "pg", "pair_base", "slot_id", "tok"))
    bank, xg, xgT, selw, basew, gsb, hit, sg, idf, idx, sl, ac, aT, ys, gu_w, dn_w = (buf[n] for n in (
        "bank", "xg", "xgT", "selw", "basew", "gsb", "hit", "sg", "idf", "idx", "sl", "ac", "aT", "ys", "gu_w", "dn_w"))
    t0b, t1b, gub, atb, y0b, y1b, c0b, c1b = bank
    wg, wu, wd = buf["wg"], buf["wu"], buf["wd"]
    with Signals(nc, f"m{layer}_") as sem:
        gu_ready, dn_ready, passed = sem("gate_up_ready"), sem("down_ready"), sem("passed")
        round_set, picked, rows_bc, gate_in, placed, indexed, going, gathered = (sem(n) for n in (
            "round_set", "picked", "rows_broadcast", "gates_in", "placed", "indexed", "gather_going", "gathered"))
        turned, in_a, in_b, gu, silu, mul, at, ate = (sem(n) for n in (
            "turned", "turned_in_a", "turned_in_b", "gate_up", "silu", "gated", "act_turned", "act_in"))
        dn, y_a, y_b, combined, added = (sem(n) for n in ("down", "y_in_a", "y_in_b", "combined", "added"))

        def over_items(eng, item, new_round=None):
            longest = eng.value_load(mem["count"][0:1, 0:1], min_val=0, max_val=T)
            with eng.If(longest > SLOTS):
                with eng.Fori(1, (longest + (SLOTS - 1)) // SLOTS) as r:
                    if new_round:
                        new_round(r)
                    with eng.Fori(0, PAIRS) as p:
                        n = r * PAIRS + p - (PAIRS - 1)
                        item(p, n)
                        eng.wait_ge(added, n * DC)
                        eng.sem_inc(passed, 1)

        with nc.Block(no_gpsimd_drain=True) as block:

            @block.sync
            def _(sp):
                def item(p, n):
                    for e in range(2):
                        w = gu_w(e)
                        sp.dma_start(w[:, :, 0:FF], wg[p * 2 + e]).then_inc(gu_ready, 16)
                        sp.dma_start(w[:, :, FF:], wu[p * 2 + e]).then_inc(gu_ready, 16)
                        sp.dma_start(dn_w(e), wd[p * 2 + e]).then_inc(dn_ready, 16)

                over_items(sp, item)

            @block.gpsimd
            def _(pool):
                def item(p, n):
                    pool.wait_ge(indexed, n)
                    pool.sem_inc(going, 1)
                    pool.indirect_dma_start(
                        out=xg[:, 0, :], out_offset=None, in_=mem["rows_dram"],
                        in_offset=bass.IndirectOffsetOnAxis(ap=idx[:, 0, :], axis=0)).then_inc(gathered, 16)

                over_items(pool, item)

            @block.tensor
            def _(pe):
                def item(p, n):
                    pe.wait_ge(picked, n)
                    pe.matmul(t0b[:, 0:T], selw[:, 0, :], pg[:, 0, :], start=True, stop=True)
                    pe.matmul(t1b[:, 0:T], selw[:, 0, :], pg[:, 1, :], start=True, stop=True).then_inc(rows_bc, 1)
                    pe.wait_ge(indexed, n)
                    pe.wait_ge(gathered, n * 16)
                    for c in range(DC):
                        mm = pe.transpose((t0b, t1b)[c // 4][:, (c % 4) * P:(c % 4 + 1) * P],
                                          xg[:, 0, c * P:(c + 1) * P], ident[:])
                    mm.then_inc(turned, 1)
                    pe.wait_ge(in_a, n)
                    pe.wait_ge(in_b, n)
                    pe.wait_ge(gu_ready, n * 64)
                    for c in range(DC):
                        for e in range(2):
                            half = slice(e * SLOTS, (e + 1) * SLOTS)
                            mm = pe.matmul(gub[half, :], xgT[:, 0, c, half], gu_w(e)[:, c, :],
                                           start=(c == 0), stop=(c == DC - 1))
                    mm.then_inc(gu, 1)
                    pe.wait_ge(mul, n)
                    for f in range(FC):
                        mm = pe.transpose(atb[:, f * P:(f + 1) * P], ac[:, f * P:(f + 1) * P], ident[:])
                    mm.then_inc(at, 1)
                    pe.wait_ge(ate, n)
                    pe.wait_ge(dn_ready, n * 32)
                    for h, yb in enumerate((y0b, y1b)):
                        for f in range(FC):
                            for e in range(2):
                                half = slice(e * SLOTS, (e + 1) * SLOTS)
                                mm = pe.matmul(yb[half, :], aT[:, f, half], dn_w(e)[:, f, h * BLOCK:(h + 1) * BLOCK],
                                               start=(f == 0), stop=(f == FC - 1))
                    mm.then_inc(dn, 1)
                    pe.wait_ge(y_a, n)
                    pe.wait_ge(y_b, n)
                    for m in range(DC):
                        if m >= 2:
                            pe.wait_ge(added, n * DC - DC + m - 1)
                        pe.matmul((c0b, c1b)[m % 2][:, 0:T], ys[:, m * P:(m + 1) * P], sg[:, 0, :],
                                  start=True, stop=True).then_inc(combined, 1)

                over_items(pe, item)

            @block.scalar
            def _(act):
                def item(p, n):
                    act.wait_ge(rows_bc, n)
                    act.copy(gsb[:], t1b[:, 0:T]).then_inc(gate_in, 1)
                    act.wait_ge(turned, n)
                    act.copy(xgT[:, 0, 0:4, :], t0b[:].rearrange("p (c n) -> p c n", c=4)).then_inc(in_a, 1)
                    act.wait_ge(gu, n)
                    act.activation(sl[:], gub[:, 0:FF], ACT.Silu).then_inc(silu, 1)
                    act.wait_ge(at, n)
                    act.copy(aT[:], atb[:, 0:FF].rearrange("p (f n) -> p f n", f=FC)).then_inc(ate, 1)
                    act.wait_ge(dn, n)
                    act.copy(ys[:, 0:BLOCK], y0b[:]).then_inc(y_a, 1)

                over_items(act, item)

            @block.vector
            def _(dve):
                def new_round(r):
                    dve.tensor_scalar_add(pg[:, 0, :], pg[:, 0, :], -float(SLOTS)).then_inc(round_set, 1)
                    dve.tensor_copy(basew[:], base[:]).then_inc(round_set, 1)
                    dve.wait_ge(round_set, r * 2)
                    dve.sem_inc(passed, 1)

                def item(p, n):
                    dve.tensor_scalar(selw[:, 0, :], basew[:], 0.0, None, ALU.is_equal).then_inc(picked, 1)
                    dve.wait_ge(gate_in, n)
                    dve.tensor_scalar_add(basew[:], basew[:], -2.0).then_inc(placed, 1)
                    dve.scalar_tensor_tensor(out=sg[:, 0, :], in0=t0b[:, 0:T], scalar=slot_id[:, 0:1], in1=gsb[:],
                                             op0=ALU.is_equal, op1=ALU.mult).then_inc(placed, 1)
                    dve.scalar_tensor_tensor(out=hit[:], in0=t0b[:, 0:T], scalar=slot_id[:, 0:1], in1=tok[:],
                                             op0=ALU.is_equal, op1=ALU.mult, accum_out=idf[:]).then_inc(placed, 1)
                    dve.wait_ge(placed, n * 3)
                    dve.tensor_copy(idx[:, 0, :], idf[:]).then_inc(indexed, 1)
                    dve.wait_ge(turned, n)
                    dve.tensor_copy(xgT[:, 0, 4:8, :], t1b[:].rearrange("p (c n) -> p c n", c=4)).then_inc(in_b, 1)
                    dve.wait_ge(silu, n)
                    dve.tensor_tensor(ac[:], sl[:], gub[:, FF:], ALU.mult).then_inc(mul, 1)
                    dve.wait_ge(dn, n)
                    dve.tensor_copy(ys[:, BLOCK:], y1b[:]).then_inc(y_b, 1)
                    for m in range(DC):
                        dve.wait_ge(combined, n * DC - DC + m + 1)
                        dve.tensor_tensor(acc[:, m, :], acc[:, m, :], (c0b, c1b)[m % 2][:, 0:T],
                                          ALU.add).then_inc(added, 1)

                over_items(dve, item, new_round)


def write_out(nc, k, mem, out):
    hT, ident = mem["hT"], mem["ident"]
    with ExitStack() as inner:
        sem = lambda name: inner.enter_context(nc.semaphore(name))
        bank = [inner.enter_context(nc.psum_tensor(f"wo{b}", [P, BLOCK], F32)) for b in range(4)]
        rows = inner.enter_context(nc.sbuf_tensor("out_rows", [P, 4, BLOCK], F32))
        turned, copied, stored = sem("out_turned"), sem("out_copied"), sem("out_stored")
        with nc.Block() as block:

            @block.tensor
            def _(pe):
                for i in range(4):
                    t0 = META + (i // 2) * P
                    for c in range(4):
                        mm = pe.transpose(bank[i][:, c * P:(c + 1) * P], hT[:, 4 * (i % 2) + c, t0:t0 + P], ident[:])
                    mm.then_inc(turned, 1)

            @block.vector
            def _(dve):
                for i in range(4):
                    dve.wait_ge(turned, i + 1)
                    dve.tensor_copy(rows[:, i, :], bank[i][:]).then_inc(copied, 1)

            @block.sync
            def _(sp):
                for i in range(4):
                    sp.wait_ge(copied, i + 1)
                    sp.dma_start(out[0, (i // 2) * P:(i // 2 + 1) * P, (i % 2) * BLOCK:(i % 2 + 1) * BLOCK],
                                 rows[:, i, :]).then_inc(stored, 16)
                sp.wait_ge(stored, 64)


def s5_discretise(dve, link, act_sem, phase_sem, mem):
    par, lam, ki = mem["s5_par"], mem["s5_lam"], mem["s5_int"]
    C1, C2 = 6.28125, 1.9350051879882812e-03
    C3 = 2.0 * math.pi - C1 - C2
    lr, li = lam[:, 0, :], lam[:, 1, :]
    dt, th, ku, r, cs, s_, h2, abr, abi, den, nr, q1, q2 = (par[:, i, :] for i in range(13))
    mag, cfr, cfi = (mem["s5_coef"][:, i, :] for i in range(3))
    link(dve.tensor_scalar(lr, lr, -1e-4, None, ALU.min))
    dve.wait_ge(act_sem, 1)
    link(dve.tensor_tensor(th, li, dt, ALU.mult))
    dve.tensor_tensor(mag, lr, dt, ALU.mult).then_inc(phase_sem, 1)
    link(dve.tensor_scalar(ku, th, 1.0 / (2.0 * math.pi), None, ALU.mult))
    link(dve.tensor_copy(ki[:], ku))
    link(dve.tensor_copy(ku, ki[:]))
    link(dve.scalar_tensor_tensor(out=r, in0=ku, scalar=-C1, in1=th, op0=ALU.mult, op1=ALU.add))
    link(dve.scalar_tensor_tensor(out=r, in0=ku, scalar=-C2, in1=r, op0=ALU.mult, op1=ALU.add))
    link(dve.scalar_tensor_tensor(out=r, in0=ku, scalar=-C3, in1=r, op0=ALU.mult, op1=ALU.add))
    dve.tensor_scalar(r, r, 3.1415925, -3.1415925, ALU.min, ALU.max).then_inc(phase_sem, 1)
    dve.wait_ge(act_sem, 4)
    link(dve.tensor_tensor(cs, h2, h2, ALU.mult))
    dve.tensor_scalar(cs, cs, -2.0, 1.0, ALU.mult, ALU.add).then_inc(phase_sem, 1)
    dve.wait_ge(phase_sem, 3)
    link(dve.tensor_tensor(abr, mag, cs, ALU.mult))
    link(dve.tensor_tensor(abi, mag, s_, ALU.mult))
    link(dve.tensor_tensor(den, lr, lr, ALU.mult))
    link(dve.tensor_tensor(q1, li, li, ALU.mult))
    link(dve.tensor_tensor(den, den, q1, ALU.add))
    link(dve.reciprocal(den, den))
    link(dve.tensor_scalar_add(nr, abr, -1.0))
    link(dve.tensor_tensor(q1, nr, lr, ALU.mult))
    link(dve.tensor_tensor(q2, abi, li, ALU.mult))
    link(dve.tensor_tensor(q1, q1, q2, ALU.add))
    link(dve.tensor_tensor(cfr, q1, den, ALU.mult))
    link(dve.tensor_tensor(q1, abi, lr, ALU.mult))
    link(dve.tensor_tensor(q2, nr, li, ALU.mult))
    link(dve.tensor_tensor(q1, q1, q2, ALU.subtract))
    link(dve.tensor_tensor(cfi, q1, den, ALU.mult))


def s5_sines(act, act_sem, phase_sem, mem):
    par = mem["s5_par"]
    act.activation(par[:, 0, :], mem["s5_lam"][:, 2, :], ACT.Exp).then_inc(act_sem, 1)
    act.wait_ge(phase_sem, 1)
    mag = mem["s5_coef"][:, 0, :]
    act.activation(mag, mag, ACT.Exp).then_inc(act_sem, 1)
    act.wait_ge(phase_sem, 2)
    act.activation(par[:, 5, :], par[:, 3, :], ACT.Sin).then_inc(act_sem, 1)
    act.activation(par[:, 6, :], par[:, 3, :], ACT.Sin, scale=0.5).then_inc(act_sem, 1)


def s5_tables(pool, link, mem, slice_done):
    J, par, table, a_full = S5_TILES, mem["s5_par"], mem["s5_table"], mem["s5_scratch"]
    q1, q2 = par[:, 13, :], par[:, 14, :]
    cosT, sinT = table[:, :, 0, :], table[:, :, 1, :]
    link(pool.memset(cosT[:, :, 0:1], 1.0))
    link(pool.memset(sinT[:, :, 0:1], 0.0))
    link(pool.tensor_copy(cosT[:, :, 1], par[:, 4, :]))
    link(pool.tensor_copy(sinT[:, :, 1], par[:, 5, :]))
    levels = []
    m = 1
    while 2 * m < T:
        cm, sm = cosT[:, :, m], sinT[:, :, m]
        link(pool.tensor_tensor(q1, cm, cm, ALU.mult))
        link(pool.tensor_tensor(q2, sm, sm, ALU.mult))
        link(pool.tensor_tensor(cosT[:, :, 2 * m], q1, q2, ALU.subtract))
        link(pool.tensor_tensor(q1, cm, sm, ALU.mult))
        link(pool.tensor_tensor(sinT[:, :, 2 * m], q1, q1, ALU.add))
        m *= 2
        levels.append((m, min(m, T - m) - 1))
        if m < 64:
            double(pool, link, table, a_full, slice(0, J), *levels.pop())
    for j0 in range(0, J, S5_SLICE):
        for m, n in levels:
            ins = double(pool, link, table, a_full, slice(j0, j0 + S5_SLICE), m, n, last=(m, n) == levels[-1])
        ins.then_inc(slice_done, 1)
        pool.wait_ge(slice_done, j0 // S5_SLICE + 1)


def double(pool, link, table, scratch, js, m, n, last=False):
    k = js.stop - js.start
    ca, sa = (table[:, js, q, m].unsqueeze(2).broadcast_to([P, k, n]) for q in range(2))
    ci, si = (table[:, js, q, 1:1 + n] for q in range(2))
    co, so = (table[:, js, q, m + 1:m + 1 + n] for q in range(2))
    a = scratch[:, 0:k * n].rearrange("p (j n) -> p j n", j=k)
    link(pool.tensor_tensor(a, si, sa, ALU.mult))
    link(pool.tensor_tensor(co, ci, ca, ALU.mult))
    link(pool.tensor_tensor(co, co, a, ALU.subtract))
    link(pool.tensor_tensor(a, ci, sa, ALU.mult))
    link(pool.tensor_tensor(so, si, ca, ALU.mult))
    ins = pool.tensor_tensor(so, so, a, ALU.add)
    if not last:
        link(ins)
    return ins


def s5_mixer(nc, k, mem):
    hT, ring = mem["hT"], mem["dense"]
    J = S5_TILES
    with ExitStack() as outer:
        yT = outer.enter_context(nc.sbuf_tensor("s5_y", [P, DC, T], F32))
        glu = outer.enter_context(Signals(nc, "glu_"))
        w_ready = [glu("w_even"), glu("w_odd")]
        w_out = k["s5_w_out"].rearrange("(c p) n -> p c n", p=P)
        with ExitStack() as inner:
            sem = inner.enter_context(Signals(nc, "s5_"))
            sb = lambda name, shape, dt=F32: inner.enter_context(nc.sbuf_tensor(f"s5_{name}", shape, dt))
            bank = [inner.enter_context(nc.psum_tensor(f"s5_b{b}", [P, BLOCK], F32)) for b in range(8)]
            table = sb("turns", [P, J, 2, T])
            c_re, c_im = sb("c_re", [P, J, 32]), sb("c_im", [P, J, 32])
            w_re, w_nre, w_nim = sb("w_re", [P, J, 32]), sb("w_nre", [P, J, 32]), sb("w_nim", [P, J, 32])
            b_re, b_im = sb("b_re", [P, DC, P]), sb("b_im", [P, DC, P])
            mag, cfr, cfi = (mem["s5_coef"][:, i, :] for i in range(3))
            R = 3
            in_bank = bank[0:4] + bank[6:8]
            b_sb = sb("b_sb", [P, R, 3, T])
            z = sb("z", [P, R, 2, T])
            by_cos, by_sin = sb("in_by_cos", [P, R, 2, T]), sb("in_by_sin", [P, R, 2, T])
            z_cos, z_sin = sb("z_by_cos", [P, R, 2, T]), sb("z_by_sin", [P, R, 2, T])
            b_loaded, c_loaded, st = sem("b_loaded"), sem("c_loaded"), sem("step")
            tables = [sem(f"table{i}_loaded") for i in range(J // S5_SLICE)]
            weighted = sem("c_weighted")
            bu, cp, cos_in, sin_in, turned = sem("bu"), sem("bu_in"), sem("in_by_cos"), sem("in_by_sin"), sem("turned")
            scanned, cos_out, sin_out, yy, fin, gel = (sem("scanned"), sem("z_by_cos"), sem("z_by_sin"), sem("y"),
                                                       sem("y_skip"), sem("gelu"))
            both = lambda x: x.unsqueeze(1).broadcast_to([P, 2, T])
            with nc.Block(no_gpsimd_drain=True) as block:

                @block.sync
                def _(sp):
                    sp.dma_start(b_re[:], k["s5_b_re"]).then_inc(b_loaded, 16)
                    sp.dma_start(b_im[:], k["s5_b_im"]).then_inc(b_loaded, 16)
                    sp.wait_ge(mem["tables_stored"], 16 * (J // S5_SLICE))
                    for i, loaded in enumerate(tables):
                        js = slice(i * S5_SLICE, (i + 1) * S5_SLICE)
                        sp.dma_start(table[:, js], k["s5_table_dram"][:, js]).then_inc(loaded, 16)
                        if i == 0:
                            sp.dma_start(c_re[:], k["s5_c_re"]).then_inc(c_loaded, 16)
                            sp.dma_start(c_im[:], k["s5_c_im"]).then_inc(c_loaded, 16)
                            sp.dma_start(mem["s5_d"][:], k["s5_d"]).then_inc(c_loaded, 16)
                    for b in range(2):
                        sp.dma_start(ring[:, b], w_out[:, :, b * BLOCK:(b + 1) * BLOCK]).then_inc(w_ready[b], 16)

                @block.tensor
                def _(pe):
                    pe.wait_ge(b_loaded, 32)

                    def inputs(j):
                        a, b = j // 4, j % 4
                        rows = slice(32 * b, 32 * b + 32)
                        if j >= R:
                            pe.wait_ge(cp, 3 * (j - (R - 1)))
                        for q, w in enumerate((b_re, b_im)):
                            pe.matmul(in_bank[2 * (j % R) + q][:, 0:T], w[rows, a, :], hT[rows, a, :],
                                      start=True, stop=True).then_inc(bu, 1)

                    def outputs(j):
                        a, b = j // 4, j % 4
                        if b == 0 and a >= 2:
                            pe.wait_ge(fin, a - 1)
                        pe.wait_ge(cos_out, j + 1)
                        pe.wait_ge(sin_out, j + 1)
                        for q, (w, zz) in enumerate(((w_re, z_cos[:, j % R, 0]), (w_nim, z_cos[:, j % R, 1]),
                                                     (w_nim, z_sin[:, j % R, 0]), (w_nre, z_sin[:, j % R, 1]))):
                            mm = pe.matmul(bank[4 + a % 2][32 * b:32 * b + 32, 0:T], w[:, j, :], zz,
                                           start=(q == 0), stop=(q == 3))
                        mm.then_inc(yy, 1)

                    for j in range(J + R):
                        if j < J:
                            inputs(j)
                        if j == R:
                            pe.wait_ge(weighted, 3)
                        if j >= R:
                            outputs(j - R)

                @block.scalar
                def _(act):
                    for j in range(J):
                        for q, (bk, scale) in enumerate(((0, 1.0), (1, 1.0), (0, -1.0))):
                            act.wait_ge(bu, 2 * j + bk + 1)
                            if j >= R:
                                act.wait_ge(cos_in, j - (R - 1))
                                act.wait_ge(sin_in, j - (R - 1))
                            act.activation(b_sb[:, j % R, q, :], in_bank[2 * (j % R) + bk][:, 0:T], ACT.Copy,
                                           scale=scale).then_inc(cp, 1)
                    for a in range(DC):
                        act.wait_ge(fin, a + 1)
                        act.activation(yT[:, a, :], yT[:, a, :], ACT.Gelu_apprx_tanh).then_inc(gel, 1)

                @block.gpsimd
                def _(pool):
                    def forward(j):
                        if j % S5_SLICE == 0:
                            pool.wait_ge(tables[j // S5_SLICE], 16)
                        pool.wait_ge(cp, 3 * j + 3)
                        if j >= R:
                            pool.wait_ge(turned, j - (R - 1))
                        pool.tensor_tensor(by_sin[:, j % R], b_sb[:, j % R, 1:3, :], both(table[:, j, 1, :]),
                                           ALU.mult).then_inc(sin_in, 1)

                    def back(j):
                        pool.wait_ge(scanned, 2 * j + 2)
                        if j >= R:
                            pool.wait_ge(yy, j - (R - 1))
                        pool.tensor_tensor(z_sin[:, j % R], z[:, j % R], both(table[:, j, 1, :]),
                                           ALU.mult).then_inc(sin_out, 1)

                    for j in range(J + 1):
                        if j < J:
                            forward(j)
                        if j >= 1:
                            back(j - 1)

                @block.vector
                def _(dve):
                    link = Chain(dve, st).done

                    def forward(j):
                        if j % S5_SLICE == 0:
                            dve.wait_ge(tables[j // S5_SLICE], 16)
                        dve.wait_ge(cp, 3 * j + 3)
                        dve.tensor_tensor(by_cos[:, j % R], b_sb[:, j % R, 0:2, :], both(table[:, j, 0, :]),
                                          ALU.mult).then_inc(cos_in, 1)

                    def scans(j):
                        dve.wait_ge(cos_in, j + 1)
                        dve.wait_ge(sin_in, j + 1)
                        dve.tensor_tensor(by_cos[:, j % R], by_cos[:, j % R], by_sin[:, j % R],
                                          ALU.add).then_inc(turned, 1)
                        dve.wait_ge(turned, j + 1)
                        if j >= R:
                            dve.wait_ge(cos_out, j - (R - 1))
                            dve.wait_ge(sin_out, j - (R - 1))
                        rho = mag[:, j:j + 1].broadcast_to([P, T])
                        for q in range(2):
                            dve.tensor_tensor_scan(z[:, j % R, q, :], rho, by_cos[:, j % R, q, :], 0.0, ALU.mult,
                                                   ALU.add).then_inc(scanned, 1)

                    def back(j):
                        dve.wait_ge(scanned, 2 * j + 2)
                        if j >= R:
                            dve.wait_ge(yy, j - (R - 1))
                        dve.tensor_tensor(z_cos[:, j % R], z[:, j % R], both(table[:, j, 0, :]),
                                          ALU.mult).then_inc(cos_out, 1)

                    def skip(a):
                        dve.wait_ge(yy, 4 * (a + 1))
                        dve.scalar_tensor_tensor(out=yT[:, a, :], in0=hT[:, a, :], scalar=mem["s5_d"][:, a:a + 1],
                                                 in1=bank[4 + a % 2][:, 0:T], op0=ALU.mult, op1=ALU.add).then_inc(fin, 1)

                    forward(0)
                    dve.wait_ge(c_loaded, 48)
                    wide = lambda x: x.unsqueeze(2).broadcast_to([P, J, 32])
                    flat = lambda x: x[:].rearrange("p a b -> p (a b)")
                    link(dve.tensor_tensor(w_re[:], c_re[:], wide(cfr), ALU.mult))
                    link(dve.tensor_tensor(w_nre[:], c_im[:], wide(cfi), ALU.mult))
                    dve.tensor_tensor(w_re[:], w_re[:], w_nre[:], ALU.subtract).then_inc(weighted, 1)
                    dve.wait_ge(weighted, 1)
                    dve.tensor_scalar(w_nre[:], w_re[:], -1.0, None, ALU.mult).then_inc(weighted, 1)
                    link(dve.tensor_tensor(w_nim[:], c_re[:], wide(cfi), ALU.mult))
                    link(dve.tensor_tensor(c_im[:], c_im[:], wide(cfr), ALU.mult))
                    dve.scalar_tensor_tensor(out=flat(w_nim), in0=flat(w_nim), scalar=-1.0, in1=flat(c_im),
                                             op0=ALU.mult, op1=ALU.subtract).then_inc(weighted, 1)
                    for j in range(J + 1):
                        if j >= 1:
                            back(j - 1)
                        if j < J:
                            scans(j)
                            if j + 1 < J:
                                forward(j + 1)
                        if j >= 5 and j % 4 == 1:
                            skip(j // 4 - 1)
                    skip(DC - 1)

        with ExitStack() as inner:
            sem = glu
            ps = [inner.enter_context(nc.psum_tensor(f"glu{b}", [P, BLOCK], F32)) for b in range(4)]
            val = inner.enter_context(nc.sbuf_tensor("glu_val", [P, DC, T], F32))
            sig = inner.enter_context(nc.sbuf_tensor("glu_sig", [P, 2, T], F32))
            ready, w = w_ready, w_out
            proj, taken, mul, added = sem("proj"), sem("taken"), sem("mul"), sem("added")
            with nc.Block(no_gpsimd_drain=True) as block:

                @block.sync
                def _(sp):
                    for b in range(2, 4):
                        sp.wait_ge(proj, 4 * (b - 1))
                        sp.dma_start(ring[:, b % 2], w[:, :, b * BLOCK:(b + 1) * BLOCK]).then_inc(ready[b % 2], 16)

                @block.tensor
                def _(pe):
                    for m in range(2 * DC):
                        b = m // 4
                        if m % 4 == 0:
                            pe.wait_ge(ready[b % 2], 16 * (b // 2 + 1))
                        if m >= 4:
                            pe.wait_ge(taken, m - 3)
                        for c in range(DC):
                            mm = pe.matmul(ps[m % 4][:, 0:T], ring[:, b % 2, c, (m % 4) * P:(m % 4 + 1) * P],
                                           yT[:, c, :], start=(c == 0), stop=(c == DC - 1))
                        mm.then_inc(proj, 1)

                @block.scalar
                def _(act):
                    for m in range(2 * DC):
                        act.wait_ge(proj, m + 1)
                        if m < DC:
                            act.copy(val[:, m, :], ps[m % 4][:, 0:T]).then_inc(taken, 1)
                        else:
                            if m >= DC + 2:
                                act.wait_ge(mul, m - DC - 1)
                            act.activation(sig[:, m % 2, :], ps[m % 4][:, 0:T], ACT.Sigmoid).then_inc(taken, 1)

                @block.vector
                def _(dve):
                    for m in range(DC):
                        dve.wait_ge(taken, DC + m + 1)
                        dve.tensor_tensor(val[:, m, :], val[:, m, :], sig[:, m % 2, :], ALU.mult).then_inc(mul, 1)
                        dve.wait_ge(mul, m + 1)
                        dve.scalar_tensor_tensor(out=hT[:, m, :], in0=hT[:, m, :], scalar=ALPHA, in1=val[:, m, :],
                                                 op0=ALU.mult, op1=ALU.add).then_inc(added, 1)


def trunk(nc, k, out, phases=4):
    with ExitStack() as ctx:
        sb = lambda name, shape, dt=F32: ctx.enter_context(nc.sbuf_tensor(name, shape, dt))
        sem = lambda name: ctx.enter_context(nc.semaphore(name))
        mem = {
            "hT": sb("hT", [P, DC, T]), "dense": sb("dense_ring", [P, 2, DC, BLOCK]),
            "ident": sb("ident", [P, P]), "ones": sb("ones", [P, P]), "eps": sb("eps", [P, 3]),
            "ln_par": sb("ln_par", [P, 8 * DC]), "s5_d": sb("s5_d", [P, DC]),
            "pair_base": sb("pair_base", [E, P]), "slot_id": sb("slot_id", [P, 1]), "tok": sb("tok", [P, T]),
            "count": sb("count", [1, 1], I32), "s5_coef": sb("s5_coef", [P, 3, S5_TILES]),
            "consts_loaded": sem("consts_loaded"), "rows_stored": sem("rows_stored"), "count_ready": sem("count_ready"),
            "tables_stored": sem("tables_stored"), "rows_dram": k["rows_dram"],
            "gate_up_ready": [[sem(f"gate_up{la}_{half}_ready") for half in "ab"] for la in range(DEPTH)],
            "down_ready": [[sem(f"down{la}_{half}_ready") for half in "ab"] for la in range(DEPTH)],
        }
        ones_set, consts2 = sem("ones_set"), sem("expert_consts_loaded")
        with nc.Block(no_gpsimd_drain=True) as block:

            @block.vector
            def _(dve):
                dve.memset(mem["ones"][:], 1.0).then_inc(ones_set, 1)

            @block.sync
            def _(sp):
                for name in ("pair_base", "slot_id", "tok"):
                    sp.dma_start(mem[name][:], k[name]).then_inc(consts2, 16)

        with ExitStack() as mix:
            msb = lambda name, shape, dt=F32: mix.enter_context(nc.sbuf_tensor(name, shape, dt))
            mem |= {
                "qkv": msb("qkv", [P, 24, T]), "xa": msb("xa", [P, DC, T]), "y": msb("y", [P, 2 * DC, T]),
                "bd": msb("bd", [HEADS, 2, T]), "conv_w": msb("conv_w", [P, 32, CONV]), "conv_b": msb("conv_b", [P, DC]),
                "w_bd": msb("w_bd", [P, DC, 2 * HEADS]), "offmask": msb("offmask", [P, LEVELS, P]),
                "causal": msb("causal", [P, P]), "sel8": msb("sel8", [HEADS, HEADS, P]), "lru_b": msb("lru_b", [P, 16]),
                "lru_lam": msb("lru_lam", [P, DC]), "head_par": msb("head_par", [HEADS, 2]),
                "norm_w": msb("norm_w", [P, 1]),
            }
            in_projection(nc, k, mix, mem)
            with nc.Block(no_gpsimd_drain=True) as block:
                for start in (block.tensor, block.scalar, block.vector, block.gpsimd):

                    @start
                    def _(eng):
                        eng.wait_ge(mem["consts_loaded"], 16 * 10)

            group_mixers(nc, k, mix, mem)
            out_projection(nc, k, mem)
        mem |= {"acc": sb("acc", [P, DC, T]), "pg": sb("places_gates", [E, 2, T])}
        ex = ctx.enter_context(ExitStack())
        mem["experts"] = ex.enter_context(nc.sbuf_tensor("experts0", [P, 4, 3 * D * FF // P], F32))
        layer_norm(nc, k, mem, 0, "hT", next_experts=0)
        with nc.Block(no_gpsimd_drain=True) as block:
            for start in (block.tensor, block.vector):

                @start
                def _(eng):
                    eng.wait_ge(consts2, 48)

        def moe(layer):
            router_and_shared(nc, k, mem, layer)
            experts(nc, k, mem, layer)
            ex.close()
            layer_norm(nc, k, mem, 2 * layer + 1, "acc")

        if phases >= 2:
            moe(0)
        if phases >= 3:
            s5_mixer(nc, k, mem)
            mem["experts"] = ex.enter_context(nc.sbuf_tensor("experts1", [P, 4, 3 * D * FF // P], F32))
            layer_norm(nc, k, mem, 2, "hT", next_experts=1)
        if phases >= 4:
            moe(1)
        write_out(nc, k, mem, out)


def constants():
    i = np.arange(P)
    f = np.float32
    offmask = np.zeros((P, LEVELS, P), f)
    for lv in range(LEVELS):
        b = 2 ** lv
        same = i[:, None] // (2 * b) == i[None, :] // (2 * b)
        offmask[:, lv, :] = same & (i[:, None] // b % 2 == 0) & (i[None, :] // b % 2 == 1)
    sel8 = np.zeros((HEADS, HEADS, P), f)
    for h in range(HEADS):
        sel8[h, h, :] = 1.0
    t = np.arange(T)
    tile_tok = i[:, None] + P * np.arange(3)[None, :]
    return {
        "ident": np.eye(P, dtype=f), "offmask": offmask,
        "causal": (i[None, :] >= i[:, None]).astype(f), "sel8": sel8,
        "eps": np.tile(np.array([[NORM_EPS, NORM_EPS * P, LN_EPS]], f), (P, 1)),
        "after": (t[None, None, :] > tile_tok[:, :, None]).astype(f),
        "lower": np.broadcast_to(np.tril(np.ones((GROUPS, GROUPS), f), -1), (P, GROUPS, GROUPS)).copy(),
        "pair_base": (np.arange(E)[:, None] - (i[None, :] >= SLOTS)).astype(f),
        "slot_id": (i % SLOTS).astype(f)[:, None],
        "tok": np.tile(t.astype(f)[None, :], (P, 1)),
    }


def layout(a):
    tile = lambda v: np.ascontiguousarray(np.asarray(v).reshape(-1, P).T)
    a = {n: np.asarray(v) for n, v in a.items()}
    r = {}
    h0 = np.concatenate([a["meta_tokens"], a["x"][0]], axis=0)
    r["h0T"] = h0.T.reshape(DC, P, T).transpose(1, 0, 2)
    r["w_in"] = a["ab_w_in"][0]
    g = a["gdn_conv_w"][0]
    conv = np.concatenate([g[:, D:2 * D], g[:, 0:D], g[:, 2 * D:], a["ab_conv_w"][0]], axis=1)
    r["conv_w"] = conv.reshape(CONV, 32, P).transpose(2, 1, 0)
    r["conv_b"] = tile(a["ab_conv_b"][0])
    w = np.stack([a["lru_w_r"][0], a["lru_w_i"][0]])
    r["lru_w"] = w.reshape(2, 4, 2, P, 2 * P).transpose(3, 0, 1, 2, 4).reshape(P, DC, BLOCK)
    r["lru_b"] = np.concatenate([tile(a["lru_b_r"][0]), tile(a["lru_b_i"][0])], axis=1)
    r["lru_lam"] = tile(a["lru_lambda"][0])
    r["head_par"] = np.stack([a["gdn_a_log"][0], a["gdn_dt_bias"][0]], axis=1)
    r["norm_w"] = a["gdn_norm_w"][0][:, None]
    r["w_out"] = a["ab_w_out"][0]
    ln = []
    for layer in range(DEPTH):
        for kind in ("mix", "ffn"):
            ln += [tile(a[f"ln_{kind}_g"][layer]), tile(a[f"ln_{kind}_b"][layer])]
    r["ln_par"] = np.concatenate(ln, axis=1)
    r["router_w"] = a["moe_w_router"].reshape(DEPTH, DC, P, E).transpose(0, 2, 1, 3)
    r["router_b"] = a["moe_router_bias"]
    r["moe_gate"], r["moe_up"], r["moe_down"] = a["moe_w_gate"], a["moe_w_up"], a["moe_w_down"]
    r["sh_gate"], r["sh_up"], r["sh_down"] = a["moe_shared_w_gate"], a["moe_shared_w_up"], a["moe_shared_w_down"]
    st = lambda v: v.reshape(S5_TILES, P).T
    dt = np.repeat(a["s5_log_dt"][0][:, None], STATES, axis=1)
    r["s5_lam"] = np.stack([st(a["s5_lambda_re"][0]), st(a["s5_lambda_im"][0]), st(dt)], axis=1)
    for name in ("re", "im"):
        b = a[f"s5_b_{name}"][0].reshape(DC, 4, 2, STATES, 16)
        wide = np.zeros((4, 2, 16, DC, 2, STATES), b.dtype)
        c = a[f"s5_c_{name}"][0].reshape(S5_TILES, 2, 16, STATES)
        cw = np.zeros((2, STATES, S5_TILES, 2, 16), c.dtype)
        for g2 in range(2):
            wide[:, g2, :, :, g2, :] = b[:, :, g2].transpose(1, 3, 0, 2)
            cw[g2, :, :, g2, :] = c[:, g2].transpose(2, 0, 1)
        r[f"s5_b_{name}"] = wide.reshape(P, DC, P)
        r[f"s5_c_{name}"] = cw.reshape(P, S5_TILES, 32)
    r["s5_d"] = tile(a["s5_d"][0])
    r["s5_w_out"] = a["s5_w_out"][0]
    return {n: np.ascontiguousarray(v) for n, v in r.items()}


def kernel(**inputs):
    import concourse.bacc as _bacc
    from concourse.bass_utils import run_bass_kernel_spmd as _run

    arrays = layout(inputs) | constants()
    nc = _bacc.Bacc("TRN2", target_bir_lowering=False, num_devices=1)
    k = {n: nc.dram_tensor(f"in_{n}", v.shape, mybir.dt.from_np(v.dtype), kind="ExternalInput").ap()
         for n, v in arrays.items()}
    k["rows_dram"] = nc.dram_tensor("rows_dram", (T, D), F32, kind="Internal").ap()
    k["s5_table_dram"] = nc.dram_tensor("s5_table_dram", (P, S5_TILES, 2, T), F32, kind="Internal").ap()
    out = nc.dram_tensor("out", (1, SEQ, D), F32, kind="ExternalOutput").ap()
    trunk(nc, k, out)
    r = _run(nc, [{f"in_{n}": v for n, v in arrays.items()}], core_ids=[0])
    return r.results[0]["out"]
```

```python
import math
from contextlib import ExitStack

import numpy as np

import concourse.bass as bass
from concourse import mybir

ALU = mybir.AluOpType
ACT = mybir.ActivationFunctionType
AX_X = mybir.AxisListType.X
F32 = mybir.dt.float32
I32 = mybir.dt.int32
U32 = mybir.dt.uint32

P = 128
D = 1024
META = 16
SEQ = 256
T = META + SEQ
DC = D // P
DEPTH = 2
ALPHA = (2.0 * DEPTH) ** 0.25
LN_EPS = 1e-5
NORM_EPS = 1e-6

HEADS = 8
CONV = 4
DECAY_ROW = 32
IN_COLS = 6 * D + 2 * HEADS
CHUNKS = ((0, META), (META, P), (META + P, P))
LEVELS = 7

STATES = 64
S5_TILES = 32
S5_SLICE = 4

E = 64
PAIRS = E // 2
FF = 256
FC = FF // P
SLOTS = 64
TOP = 8
GROUPS = 8
TOP_GROUPS = 4
SCALE = 2.5
TILES = ((0, P), (P, P), (2 * P, META))
BLOCK = 512
LOG1P_TERMS = 9


class Chain:

    def __init__(self, eng, sem):
        self.eng, self.sem, self.n = eng, sem, 0

    def done(self, ins):
        ins.then_inc(self.sem, 1)
        self.n += 1
        self.eng.wait_ge(self.sem, self.n)


class Signals:

    def __init__(self, nc, prefix=""):
        self.nc, self.prefix, self.held = nc, prefix, []

    def __enter__(self):
        return self

    def __call__(self, name):
        self.held.append(self.nc.alloc_semaphore(self.prefix + name))
        return self.held[-1]

    def __exit__(self, *failed):
        if not failed[0]:
            self.nc.clear_and_free_semaphores(self.held)
            self.nc.all_engine_barrier()


def log1p_steps(v, link, out, e, z, z2):
    link(v.tensor_scalar_add(z, e, 2.0))
    link(v.reciprocal(z, z))
    link(v.tensor_tensor(z, z, e, ALU.mult))
    link(v.tensor_tensor(z2, z, z, ALU.mult))
    link(v.memset(out, 1.0 / (2 * LOG1P_TERMS + 1)))
    for k in range(LOG1P_TERMS - 1, -1, -1):
        link(v.tensor_tensor(out, out, z2, ALU.mult))
        link(v.tensor_scalar_add(out, out, 1.0 / (2 * k + 1)))
    link(v.scalar_tensor_tensor(out=out, in0=out, scalar=2.0, in1=z, op0=ALU.mult, op1=ALU.mult))


def in_projection(nc, k, ctx, mem):
    cols = [3 * D, 3 * D + BLOCK, 2 * D, 2 * D + BLOCK, 4 * D, 4 * D + BLOCK, 5 * D, 5 * D + BLOCK,
            D, D + BLOCK, 0, BLOCK]
    per = BLOCK // P
    place = lambda n: n if n < per else n + 1
    N_CONV = 32
    conv_of = {n: n for n in range(24)} | {n: n - 8 for n in range(32, 40)}
    conv_w, conv_b, w_bd = mem["conv_w"], mem["conv_b"], mem["w_bd"]
    qkv, xa, y, bd = mem["qkv"], mem["xa"], mem["y"], mem["bd"]
    hT, ring, ones = mem["hT"], mem["dense"], mem["ones"]
    with ExitStack() as inner:
        sem = inner.enter_context(Signals(nc))
        cin = inner.enter_context(nc.sbuf_tensor("cin", [P, 4, T + CONV - 1], F32))
        ps = [inner.enter_context(nc.psum_tensor(f"proj{b}", [P, BLOCK], F32)) for b in range(4)]
        sums = [inner.enter_context(nc.psum_tensor(f"norm_sums{b}", [P, BLOCK], F32)) for b in range(2)]
        sq = inner.enter_context(nc.sbuf_tensor("qk_squares", [P, 2, T], F32))
        nrm = inner.enter_context(nc.sbuf_tensor("qk_norms", [P, 2, T], F32))
        small = inner.enter_context(nc.sbuf_tensor("decay_scratch", [HEADS, 4, T], F32))
        l8 = inner.enter_context(nc.sbuf_tensor("lam_scratch", [P, 4, DC], F32))
        ea = inner.enter_context(nc.sbuf_tensor("exp_a_log", [HEADS, 1], F32))
        s0, s1, s2, s3 = (small[:, i, :] for i in range(4))
        beta, G, c8, eps = mem["beta_G"][:, 0, :], mem["beta_G"][:, 1, :], mem["c8"], mem["eps"]
        squared, summed, rooted, normed = sem("qk_squared"), sem("qk_summed"), sem("qk_rooted"), sem("qk_normed")
        decay_in, decay_exp, act_step = sem("decay_in"), sem("decay_exp"), sem("inproj_act_step")
        loaded, h_loaded = sem("inproj_loaded"), sem("h_loaded")
        w_ready = [sem("w_in_even_ready"), sem("w_in_odd_ready")]
        first_ready = [sem(f"w_in_first{j}_ready") for j in range(per)]
        proj_done, evacuated, pads_zero = sem("proj_done"), sem("proj_evacuated"), sem("pads_zero")
        conv_done, conv_step, silu_done = sem("conv_done"), sem("conv_step"), sem("silu_done")
        lam_loaded, angles, sines = sem("s5_lam_loaded"), sem("s5_angles"), sem("s5_sines")
        s5_step, table_step, sliced = sem("s5_coef_step"), sem("s5_doubling_step"), sem("s5_slice_done")
        smem = dict(mem)
        for name, shape, dt in (("lam", [P, 3, S5_TILES], F32), ("par", [P, 15, S5_TILES], F32),
                                ("int", [P, S5_TILES], I32), ("table", [P, S5_TILES, 2, T], F32),
                                ("scratch", [P, S5_TILES * 32], F32)):
            smem[f"s5_{name}"] = inner.enter_context(nc.sbuf_tensor(f"s5_{name}", shape, dt))
        w_in = k["w_in"].rearrange("(c p) n -> p c n", p=P)
        with nc.Block(no_gpsimd_drain=True) as block:

            @block.sync
            def _(sp):
                sp.dma_start(hT[:], k["h0T"]).then_inc(h_loaded, 16)
                def store_tables(i):
                    js = slice(i * S5_SLICE, (i + 1) * S5_SLICE)
                    sp.wait_ge(sliced, i + 1)
                    sp.dma_start(k["s5_table_dram"][:, js], smem["s5_table"][:, js]).then_inc(mem["tables_stored"], 16)

                n_slices = S5_TILES // S5_SLICE
                for b, c0 in enumerate(cols):
                    if b >= 2:
                        sp.wait_ge(proj_done, 1 + per * (b - 1))
                    if b > len(cols) - n_slices:
                        store_tables(b - len(cols) + n_slices - 1)
                    if b == 0:
                        for j in range(per):
                            js = slice(j * P, (j + 1) * P)
                            sp.dma_start(ring[:, 0, :, js], w_in[:, :, c0 + j * P:c0 + (j + 1) * P]).then_inc(
                                first_ready[j], 16)
                    else:
                        sp.dma_start(ring[:, b % 2], w_in[:, :, c0:c0 + BLOCK]).then_inc(w_ready[b % 2], 16)
                    if b == 0:
                        sp.dma_start(smem["s5_lam"][:], k["s5_lam"]).then_inc(lam_loaded, 16)
                        sp.dma_start(w_bd[:], k["w_bd"]).then_inc(loaded, 16)
                        sp.dma_start(conv_w[:], k["conv_w"]).then_inc(loaded, 16)
                        sp.dma_start(conv_b[:], k["conv_b"]).then_inc(loaded, 16)
                        for name in ("ident", "offmask", "causal", "sel8", "lru_b", "lru_lam", "head_par", "norm_w",
                                     "ln_par", "eps"):
                            sp.dma_start(mem[name][:], k[name]).then_inc(mem["consts_loaded"], 16)
                sp.wait_ge(proj_done, 1 + per * (len(cols) - 1))
                sp.dma_start(ring[:, 0], k["lru_w"]).then_inc(mem["lru_w_ready"], 16)
                store_tables(n_slices - 1)
                sp.wait_ge(mem["tables_stored"], 16 * (S5_TILES // S5_SLICE))

            @block.tensor
            def _(pe):
                pe.wait_ge(h_loaded, 16)
                for n in range(per * len(cols)):
                    if n == per:
                        pe.wait_ge(loaded, 48)
                        pe.wait_ge(evacuated, 1)
                        for c in range(DC):
                            mm = pe.matmul(ps[0][0:DECAY_ROW + HEADS, 0:T], w_bd[:, c, :], hT[:, c, :],
                                           start=(c == 0), stop=(c == DC - 1))
                        mm.then_inc(proj_done, 1)
                    g, b = place(n), n // per
                    if b == 0:
                        pe.wait_ge(first_ready[n], 16)
                    elif n % per == 0:
                        pe.wait_ge(w_ready[b % 2], 16 * ((b + 1) // 2))
                    if g >= 4:
                        pe.wait_ge(evacuated, g - 3)
                    j = n % per
                    for c in range(DC):
                        mm = pe.matmul(ps[g % 4][:, 0:T], ring[:, b % 2, c, j * P:(j + 1) * P], hT[:, c, :],
                                       start=(c == 0), stop=(c == DC - 1))
                    mm.then_inc(proj_done, 1)
                    if 4 <= n < 20:
                        i = n - 4
                        pe.wait_ge(squared, i + 1)
                        if i >= 2:
                            pe.wait_ge(rooted, i - 1)
                        pe.matmul(sums[i % 2][:, 0:T], ones[:], sq[:, i % 2, :], start=True, stop=True).then_inc(summed, 1)

            @block.scalar
            def _(act):
                def silu(n):
                    act.wait_ge(conv_done, n + 1)
                    act.activation(qkv[:, n, :], qkv[:, n, :], ACT.Silu).then_inc(silu_done, 1)

                step = Chain(act, act_step)
                act.wait_ge(lam_loaded, 16)
                s5_sines(act, sines, angles, smem)
                act.wait_ge(pads_zero, 1)
                act.wait_ge(mem["consts_loaded"], 16 * 10)
                for n in range(per * len(cols)):
                    if n == per:
                        act.wait_ge(proj_done, per + 1)
                        act.copy(bd[:, 0, :], ps[0][0:HEADS, 0:T])
                        act.copy(bd[:, 1, :], ps[0][DECAY_ROW:DECAY_ROW + HEADS, 0:T]).then_inc(evacuated, 1)
                    src = ps[place(n) % 4][:, 0:T]
                    act.wait_ge(proj_done, place(n) + 1)
                    if n in conv_of:
                        cs = conv_of[n]
                        if cs >= 4:
                            act.wait_ge(conv_done, cs - 3)
                        act.copy(cin[:, cs % 4, CONV - 1:], src).then_inc(evacuated, 1)
                    elif n < 32:
                        act.activation(y[:, n - 24 + DC, :], src, ACT.Silu).then_inc(evacuated, 1)
                    else:
                        act.activation(y[:, n - 40, :], src, ACT.Gelu_apprx_tanh).then_inc(evacuated, 1)
                    if 2 <= n < 26:
                        silu(n - 2)
                    if 2 <= n < 18:
                        i = n - 2
                        act.wait_ge(silu_done, i + 1)
                        if i >= 2:
                            act.wait_ge(summed, i - 1)
                        act.activation(sq[:, i % 2, :], qkv[:, i, :], ACT.Square).then_inc(squared, 1)
                    if 5 <= n < 21:
                        i = n - 5
                        act.wait_ge(summed, i + 1)
                        if i >= 2:
                            act.wait_ge(normed, i - 1)
                        q = i // DC
                        act.activation(nrm[:, i % 2, :], sums[i % 2][:, 0:T], ACT.Sqrt, scale=float(P) if q else 1.0,
                                       bias=eps[:, q:q + 1]).then_inc(rooted, 1)
                    if n == 26:
                        act.activation(ea[:], mem["head_par"][:, 0:1], ACT.Exp).then_inc(decay_exp, 1)
                        act.wait_ge(decay_in, 1)
                        step.done(act.activation(s1, s0, ACT.Abs))
                        act.activation(s1, s1, ACT.Exp, scale=-1.0).then_inc(decay_exp, 1)
                        step.done(act.activation(l8[:, 1, :], mem["lru_lam"][:], ACT.Abs))
                        act.activation(l8[:, 1, :], l8[:, 1, :], ACT.Exp, scale=-1.0).then_inc(decay_exp, 1)
                        act.activation(beta, bd[:, 0, :], ACT.Sigmoid).then_inc(decay_exp, 1)

            @block.gpsimd
            def _(pool):
                pool.wait_ge(angles, 3)
                pool.wait_ge(sines, 4)
                s5_tables(pool, Chain(pool, table_step).done, smem, sliced)

            @block.vector
            def _(dve):
                step = Chain(dve, conv_step)
                dve.memset(cin[:, :, 0:CONV - 1], 0.0).then_inc(pads_zero, 1)
                dve.wait_ge(pads_zero, 1)
                dve.wait_ge(lam_loaded, 16)
                s5_discretise(dve, Chain(dve, s5_step).done, sines, angles, smem)
                dve.wait_ge(loaded, 48)
                dve.wait_ge(mem["consts_loaded"], 16 * 10)
                hp, lam, link = mem["head_par"], mem["lru_lam"], step.done

                def decays():
                    dve.wait_ge(decay_exp, 4)
                    log1p_steps(dve, link, s2, s1, s3, bd[:, 1, :])
                    link(dve.scalar_tensor_tensor(out=s0, in0=s0, scalar=0.0, in1=s2, op0=ALU.max, op1=ALU.add))
                    link(dve.tensor_scalar(s0, s0, ea[:, 0:1], -1.0, ALU.mult, ALU.mult))
                    link(dve.memset(s1, 1.0))
                    for t0, n in CHUNKS:
                        link(dve.tensor_tensor_scan(G[:, t0:t0 + n], s1[:, t0:t0 + n], s0[:, t0:t0 + n], 0.0,
                                                    ALU.mult, ALU.add))
                    log1p_steps(dve, link, l8[:, 0, :], l8[:, 1, :], l8[:, 2, :], l8[:, 3, :])
                    link(dve.tensor_scalar(l8[:, 2, :], lam[:], -1.0, 0.0, ALU.mult, ALU.max))
                    link(dve.tensor_tensor(l8[:, 0, :], l8[:, 0, :], l8[:, 2, :], ALU.add))
                    link(dve.tensor_scalar(c8[:], l8[:, 0, :], -8.0, None, ALU.mult))

                for n, cs in conv_of.items():
                    if n == 32:
                        decays()
                    dve.wait_ge(evacuated, place(n) + 1)
                    src, dst = cin[:, cs % 4, :], qkv[:, n, :] if n < 24 else xa[:, n - 32, :]
                    w = lambda j: conv_w[:, cs, j:j + 1]
                    if n < 24:
                        step.done(dve.tensor_scalar(dst, src[:, 0:T], w(0), None, ALU.mult))
                    else:
                        step.done(dve.tensor_scalar(dst, src[:, 0:T], w(0), conv_b[:, n - 32:n - 31],
                                                    ALU.mult, ALU.add))
                    for j in (1, 2):
                        step.done(dve.scalar_tensor_tensor(out=dst, in0=src[:, j:j + T], scalar=w(j), in1=dst,
                                                           op0=ALU.mult, op1=ALU.add))
                    dve.scalar_tensor_tensor(out=dst, in0=src[:, 3:3 + T], scalar=w(3), in1=dst,
                                             op0=ALU.mult, op1=ALU.add).then_inc(conv_done, 1)
                    if n == 5:
                        dve.tensor_scalar(s0, bd[:, 1, :], hp[:, 1:2], None, ALU.add).then_inc(decay_in, 1)
                    if 6 <= n < 22:
                        i = n - 6
                        dve.wait_ge(rooted, i + 1)
                        link(dve.reciprocal(nrm[:, i % 2, :], nrm[:, i % 2, :]))
                        dve.tensor_tensor(qkv[:, i, :], qkv[:, i, :], nrm[:, i % 2, :], ALU.mult).then_inc(normed, 1)


def group_mixers(nc, k, ctx, mem):
    qkv, xa, y, bd, ring = mem["qkv"], mem["xa"], mem["y"], mem["bd"], mem["dense"]
    ident, offmask, causal, sel8, ones = mem["ident"], mem["offmask"], mem["causal"], mem["sel8"], mem["ones"]
    keys, queries, values = qkv[:, 0:8, :], qkv[:, 8:16, :], qkv[:, 16:24, :]
    NQ = 4
    SETS = [(1, 0, 4), (1, 4, 4), (2, 0, 4), (2, 4, 4), (0, 0, 8)]
    with ExitStack() as inner:
        sem = inner.enter_context(Signals(nc))
        sb = lambda name, shape: inner.enter_context(nc.sbuf_tensor(name, shape, F32))
        bank = [inner.enter_context(nc.psum_tensor(f"mix{b}", [P, BLOCK], F32)) for b in range(8)]
        gates = sb("gates", [P, 2 * DC, T])
        kdec = sb("kdec", [P, 3, HEADS * P])
        vbeta = sb("vbeta", [P, 3, HEADS * P])
        lru_t = xa
        gb = sb("g_rows", [P, HEADS, T])
        kb_o = sb("kb_then_o", [P, HEADS, T])
        sq = sb("squares", [P, 2, T])
        nrm = sb("norms", [P, 2, T])
        lru_u = nrm
        LT = sb("LT", [P, 5, 4, P])
        X = sb("X", [P, 4, 4, P])
        Y = sb("Y", [P, 4, 4, P])
        QK = sb("QK", [P, 4, 4, P])
        X0, Y0, QK0 = (sb(n, [META, HEADS, META]) for n in ("X0", "Y0", "QK0"))
        T1, LTo, r, vn = (ring[:, 1, 2 * i:2 * i + 2, :] for i in range(4))
        S = gates[:].rearrange("p c t -> p (c t)")[:, 0:HEADS * P].rearrange("p (h d) -> p h d", h=HEADS)
        colg, colb, kd, egl, nbeg = (sb(n, [P, 3, HEADS]) for n in ("colg", "colb", "kd", "egl", "nbeg"))
        c8, beta, G, hT = mem["c8"], mem["beta_G"][:, 0, :], mem["beta_G"][:, 1, :], mem["hT"]
        w_out = k["w_out"].rearrange("(q c p) n -> q p c n", q=2, p=P)
        w_out_ready = [[sem(f"w_out_{half}_{q}_ready") for q in ("lru", "delta")] for half in "ab"]
        projected, added = sem("out_projected"), sem("out_added")
        half_used = [sem("w_out_lru_used"), sem("w_out_delta_used")]
        s_lg, s_gate = sem("lru_gates_ready"), sem("gates_done")
        act_step, dve_step, pool_step = sem("act_step"), sem("dve_step"), sem("pool_step")
        s_th, s_m, s_sqrt, s_u, s_b, s_scan, s_y = (sem(n) for n in ("tanh_a", "lru_m", "lru_sqrt", "lru_ix",
                                                                     "lru_b_done", "lru_scan", "lru_y"))
        s_bc, s_gb, s_eg, s_kb, s_qg = (sem(n) for n in ("bcast_ready", "g_rows_done", "eg_done", "kb_done", "qg_done"))
        s_col, s_colc, s_kdx, s_kde, s_nb = (sem(n) for n in ("cols_ready", "cols_done", "kd_diff", "kd_exp", "nbeg"))
        s_tt, s_tok = sem("tok_ready"), sem("tok_done")
        s_diff, s_dexp, s_mask, s_kk, s_lt = (sem(n) for n in ("diff", "decay_mat", "decay_masked", "kk_ready", "lt_done"))
        s_lto, s_t1, s_t1c, s_pq, s_x2 = (sem(n) for n in ("lt_off", "t1_ready", "t1_done", "pq_ready", "xy_done"))
        s_init = sem("xy_init")
        s_ks, s_r, s_vn, s_vnc, s_o, s_oc, s_s, s_sc = (sem(n) for n in (
            "ks_ready", "rhs_done", "vnew_ready", "vnew_done", "o_ready", "o_done", "s_ready", "s_done"))
        s_osq, s_osum, s_on, s_of = (sem(n) for n in ("o_squared", "o_sums", "o_norm", "o_final"))
        lru_w = ring[:, 0].rearrange("p c n -> p (c n)").rearrange("p (g h q n) -> p g h q n", g=2, h=4, q=2)

        n_lv = lambda s: LEVELS if s < 4 else 4
        work = [(lv, s) for lv in range(LEVELS) for s in range(5) if lv < n_lv(s)]
        place = {w: i for i, w in enumerate(work)}

        def updates(i):
            lv, s = work[i]
            return (1,) if lv == n_lv(s) - 1 else (0, 1)

        rec = [(cc, half) for cc in range(3) for half in range(2)]

        with nc.Block(no_gpsimd_drain=True) as block:

            @block.sync
            def _(sp):
                sp.wait_ge(s_lg, 16)
                sp.dma_start(ring[:, 0], w_out[0][:, :, 0:BLOCK]).then_inc(w_out_ready[0][0], 16)
                sp.wait_ge(s_o, 6)
                sp.dma_start(ring[:, 1], w_out[1][:, :, 0:BLOCK]).then_inc(w_out_ready[0][1], 16)
                for q in range(2):
                    sp.wait_ge(half_used[q], 1)
                    sp.dma_start(ring[:, q], w_out[q][:, :, BLOCK:]).then_inc(w_out_ready[1][q], 16)

            @block.tensor
            def _(pe):
                for cc, (t0, n) in enumerate(CHUNKS):
                    for q, row in enumerate((G, beta)):
                        mm = pe.transpose(bank[0][0:n, (2 * cc + q) * HEADS:(2 * cc + q + 1) * HEADS],
                                          row[:, t0:t0 + n], ident[0:HEADS, 0:HEADS])
                mm.then_inc(s_col, 1)
                for h in range(HEADS):
                    if h >= 2:
                        pe.wait_ge(s_gb, h - 1)
                        pe.wait_ge(s_kb, h - 1)
                    o = 4 + 2 * (h % 2)
                    pe.matmul(bank[o][:, 0:T], sel8[:, h, :], G, start=True, stop=True).then_inc(s_bc, 1)
                    pe.matmul(bank[o + 1][:, 0:T], sel8[:, h, :], beta, start=True, stop=True).then_inc(s_bc, 1)
                pe.wait_ge(mem["lru_w_ready"], 16)
                for i in range(16):
                    g, m = i // 8, i % 8
                    if i >= 2:
                        pe.wait_ge(s_gate, i - 1)
                    for q in range(2):
                        mm = pe.matmul(bank[2 + i % 2][:, 0:T], lru_w[:, g, m // 2, q, (m % 2) * P:(m % 2 + 1) * P],
                                       xa[:, 2 * (m // 2) + q, :], start=(q == 0), stop=(q == 1))
                    mm.then_inc(s_lg, 1)
                pe.wait_ge(s_gate, 16)
                pe.wait_ge(s_colc, 2)
                for i in range(12):
                    cc, q, half = i // 4, i // 2 % 2, i % 2
                    t0, n = CHUNKS[cc]
                    if i >= 4:
                        pe.wait_ge(s_tok, i - 3)
                    for h in range(4):
                        src = (keys, values)[q]
                        mm = pe.transpose(bank[i % 4][0:n, h * P:(h + 1) * P], src[:, 4 * half + h, t0:t0 + n], ident[:])
                    mm.then_inc(s_tt, 1)
                pe.wait_ge(s_kb, HEADS)
                pe.wait_ge(s_gb, HEADS)
                for s, (cc, h0, nh) in enumerate(SETS):
                    t0, n = CHUNKS[cc]
                    if s >= 2:
                        pe.wait_ge(s_lt, 2 * (s - 1))
                    o = 4 + 2 * (s % 2)
                    for q, rhs in enumerate((kb_o, queries)):
                        for h in range(nh):
                            mm = pe.matmul(bank[o + q][0:n, h * n:(h + 1) * n], keys[:, h0 + h, t0:t0 + n],
                                           rhs[:, h0 + h, t0:t0 + n], start=True, stop=True)
                        mm.then_inc(s_kk, 1)
                pe.wait_ge(s_tok, 12)
                pe.wait_ge(s_lt, 10)

                def off_times_x(i):
                    lv, s = work[i]
                    cc, h0, nh = SETS[s]
                    n = CHUNKS[cc][1]
                    pe.wait_ge(s_lto, i + 1)
                    if lv > 0:
                        pe.wait_ge(s_x2, 2 * (place[(lv - 1, s)] + 1))
                    if i >= 2:
                        pe.wait_ge(s_t1c, i - 1)
                    for h in range(nh):
                        lto = LTo[0:n, i % 2, h * n:(h + 1) * n]
                        rhs = ident[0:n, 0:n] if lv == 0 else (X[:, s, h, :] if s < 4 else X0[:, h, :])
                        mm = pe.matmul(bank[i % 2][0:n, h * n:(h + 1) * n], lto, rhs, start=True, stop=True)
                    mm.then_inc(s_t1, 1)

                def products(i):
                    lv, s = work[i]
                    if lv == 0:
                        return
                    cc, h0, nh = SETS[s]
                    n = CHUNKS[cc][1]
                    pe.wait_ge(s_t1c, i + 1)
                    if i >= 2:
                        pe.wait_ge(s_x2, 2 * (i - 1))
                    o = 2 + 2 * (i % 2)
                    for q in updates(i):
                        for h in range(nh):
                            t1 = T1[0:n, i % 2, h * n:(h + 1) * n]
                            yy = Y[:, s, h, :] if s < 4 else Y0[:, h, :]
                            a, b = (yy, t1) if q == 0 else (t1, yy)
                            mm = pe.matmul(bank[o + q][0:n, h * n:(h + 1) * n], a, b, start=True, stop=True)
                        mm.then_inc(s_pq, 2 // len(updates(i)))

                for i in range(len(work) + 1):
                    if i < len(work):
                        off_times_x(i)
                    if i >= 1:
                        products(i - 1)
                pe.wait_ge(s_x2, 2 * len(work))
                pe.wait_ge(s_qg, 1)
                pe.wait_ge(s_nb, 1)

                def solve_rhs(i):
                    cc, half = rec[i]
                    t0, n = CHUNKS[cc]
                    if cc > 0:
                        pe.wait_ge(s_sc, i - 1)
                        for h in range(4):
                            mm = pe.matmul(bank[half][:, h * P:(h + 1) * P], keys[:, 4 * half + h, t0:t0 + n],
                                           S[:, 4 * half + h, :], start=True, stop=True)
                        mm.then_inc(s_ks, 1)

                def new_values(i):
                    cc, half = rec[i]
                    t0, n = CHUNKS[cc]
                    if cc > 0:
                        pe.wait_ge(s_r, i - 1)
                    if i >= 2:
                        pe.wait_ge(s_vnc, i - 1)
                    for h in range(4):
                        hh = 4 * half + h
                        if cc > 0:
                            yy, rhs = Y[:, 2 * (cc - 1) + half, h, :], r[:, half, h * P:(h + 1) * P]
                        else:
                            yy, rhs = Y0[:, hh, :], vbeta[0:n, 0, hh * P:(hh + 1) * P]
                        mm = pe.matmul(bank[2 + half][0:n, h * P:(h + 1) * P], yy, rhs, start=True, stop=True)
                    mm.then_inc(s_vn, 1)

                def outputs(i):
                    cc, half = rec[i]
                    t0, n = CHUNKS[cc]
                    pe.wait_ge(s_vnc, i + 1)
                    if i >= 2:
                        pe.wait_ge(s_oc, i - 1)
                    for h in range(4):
                        hh = 4 * half + h
                        out = bank[4 + half][:, h * n:(h + 1) * n]
                        v = vn[0:n, half, h * P:(h + 1) * P]
                        qk = QK[:, 2 * (cc - 1) + half, h, :] if cc > 0 else QK0[:, hh, :]
                        if cc > 0:
                            pe.matmul(out, S[:, hh, :], queries[:, hh, t0:t0 + n], start=True, stop=False)
                        mm = pe.matmul(out, v, qk, start=(cc == 0), stop=True)
                    mm.then_inc(s_o, 1)
                    if cc < 2:
                        if i >= 2:
                            pe.wait_ge(s_sc, i - 1)
                        for h in range(4):
                            hh = 4 * half + h
                            mm = pe.matmul(bank[6 + half][:, h * P:(h + 1) * P], kdec[0:n, cc, hh * P:(hh + 1) * P],
                                           vn[0:n, half, h * P:(h + 1) * P], start=True, stop=True)
                        mm.then_inc(s_s, 1)

                for cc in range(3):
                    for f in (solve_rhs, new_values, outputs):
                        for half in range(2):
                            f(2 * cc + half)
                def project(m, q, first, last):
                    out = bank[(m + 2) % 8][:, 0:T]
                    for c in range(DC):
                        if q == 1 and m == 0:
                            pe.wait_ge(s_of, c + 1)
                        mm = pe.matmul(out, ring[:, q, c, (m % 4) * P:(m % 4 + 1) * P], y[:, q * DC + c, :],
                                       start=(q == 0 and c == 0), stop=(q == 1 and c == DC - 1))
                    return mm

                pe.wait_ge(s_oc, 6)
                pe.wait_ge(s_y, DC)
                for half in range(2):
                    for q in range(2):
                        for m in range(4 * half, 4 * half + 4):
                            if half == 0 and q == 0:
                                for h in (2 * m, 2 * m + 1):
                                    pe.wait_ge(s_osq, h + 1)
                                    if h >= 2:
                                        pe.wait_ge(s_on, h - 1)
                                    pe.matmul(bank[h % 2][:, 0:T], ones[:], sq[:, h % 2, :], start=True,
                                              stop=True).then_inc(s_osum, 1)
                            if m % 4 == 0:
                                pe.wait_ge(w_out_ready[half][q], 16)
                            if half == 1 and q == 0 and m % 4 == 2:
                                pe.wait_ge(s_on, HEADS)
                            mm = project(m, q, q == 0, q == 1)
                            if q == 1:
                                mm.then_inc(projected, 1)
                                if m == 3:
                                    pe.wait_ge(projected, 4)
                                    pe.sem_inc(half_used[1], 1)
                            elif m == 3:
                                mm.then_inc(half_used[0], 1)

            @block.scalar
            def _(act):
                eps = mem["eps"]
                step = Chain(act, act_step)
                for h in range(HEADS):
                    act.wait_ge(s_bc, 2 * h + 1)
                    src = bank[4 + 2 * (h % 2)][:, 0:T]
                    act.copy(gb[:, h, :], src).then_inc(s_gb, 1)
                for i in range(16):
                    act.wait_ge(s_lg, i + 1)
                    act.activation(gates[:, i, :], bank[2 + i % 2][:, 0:T], ACT.Sigmoid,
                                   bias=mem["lru_b"][:, i:i + 1]).then_inc(s_gate, 1)
                act.wait_ge(s_kdx, 1)
                act.activation(kd[:], kd[:], ACT.Exp).then_inc(s_kde, 1)
                act.activation(egl[:], egl[:], ACT.Exp).then_inc(s_kde, 1)
                act.activation(nbeg[:], nbeg[:], ACT.Exp).then_inc(s_kde, 1)
                for s, (cc, h0, nh) in enumerate(SETS):
                    n = CHUNKS[cc][1]
                    act.wait_ge(s_diff, s + 1)
                    d = LT[0:n, s].rearrange("p a b -> p (a b)")[:, 0:nh * n]
                    act.activation(d, d, ACT.Exp).then_inc(s_dexp, 1)
                act.activation(gb[:], gb[:], ACT.Exp).then_inc(s_eg, 1)
                for c in range(DC):
                    act.wait_ge(s_u, c + 1)
                    act.activation(lru_t[:, c, :], gates[:, c, :], ACT.Tanh, scale=c8[:, c:c + 1]).then_inc(s_th, 1)
                act.wait_ge(s_th, DC)
                for c in range(DC):
                    act.activation(gates[:, c, :], gates[:, c, :], ACT.Exp, scale=c8[:, c:c + 1]).then_inc(s_th, 1)
                for i, (lv, s) in enumerate(work):
                    cc, h0, nh = SETS[s]
                    n = CHUNKS[cc][1]
                    act.wait_ge(s_t1, i + 1)
                    if i >= 2:
                        before = sum(1 for w in work[:i - 1] if w[0] > 0)
                        if before:
                            act.wait_ge(s_pq, 2 * before)
                        if work[i - 2][0] == 0:
                            act.wait_ge(s_x2, 2 * (i - 1))
                    act.copy(T1[0:n, i % 2, 0:nh * n], bank[i % 2][0:n, 0:nh * n]).then_inc(s_t1c, 1)
                    if i % 3 == 0 and 0 < i <= 3 * DC:
                        c = i // 3 - 1
                        act.wait_ge(s_m, c + 1)
                        act.activation(lru_t[:, c, :], lru_t[:, c, :], ACT.Sqrt).then_inc(s_sqrt, 1)
                for cc in range(3):
                    t0, n = CHUNKS[cc]
                    for half in range(2):
                        i = 2 * cc + half
                        act.wait_ge(s_vn, i + 1)
                        if i >= 2:
                            act.wait_ge(s_o, i - 1)
                            act.wait_ge(s_s, i - 1)
                        act.copy(vn[0:n, half, :], bank[2 + half][0:n, :]).then_inc(s_vnc, 1)
                    for half in range(2):
                        i = 2 * cc + half
                        act.wait_ge(s_o, i + 1)
                        act.copy(kb_o[:, 4 * half:4 * half + 4, t0:t0 + n],
                                 bank[4 + half][:, 0:4 * n].rearrange("p (h t) -> p h t", h=4)).then_inc(s_oc, 1)
                act.wait_ge(s_oc, 6)
                for h in range(HEADS + 1):
                    if h < HEADS:
                        if h >= 2:
                            act.wait_ge(s_osum, h - 1)
                        act.activation(sq[:, h % 2, :], kb_o[:, h, :], ACT.Square).then_inc(s_osq, 1)
                    if h >= 1:
                        j = h - 1
                        act.wait_ge(s_osum, j + 1)
                        if j >= 2:
                            act.wait_ge(s_of, j - 1)
                        act.activation(nrm[:, j % 2, :], bank[j % 2][:, 0:T], ACT.Sqrt, scale=1.0 / P,
                                       bias=eps[:, 0:1]).then_inc(s_on, 1)

            @block.gpsimd
            def _(pool):
                step = Chain(pool, pool_step)
                pool.wait_ge(s_gate, 16)
                for c in range(DC):
                    pool.tensor_tensor(gates[:, DC + c, :], gates[:, DC + c, :], xa[:, c, :], ALU.mult).then_inc(s_u, 1)
                for s, (cc, h0, nh) in enumerate(SETS):
                    n = CHUNKS[cc][1]
                    pool.wait_ge(s_dexp, s + 1)
                    d = LT[0:n, s].rearrange("p a b -> p (a b)")[:, 0:nh * n].rearrange("p (h t) -> p h t", h=nh)
                    pool.tensor_tensor(d, d, causal[0:n, 0:n].unsqueeze(1).broadcast_to([n, nh, n]),
                                       ALU.mult).then_inc(s_mask, 1)
                pool.wait_ge(s_lt, 10)
                for i, (lv, s) in enumerate(work):
                    cc, h0, nh = SETS[s]
                    n = CHUNKS[cc][1]
                    if i >= 2:
                        pool.wait_ge(s_t1, i - 1)
                        if work[i - 2][0] == 0:
                            pool.wait_ge(s_x2, 2 * (i - 1))
                    d = LT[0:n, s].rearrange("p a b -> p (a b)")[:, 0:nh * n].rearrange("p (h t) -> p h t", h=nh)
                    o = LTo[0:n, i % 2, 0:nh * n].rearrange("p (h t) -> p h t", h=nh)
                    pool.tensor_tensor(o, d, offmask[0:n, lv, 0:n].unsqueeze(1).broadcast_to([n, nh, n]),
                                       ALU.mult).then_inc(s_lto, 1)
                    if i % 3 == 0 and 9 <= i <= 3 * DC + 6:
                        c = i // 3 - 3
                        pool.wait_ge(s_scan, c + 1)
                        pool.tensor_tensor(y[:, c, :], y[:, c, :], xa[:, c, :], ALU.mult).then_inc(s_y, 1)

            @block.vector
            def _(dve):
                step = Chain(dve, dve_step)
                link = step.done
                link(dve.memset(colg[:], 0.0))
                link(dve.memset(colb[:], 0.0))
                for h in range(HEADS):
                    dve.wait_ge(s_bc, 2 * h + 2)
                    dve.tensor_tensor(kb_o[:, h, :], keys[:, h, :], bank[5 + 2 * (h % 2)][:, 0:T],
                                      ALU.mult).then_inc(s_kb, 1)
                dve.wait_ge(s_col, 1)
                for q, dst in enumerate((colg, colb)):
                    src = bank[0][:, 0:6 * HEADS].rearrange("p (c q h) -> p c q h", c=3, q=2)
                    link(dve.tensor_copy(dst[0:META, 0, :], src[0:META, 0, q, :]))
                    dve.tensor_copy(dst[:, 1:3, :], src[:, 1:3, q, :]).then_inc(s_colc, 1)
                    dve.wait_ge(s_colc, q + 1)
                dve.wait_ge(s_gb, HEADS)
                for cc, (t0, n) in enumerate(CHUNKS):
                    link(dve.tensor_copy(egl[:, cc, :], gb[:, :, t0 + n - 1]))
                link(dve.tensor_copy(nbeg[:], colg[:]))
                dve.tensor_tensor(kd[:], egl[:], colg[:], ALU.subtract).then_inc(s_kdx, 1)
                for s, (cc, h0, nh) in enumerate(SETS):
                    t0, n = CHUNKS[cc]
                    d = LT[0:n, s].rearrange("p a b -> p (a b)")[:, 0:nh * n].rearrange("p (h t) -> p h t", h=nh)
                    link(dve.tensor_tensor(d, gb[0:n, h0:h0 + nh, t0:t0 + n],
                                           colg[0:n, cc, h0:h0 + nh].unsqueeze(2).broadcast_to([n, nh, n]),
                                           ALU.subtract))
                    dve.tensor_scalar(d, d, 0.0, None, ALU.min).then_inc(s_diff, 1)
                dve.wait_ge(s_kde, 3)
                dve.scalar_tensor_tensor(out=nbeg[:].rearrange("p a b -> p (a b)"),
                                         in0=nbeg[:].rearrange("p a b -> p (a b)"), scalar=-1.0,
                                         in1=colb[:].rearrange("p a b -> p (a b)"), op0=ALU.mult,
                                         op1=ALU.mult).then_inc(s_nb, 1)
                for i in range(12):
                    cc, q, half = i // 4, i // 2 % 2, i % 2
                    t0, n = CHUNKS[cc]
                    dve.wait_ge(s_tt, i + 1)
                    dst, col = ((kdec, kd), (vbeta, colb))[q]
                    dve.tensor_tensor(
                        dst[0:n, cc, 4 * half * P:4 * (half + 1) * P].rearrange("p (h d) -> p h d", h=4),
                        bank[i % 4][0:n, :].rearrange("p (h d) -> p h d", h=4),
                        col[0:n, cc, 4 * half:4 * half + 4].unsqueeze(2).broadcast_to([n, 4, P]),
                        ALU.mult).then_inc(s_tok, 1)
                for s, (cc, h0, nh) in enumerate(SETS):
                    n = CHUNKS[cc][1]
                    o = 4 + 2 * (s % 2)
                    d = LT[0:n, s].rearrange("p a b -> p (a b)")[:, 0:nh * n]
                    qk = QK[:, s].rearrange("p a b -> p (a b)") if s < 4 else QK0[:].rearrange("p a b -> p (a b)")
                    dve.wait_ge(s_mask, s + 1)
                    dve.wait_ge(s_kk, 2 * s + 2)
                    dve.tensor_tensor(qk, d, bank[o + 1][0:n, 0:nh * n], ALU.mult).then_inc(s_lt, 1)
                    dve.wait_ge(s_lt, 2 * s + 1)
                    dve.tensor_tensor(d, d, bank[o][0:n, 0:nh * n], ALU.mult).then_inc(s_lt, 1)
                def recurrent_unit(i):
                    c, third = divmod(i - 1, 3)
                    if third == 0 and c < DC:
                        dve.wait_ge(s_th, DC + c + 1)
                        link(dve.tensor_scalar(lru_u[:, c % 2, :], lru_t[:, c, :], -1.0, 1.0, ALU.mult, ALU.add))
                        link(dve.reciprocal(lru_u[:, c % 2, :], lru_u[:, c % 2, :]))
                    if third == 1 and c < DC:
                        dve.scalar_tensor_tensor(out=lru_t[:, c, :], in0=lru_t[:, c, :], scalar=-2.0,
                                                 in1=lru_u[:, c % 2, :], op0=ALU.mult, op1=ALU.mult).then_inc(s_m, 1)
                    if third == 2 and 1 <= c <= DC:
                        c -= 1
                        dve.wait_ge(s_sqrt, c + 1)
                        link(dve.tensor_tensor(gates[:, DC + c, :], gates[:, DC + c, :], lru_t[:, c, :], ALU.mult))
                        dve.tensor_tensor_scan(xa[:, c, :], gates[:, c, :], gates[:, DC + c, :], 0.0,
                                               ALU.mult, ALU.add).then_inc(s_scan, 1)
                    if i == 3 * DC + 4:
                        dve.wait_ge(s_eg, 1)
                        dve.tensor_tensor(queries, queries, gb[:], ALU.mult).then_inc(s_qg, 1)

                for i, (lv, s) in enumerate(work):
                    cc, h0, nh = SETS[s]
                    n = CHUNKS[cc][1]
                    if lv == 0:
                        idb = ident[0:n, 0:n].unsqueeze(1).broadcast_to([n, nh, n])
                        xx = X[:, s] if s < 4 else X0[:]
                        yy = Y[:, s] if s < 4 else Y0[:]
                        dve.wait_ge(s_t1c, i + 1)
                        dve.tensor_tensor(xx, idb, T1[0:n, i % 2, 0:nh * n].rearrange("p (h t) -> p h t", h=nh),
                                          ALU.subtract).then_inc(s_x2, 1)
                        dve.tensor_tensor(yy, idb, LTo[0:n, i % 2, 0:nh * n].rearrange("p (h t) -> p h t", h=nh),
                                          ALU.subtract).then_inc(s_x2, 1)
                        recurrent_unit(i)
                        continue
                    o = 2 + 2 * (i % 2)
                    m = sum(1 for w in work[:i + 1] if w[0] > 0)
                    for q in updates(i):
                        t = ((X, X0), (Y, Y0))[q][s == 4]
                        t = (t[:, s] if s < 4 else t[:]).rearrange("p a b -> p (a b)")
                        dve.wait_ge(s_pq, 2 * m)
                        if i >= 1:
                            dve.wait_ge(s_x2, 2 * i)
                        dve.tensor_tensor(t, t, bank[o + q][0:n, 0:nh * n], ALU.subtract).then_inc(
                            s_x2, 2 // len(updates(i)))
                    recurrent_unit(i)
                for cc in range(3):
                    t0, n = CHUNKS[cc]
                    if cc > 0:
                        for half in range(2):
                            i = 2 * cc + half
                            dve.wait_ge(s_ks, i - 1)
                            rr = r[:, half, :].rearrange("p (h d) -> p h d", h=4)
                            if cc > 1:
                                dve.wait_ge(s_vn, i - 1)
                            link(dve.tensor_tensor(rr, bank[half][:].rearrange("p (h d) -> p h d", h=4),
                                                   nbeg[:, cc, 4 * half:4 * half + 4].unsqueeze(2).broadcast_to([P, 4, P]),
                                                   ALU.mult))
                            dve.tensor_tensor(r[:, half, :], r[:, half, :],
                                              vbeta[:, cc, 4 * half * P:4 * (half + 1) * P], ALU.add).then_inc(s_r, 1)
                    if cc < 2:
                        for half in range(2):
                            i = 2 * cc + half
                            sh = S[:, 4 * half:4 * half + 4, :]
                            dve.wait_ge(s_s, i + 1)
                            src = bank[6 + half][:].rearrange("p (h d) -> p h d", h=4)
                            if cc == 0:
                                dve.tensor_copy(sh, src).then_inc(s_sc, 1)
                                continue
                            link(dve.tensor_tensor(sh, sh, egl[:, cc, 4 * half:4 * half + 4].unsqueeze(2).broadcast_to(
                                [P, 4, P]), ALU.mult))
                            dve.tensor_tensor(sh, sh, src, ALU.add).then_inc(s_sc, 1)
                for h in range(HEADS):
                    dve.wait_ge(s_on, h + 1)
                    link(dve.reciprocal(nrm[:, h % 2, :], nrm[:, h % 2, :]))
                    link(dve.tensor_tensor(kb_o[:, h, :], kb_o[:, h, :], nrm[:, h % 2, :], ALU.mult))
                    dve.scalar_tensor_tensor(out=y[:, DC + h, :], in0=kb_o[:, h, :], scalar=mem["norm_w"][:, 0:1],
                                             in1=y[:, DC + h, :], op0=ALU.mult, op1=ALU.mult).then_inc(s_of, 1)
                for m in range(DC):
                    dve.wait_ge(projected, m + 1)
                    dve.scalar_tensor_tensor(out=hT[:, m, :], in0=hT[:, m, :], scalar=ALPHA,
                                             in1=bank[(m + 2) % 8][:, 0:T], op0=ALU.mult, op1=ALU.add).then_inc(added, 1)


def gate_up_weights(mem, s):
    return mem["experts"][:, s, 0:2 * D * FF // P].rearrange("p (c n) -> p c n", c=DC)


def down_weights(mem, s):
    return mem["experts"][:, s, 2 * D * FF // P:].rearrange("p (c n) -> p c n", c=FC)


def load_gate_up(sp, k, mem, layer, q, u):
    for e in range(2):
        w = gate_up_weights(mem, 2 * (u % 2) + e)
        for name, cols in (("moe_gate", slice(0, FF)), ("moe_up", slice(FF, 2 * FF))):
            src = k[name][layer].rearrange("e (p c) f -> e p c f", p=P)[q * 2 + e]
            sp.dma_start(w[:, :, cols], src).then_inc(mem["gate_up_ready"][layer][u % 2], 16)


def load_down(sp, k, mem, layer, q, u):
    for e in range(2):
        src = k["moe_down"][layer].rearrange("e (c p) d -> e p c d", p=P)[q * 2 + e]
        sp.dma_start(down_weights(mem, 2 * (u % 2) + e), src).then_inc(mem["down_ready"][layer][u % 2], 16)


def load_router(sp, k, mem, layer):
    loaded = mem["router_loaded"]
    sp.dma_start(mem["router_w"][:], k["router_w"][layer]).then_inc(loaded, 16)
    sp.dma_start(mem["router_b"][:], k["router_b"][layer:layer + 1, :].broadcast_to([P, E])).then_inc(loaded, 16)
    sp.dma_start(mem["after"][:], k["after"]).then_inc(loaded, 16)
    sp.dma_start(mem["lower"][:], k["lower"]).then_inc(loaded, 16)
    w_gu, w_dn = shared_weights(mem)
    for q, name in enumerate(("sh_gate", "sh_up")):
        sp.dma_start(w_gu[:, :, q * FF:(q + 1) * FF],
                     k[name][layer].rearrange("(c p) f -> p c f", p=P)).then_inc(mem["shared_gate_up_ready"], 16)
    sp.dma_start(w_dn, k["sh_down"][layer].rearrange("(c p) d -> p c d", p=P)).then_inc(mem["shared_down_ready"], 16)


def shared_weights(mem):
    ring = mem["dense"]
    return ring[:, 0], ring[:, 1].rearrange("p c n -> p (c n)")[:, 0:FC * D].rearrange("p (c n) -> p c n", c=FC)


def load_first_experts(sp, k, mem, layer):
    for q in range(2):
        load_gate_up(sp, k, mem, layer, q, q)
        load_down(sp, k, mem, layer, q, q)


def layer_norm(nc, k, mem, which, source, loads=None, pool_work=None):
    hT, acc, ones, ln, eps = mem["hT"], mem["acc"], mem["ones"], mem["ln_par"], mem["eps"]
    with ExitStack() as inner:
        sem = inner.enter_context(Signals(nc, f"ln{which}_"))
        sb = lambda name, shape: inner.enter_context(nc.sbuf_tensor(f"ln{which}_{name}", shape, F32))
        sums = inner.enter_context(nc.psum_tensor(f"ln{which}_sums", [P, BLOCK], F32))
        sqs = inner.enter_context(nc.psum_tensor(f"ln{which}_sqs", [P, BLOCK], F32))
        sq = sb("sq", [P, DC, T])
        mean, rstd = sb("mean", [P, T]), sb("rstd", [P, T])
        added, summed, meaned, centred = sem("added"), sem("summed"), sem("meaned"), sem("centred")
        squared, sq_summed, rooted, inverted, scaled, out = (sem("squared"), sem("sq_summed"), sem("rooted"),
                                                             sem("inverted"), sem("scaled"), sem("out"))
        with nc.Block(no_gpsimd_drain=True) as block:
            if loads is not None:

                @block.sync
                def _(sp):
                    loads(sp)

            if pool_work is not None:

                @block.gpsimd
                def _(pool):
                    pool_work(pool)

            @block.tensor
            def _(pe):
                for c in range(DC):
                    if source == "acc":
                        pe.wait_ge(added, c + 1)
                    mm = pe.matmul(sums[:, 0:T], ones[:], hT[:, c, :], start=(c == 0), stop=(c == DC - 1))
                mm.then_inc(summed, 1)
                for c in range(DC):
                    pe.wait_ge(squared, c + 1)
                    mm = pe.matmul(sqs[:, 0:T], ones[:], sq[:, c, :], start=(c == 0), stop=(c == DC - 1))
                mm.then_inc(sq_summed, 1)

            @block.scalar
            def _(act):
                for c in range(DC):
                    act.wait_ge(centred, c + 1)
                    act.activation(sq[:, c, :], hT[:, c, :], ACT.Square).then_inc(squared, 1)
                act.wait_ge(sq_summed, 1)
                act.activation(rstd[:], sqs[:, 0:T], ACT.Sqrt, scale=1.0 / D, bias=eps[:, 2:3]).then_inc(rooted, 1)
                for c in range(DC):
                    gain, shift = (ln[:, (2 * which + i) * DC + c:(2 * which + i) * DC + c + 1] for i in range(2))
                    act.wait_ge(scaled, c + 1)
                    act.activation(hT[:, c, :], hT[:, c, :], ACT.Identity, scale=gain, bias=shift).then_inc(out, 1)

            @block.vector
            def _(dve):
                if source == "acc":
                    for c in range(DC):
                        dve.tensor_tensor(hT[:, c, :], hT[:, c, :], acc[:, c, :], ALU.add).then_inc(added, 1)
                dve.wait_ge(summed, 1)
                dve.tensor_scalar(mean[:], sums[:, 0:T], 1.0 / D, None, ALU.mult).then_inc(meaned, 1)
                dve.wait_ge(meaned, 1)
                for c in range(DC):
                    dve.tensor_tensor(hT[:, c, :], hT[:, c, :], mean[:], ALU.subtract).then_inc(centred, 1)
                dve.wait_ge(rooted, 1)
                dve.reciprocal(rstd[:], rstd[:]).then_inc(inverted, 1)
                dve.wait_ge(inverted, 1)
                for c in range(DC):
                    dve.tensor_tensor(hT[:, c, :], hT[:, c, :], rstd[:], ALU.mult).then_inc(scaled, 1)


def router_and_shared(nc, k, mem, layer):
    hT, ident, pg = mem["hT"], mem["ident"], mem["pg"]
    with ExitStack() as inner:
        sem = inner.enter_context(Signals(nc, f"r{layer}_"))
        sb = lambda name, shape, dt=F32: inner.enter_context(nc.sbuf_tensor(f"r{layer}_{name}", shape, dt))
        bank = [inner.enter_context(nc.psum_tensor(f"r{layer}_b{b}", [P, BLOCK], F32)) for b in range(8)]
        rows = sb("rows", [P, 3, D])
        wr, rb, after, lower = (mem[n] for n in ("router_w", "router_b", "after", "lower"))
        sc, bi, mb, mr, sel, gt = (sb(n, [P, 3, E]) for n in ("sc", "bi", "mb", "mr", "sel", "gt"))
        m8 = sb("m8", [P, 3 * GROUPS, 8])
        gs, rk, gm = (sb(n, [P, 3, GROUPS]) for n in ("gs", "rk", "gm"))
        cmp, eq = sb("cmp", [P, 3 * GROUPS, GROUPS]), sb("eq", [P, 3 * GROUPS, GROUPS])
        t8, ws = sb("t8", [P, 3, 8]), sb("ws", [P, 3])
        maskT = sb("maskT", [E, T])
        cm = sb("cm", [E, 1])
        row = sb("row", [1, 2])
        silu = mem["shared_act"]
        loaded, gu_ready = mem["router_loaded"], mem["shared_gate_up_ready"]
        rows_t, rows_c, stored = sem("rows_turned"), sem("rows_copied"), mem["rows_stored"]
        zero, logits, scored, step_s = sem("zeroed"), sem("logits"), sem("scored"), sem("step")
        selected, gated, ranked, placed = sem("selected"), sem("gated"), sem("ranked"), sem("placed")
        counted, maxed = sem("count_turned"), mem["count_ready"]
        sh_gu, sh_act, sum_zero = sem("sh_gate"), sem("sh_silu"), sem("sum_zeroed")
        w_gu, _ = shared_weights(mem)
        with nc.Block(no_gpsimd_drain=True) as block:

            @block.sync
            def _(sp):
                for tt, (t0, n) in enumerate(TILES):
                    sp.wait_ge(rows_c, 2 * tt + 2)
                    sp.dma_start(mem["rows_dram"][t0:t0 + n, :], rows[0:n, tt, :]).then_inc(stored, 16)

            @block.tensor
            def _(pe):
                pe.wait_ge(loaded, 64 * (layer + 1))
                for tt, (t0, n) in enumerate(TILES):
                    for c in range(DC):
                        mm = pe.matmul(bank[0][0:n, tt * E:(tt + 1) * E], hT[:, c, t0:t0 + n], wr[:, c, :],
                                       start=(c == 0), stop=(c == DC - 1))
                mm.then_inc(logits, 1)
                for i in range(6):
                    tt, half = i // 2, i % 2
                    t0, n = TILES[tt]
                    if i >= 2:
                        pe.wait_ge(rows_c, i - 1)
                    for c in range(4):
                        mm = pe.transpose(bank[1 + i % 2][0:n, c * P:(c + 1) * P], hT[:, 4 * half + c, t0:t0 + n],
                                          ident[:])
                    mm.then_inc(rows_t, 1)
                pe.wait_ge(gu_ready, 32 * (layer + 1))
                for m in range(FC):
                    for c in range(DC):
                        mm = pe.matmul(bank[3 + m][:, 0:T], w_gu[:, c, m * P:(m + 1) * P], hT[:, c, :],
                                       start=(c == 0), stop=(c == DC - 1))
                    mm.then_inc(sh_gu, 1)
                pe.wait_ge(selected, 1)
                for tt, (t0, n) in enumerate(TILES):
                    mm = pe.matmul(bank[7][0:E, 0:T], sel[0:n, tt, :], after[0:n, tt, :], start=(tt == 0), stop=(tt == 2))
                mm.then_inc(ranked, 1)
                pe.wait_ge(gated, 1)
                pe.wait_ge(rows_c, 6)
                for q, src in enumerate((sel, gt)):
                    for tt, (t0, n) in enumerate(TILES):
                        mm = pe.transpose(bank[1 + q][0:E, t0:t0 + n], src[0:n, tt, :], ident[0:n, 0:n])
                    mm.then_inc(ranked, 1)
                pe.wait_ge(counted, 1)
                pe.transpose(bank[0][0:1, 0:E], cm[:, 0:1], ident[0:E, 0:E]).then_inc(ranked, 1)

            @block.scalar
            def _(act):
                act.wait_ge(logits, 1)
                act.wait_ge(zero, 1)
                lg = bank[0][:, 0:3 * E].rearrange("p (t e) -> p t e", t=3)
                act.activation(sc[:, 0:2, :], lg[:, 0:2, :], ACT.Sigmoid).then_inc(scored, 1)
                act.activation(sc[0:META, 2, :], lg[0:META, 2, :], ACT.Sigmoid).then_inc(scored, 1)
                for i in range(6):
                    tt, half = i // 2, i % 2
                    n = TILES[tt][1]
                    act.wait_ge(rows_t, i + 1)
                    src = bank[1 + i % 2][0:n, :].rearrange("p (c q r) -> p c q r", c=4, r=DC)
                    dst = rows[0:n, tt, :].rearrange("p (r c q) -> p c q r", r=DC, c=DC)[:, 4 * half:4 * half + 4]
                    act.copy(dst, src).then_inc(rows_c, 1)
                for m in range(FC):
                    act.wait_ge(sh_gu, m + 1)
                    act.activation(silu[:, m, :], bank[3 + m][:, 0:T], ACT.Silu).then_inc(sh_act, 1)

            @block.gpsimd
            def _(pool):
                pool.memset(mem["acc"][:], 0.0).then_inc(sum_zero, 1)

            @block.vector
            def _(dve):
                step = Chain(dve, step_s)
                link = step.done
                dve.memset(sc[:], 0.5).then_inc(zero, 1)
                dve.wait_ge(loaded, 64 * (layer + 1))
                dve.wait_ge(scored, 2)
                link(dve.tensor_tensor(bi[:], sc[:], rb[:].unsqueeze(1).broadcast_to([P, 3, E]), ALU.add))
                for i in range(3 * GROUPS):
                    ins = dve.max(out=m8[:, i, :], in_=bi[:, i // GROUPS, (i % GROUPS) * 8:(i % GROUPS + 1) * 8])
                link(ins)
                gsf = gs[:].rearrange("p t g -> p (t g)")
                link(dve.tensor_tensor(gsf, m8[:, :, 0], m8[:, :, 1], ALU.add))
                for tt in range(3):
                    a = gs[:, tt, :].unsqueeze(1).broadcast_to([P, GROUPS, GROUPS])
                    b = gs[:, tt, :].unsqueeze(2).broadcast_to([P, GROUPS, GROUPS])
                    o = slice(tt * GROUPS, (tt + 1) * GROUPS)
                    link(dve.tensor_tensor(cmp[:, o, :], a, b, ALU.is_gt))
                    link(dve.tensor_tensor(eq[:, o, :], a, b, ALU.is_equal))
                    link(dve.tensor_tensor(eq[:, o, :], eq[:, o, :], lower[:], ALU.mult))
                link(dve.tensor_tensor(cmp[:], cmp[:], eq[:], ALU.add))
                link(dve.tensor_reduce(rk[:].rearrange("p t g -> p (t g)"), cmp[:], AX_X, ALU.add))
                link(dve.tensor_scalar(gm[:], rk[:], float(TOP_GROUPS), None, ALU.is_lt))
                link(dve.tensor_scalar(rk[:], gm[:], 1e30, -1e30, ALU.mult, ALU.add))
                wide = lambda t: t[:].rearrange("p t g -> p (t g)").unsqueeze(2).broadcast_to([P, 3 * GROUPS, 8])
                flat = lambda t: t[:].rearrange("p t (g i) -> p (t g) i", i=8)
                link(dve.tensor_tensor(flat(mb), flat(bi), wide(gm), ALU.mult))
                link(dve.tensor_tensor(flat(mb), flat(mb), wide(rk), ALU.add))
                for tt in range(3):
                    link(dve.max(out=t8[:, tt, :], in_=mb[:, tt, :]))
                    link(dve.match_replace(out=mr[:, tt, :], in_to_replace=t8[:, tt, :], in_values=mb[:, tt, :],
                                           imm_value=-3e30))
                dve.tensor_tensor(sel[:], mr[:], mb[:], ALU.not_equal).then_inc(selected, 1)
                dve.wait_ge(selected, 1)
                link(dve.tensor_tensor(gt[:], sc[:], sel[:], ALU.mult))
                link(dve.tensor_reduce(ws[:], gt[:], AX_X, ALU.add))
                link(dve.reciprocal(ws[:], ws[:]))
                link(dve.tensor_scalar(ws[:], ws[:], SCALE, None, ALU.mult))
                dve.tensor_tensor(gt[:], gt[:], ws[:].unsqueeze(2).broadcast_to([P, 3, E]), ALU.mult).then_inc(gated, 1)
                dve.wait_ge(ranked, 2)
                link(dve.tensor_copy(maskT[:], bank[1][0:E, 0:T]))
                link(dve.scalar_tensor_tensor(out=pg[:, 0, :], in0=bank[7][0:E, 0:T], scalar=1.0, in1=maskT[:],
                                              op0=ALU.add, op1=ALU.mult))
                link(dve.tensor_reduce(cm[:], pg[:, 0, :], AX_X, ALU.max))
                dve.tensor_scalar_add(pg[:, 0, :], pg[:, 0, :], -1.0).then_inc(counted, 1)
                dve.wait_ge(ranked, 3)
                dve.tensor_copy(pg[:, 1, :], bank[2][0:E, 0:T]).then_inc(placed, 1)
                dve.wait_ge(ranked, 4)
                link(dve.tensor_reduce(row[:, 0:1], bank[0][0:1, 0:E], AX_X, ALU.max))
                dve.tensor_copy(mem["count"][:], row[:, 0:1]).then_inc(maxed, 1)


def experts(nc, k, mem, layer):
    acc, ident, pg = mem["acc"], mem["ident"], mem["pg"]
    base, slot_id, tok = mem["pair_base"], mem["slot_id"], mem["tok"]
    AHEAD = 3
    with ExitStack() as inner:
        sem = inner.enter_context(Signals(nc, f"e{layer}_"))
        sb = lambda name, shape, dt=F32: inner.enter_context(nc.sbuf_tensor(f"e{layer}_{name}", shape, dt))
        bank = [inner.enter_context(nc.psum_tensor(f"e{layer}_b{b}", [P, BLOCK], F32)) for b in range(8)]
        t0b, t1b, gub, atb, y0b, y1b = bank[:6]
        cb = bank[6:] + [y0b, y1b]
        xg = sb("xg", [P, 2, D])
        xgT = sb("xgT", [P, 2, DC, P])
        selw = sb("selw", [E, 2, P])
        basew = sb("basew", [E, P])
        gsb, hit = sb("gsb", [P, T]), sb("hit", [P, T])
        sg = sb("sg", [P, 4, T])
        idf, idx = sb("idf", [P, 1]), sb("idx", [P, 4, 1], I32)
        sl, ac, aT, ys = sb("sl", [P, FF]), sb("ac", [P, FF]), sb("aT", [P, FC, P]), sb("ys", [P, D])
        gu_ready, dn_ready = mem["gate_up_ready"][layer], mem["down_ready"][layer]
        based, selw_ok, sel_mm, gate_in, sg_ok, idf_ok, idx_ok = (sem(n) for n in (
            "base_moved", "pair_selected", "rows_broadcast", "gates_in", "scatter_ready", "index_summed", "index_ready"))
        sh_up, sh_mul, sh_dn, sh_out = (sem(n) for n in ("sh_up", "sh_mul", "sh_down", "sh_out"))
        hT, shared_act = mem["hT"], mem["shared_act"]
        sh_gate_up_w, sh_down_w = shared_weights(mem)
        gathered = [sem("gathered_even"), sem("gathered_odd")]
        going = sem("gather_going")
        turned, ev0, ev1 = sem("turned"), sem("turned_in_a"), sem("turned_in_b")
        gu, sil, mul, at, ate = sem("gate_up"), sem("silu"), sem("gated_act"), sem("act_turned"), sem("act_in")
        dn, ye0, ye1, cmm, addd = sem("down"), sem("y_in_a"), sem("y_in_b"), sem("combined"), sem("added")
        wg = k["moe_gate"][layer].rearrange("e (p c) f -> e p c f", p=P)
        wu = k["moe_up"][layer].rearrange("e (p c) f -> e p c f", p=P)
        wd = k["moe_down"][layer].rearrange("e (c p) d -> e p c d", p=P)
        gu_w = lambda s: gate_up_weights(mem, s)
        dn_w = lambda s: down_weights(mem, s)
        FULL = PAIRS - 4
        SHARED = DC // 2

        def in_loop(eng, body, first=1):
            with eng.Fori(0, (FULL + 1 - first) // 4) as i:
                for v in range(4):
                    body(i * 4 + (first + v), (first + v) % 4)

        with nc.Block(no_gpsimd_drain=True) as block:

            @block.sync
            def _(sp):
                def load(q, u):
                    sp.wait_ge(gu, q - 1)
                    load_gate_up(sp, k, mem, layer, q, u)
                    sp.wait_ge(dn, q - 1)
                    load_down(sp, k, mem, layer, q, u)

                with sp.Fori(0, FULL // 4) as i:
                    for v in range(4):
                        load(i * 4 + (2 + v), (2 + v) % 4)
                for q in range(PAIRS - 2, PAIRS):
                    load(q, q % 4)

            @block.gpsimd
            def _(pool):
                def gather(q, u):
                    pool.wait_ge(idx_ok, q + 1)
                    pool.sem_inc(going, 1)
                    pool.indirect_dma_start(
                        out=xg[:, u % 2, :], out_offset=None, in_=mem["rows_dram"],
                        in_offset=bass.IndirectOffsetOnAxis(ap=idx[:, u, :], axis=0)).then_inc(gathered[u % 2], 16)

                pool.wait_ge(mem["rows_stored"], 16 * 3 * (layer + 1))
                gather(0, 0)
                gather(1, 1)

                def next_gather(q, u):
                    pool.wait_ge(turned, q)
                    gather(q + 1, (u + 1) % 4)

                in_loop(pool, next_gather)
                for q in range(PAIRS - 3, PAIRS - 1):
                    next_gather(q, q % 4)

            @block.tensor
            def _(pe):
                def broadcast(q, u, first=False):
                    pe.wait_ge(selw_ok, q + 1)
                    if not first:
                        pe.wait_ge(ev0, q - (AHEAD - 2))
                        pe.wait_ge(ev1, q - (AHEAD - 2))
                    pe.matmul(t0b[:, 0:T], selw[:, u % 2, :], pg[:, 0, :], start=True, stop=True)
                    pe.matmul(t1b[:, 0:T], selw[:, u % 2, :], pg[:, 1, :], start=True, stop=True).then_inc(sel_mm, 1)

                def turn(q, u, known):
                    pe.wait_ge(gathered[u % 2], ((q - u % 2) // 2) * 16 + 16 if isinstance(q, int) else known[1])
                    pe.wait_ge(idf_ok, known[0])
                    pe.wait_ge(gate_in, known[0])
                    for c in range(DC):
                        mm = pe.transpose((t0b, t1b)[c // 4][:, (c % 4) * P:(c % 4 + 1) * P],
                                          xg[:, u % 2, c * P:(c + 1) * P], ident[:])
                        if c == DC - 1:
                            mm.then_inc(turned, 1)

                def gate_up(q, u, ready):
                    pe.wait_ge(gu_ready[u % 2], ready)
                    pe.wait_ge(ev0, q + 1)
                    pe.wait_ge(ev1, q + 1)
                    if not (isinstance(q, int) and q == 0):
                        pe.wait_ge(mul, q)
                    for c in range(DC):
                        for e in range(2):
                            mm = pe.matmul(gub[e * SLOTS:(e + 1) * SLOTS, :], xgT[:, u % 2, c, e * SLOTS:(e + 1) * SLOTS],
                                           gu_w(2 * (u % 2) + e)[:, c, :], start=(c == 0), stop=(c == DC - 1))
                    mm.then_inc(gu, 1)

                def combine(q, u):
                    pe.wait_ge(ye0, q + 1)
                    pe.wait_ge(ye1, q + 1)
                    for m in range(DC):
                        if m >= 4:
                            pe.wait_ge(addd, q * DC + (m - 2))
                        elif m == 0:
                            pe.wait_ge(addd, q * DC + 1)
                        pe.matmul(cb[m % 4][:, 0:T], ys[:, m * P:(m + 1) * P], sg[:, u, :],
                                  start=True, stop=True).then_inc(cmm, 1)

                def turn_act(q, u):
                    pe.wait_ge(mul, q + 1)
                    if not (isinstance(q, int) and q == 0):
                        pe.wait_ge(ate, q)
                    for f in range(FC):
                        mm = pe.transpose(atb[:, f * P:(f + 1) * P], ac[:, f * P:(f + 1) * P], ident[:])
                    mm.then_inc(at, 1)

                def down(q, u, ready):
                    pe.wait_ge(dn_ready[u % 2], ready)
                    pe.wait_ge(ate, q + 1)
                    if not (isinstance(q, int) and q == 0):
                        pe.wait_ge(addd, q * DC + 1)
                    for h, yb in enumerate((y0b, y1b)):
                        for f in range(FC):
                            for e in range(2):
                                mm = pe.matmul(yb[e * SLOTS:(e + 1) * SLOTS, :], aT[:, f, e * SLOTS:(e + 1) * SLOTS],
                                               dn_w(2 * (u % 2) + e)[:, f, h * BLOCK:(h + 1) * BLOCK],
                                               start=(f == 0), stop=(f == FC - 1))
                    mm.then_inc(dn, 1)

                def pair(q, u, half, tail=0):
                    nxt = half + 1 if u % 2 else half
                    gate_up(q, u, half * 64 + 64)
                    if tail < 3:
                        turn(q + 1, (u + 1) % 4, (q + AHEAD if tail == 0 else PAIRS, nxt * 16 + 16))
                    turn_act(q, u)
                    if not (isinstance(q, int) and q == 0):
                        combine(q - 1, (u + 3) % 4)
                    if tail == 0:
                        broadcast(q + AHEAD, (u + AHEAD) % 4)
                    down(q, u, half * 32 + 32)

                for q in range(AHEAD):
                    if q:
                        pe.wait_ge(idf_ok, q)
                        pe.wait_ge(gate_in, q)
                    broadcast(q, q, first=True)
                turn(0, 0, (AHEAD, 16))
                pair(0, 0, 0)
                for m in range(FC):
                    for c in range(DC):
                        mm = pe.matmul(cb[m][:, 0:T], sh_gate_up_w[:, c, FF + m * P:FF + (m + 1) * P],
                                       hT[:, c, :], start=(c == 0), stop=(c == DC - 1))
                    mm.then_inc(sh_up, 1)
                pe.wait_ge(mem["shared_down_ready"], 16 * (layer + 1))
                pe.wait_ge(sh_mul, FC)
                for q in range(1, SHARED + 1):
                    pair(q, q % 4, q // 2)
                    for m in (2 * q - 2, 2 * q - 1):
                        for c in range(FC):
                            mm = pe.matmul(cb[m % 2][:, 0:T], sh_down_w[:, c, m * P:(m + 1) * P], shared_act[:, c, :],
                                           start=(c == 0), stop=(c == FC - 1))
                        mm.then_inc(sh_dn, 1)
                    pe.wait_ge(sh_out, 2 * q)
                with pe.Fori(0, (FULL - SHARED) // 4) as i:
                    for v in range(4):
                        pair(i * 4 + (SHARED + 1 + v), (1 + v) % 4, i * 2 + (SHARED + 1 + v) // 2)
                for q in range(PAIRS - 3, PAIRS):
                    pair(q, q % 4, q // 2, tail=q - (PAIRS - 4))
                combine(PAIRS - 1, 3)

            @block.scalar
            def _(act):
                def gates(q, u):
                    act.wait_ge(sel_mm, q + 1)
                    if not (isinstance(q, int) and q == 0):
                        act.wait_ge(sg_ok, q)
                    act.copy(gsb[:], t1b[:, 0:T]).then_inc(gate_in, 1)

                def turned_in(q, u, early=False):
                    act.wait_ge(turned, q + 1)
                    if not early:
                        act.wait_ge(gu, q - 1)
                    act.copy(xgT[:, u % 2, 0:4, :], t0b[:].rearrange("p (c n) -> p c n", c=4)).then_inc(ev0, 1)

                def pair(q, u, tail=0, early=False):
                    act.wait_ge(gu, q + 1)
                    if not (isinstance(q, int) and q == 0):
                        act.wait_ge(mul, q)
                    act.activation(sl[:], gub[:, 0:FF], ACT.Silu).then_inc(sil, 1)
                    if tail < 3:
                        turned_in(q + 1, (u + 1) % 4, early)
                    act.wait_ge(at, q + 1)
                    if not (isinstance(q, int) and q == 0):
                        act.wait_ge(dn, q)
                    act.copy(aT[:], atb[:, 0:FF].rearrange("p (f n) -> p f n", f=FC)).then_inc(ate, 1)
                    if tail == 0:
                        gates(q + AHEAD, (u + AHEAD) % 4)
                    act.wait_ge(dn, q + 1)
                    act.copy(ys[:, 0:BLOCK], y0b[:]).then_inc(ye0, 1)

                for q in range(AHEAD):
                    gates(q, q)
                turned_in(0, 0, True)
                pair(0, 0, early=True)
                in_loop(act, pair)
                for q in range(PAIRS - 3, PAIRS):
                    pair(q, q % 4, tail=q - (PAIRS - 4))

            @block.vector
            def _(dve):
                def select(q, u, start=False):
                    if q_ge2(q):
                        dve.wait_ge(sel_mm, q - 1)
                    dve.tensor_scalar(selw[:, u % 2, :], basew[:], 0.0, None, ALU.is_equal).then_inc(selw_ok, 1)
                    dve.wait_ge(selw_ok, q + 1)
                    dve.tensor_scalar_add(basew[:], basew[:], -2.0).then_inc(based, 1)
                    dve.wait_ge(based, q + 2)

                def q_ge2(q):
                    return not isinstance(q, int) or q >= 2

                def places(q, u):
                    dve.wait_ge(gate_in, q + 1)
                    if not (isinstance(q, int) and q < 4):
                        dve.wait_ge(cmm, q * DC - 3 * DC)
                    dve.scalar_tensor_tensor(out=sg[:, u, :], in0=t0b[:, 0:T], scalar=slot_id[:, 0:1], in1=gsb[:],
                                             op0=ALU.is_equal, op1=ALU.mult).then_inc(sg_ok, 1)
                    if not (isinstance(q, int) and q == 0):
                        dve.wait_ge(idx_ok, q)
                    dve.scalar_tensor_tensor(out=hit[:], in0=t0b[:, 0:T], scalar=slot_id[:, 0:1], in1=tok[:],
                                             op0=ALU.is_equal, op1=ALU.mult, accum_out=idf[:]).then_inc(idf_ok, 1)
                    dve.wait_ge(idf_ok, q + 1)
                    if not (isinstance(q, int) and q < 4):
                        dve.wait_ge(gathered[u % 2], gather_count(q, u))
                    dve.tensor_copy(idx[:, u, :], idf[:]).then_inc(idx_ok, 1)

                def gather_count(q, u):
                    return (q - u % 2 - 2) * 8

                def turned_in(q, u, early=False):
                    dve.wait_ge(turned, q + 1)
                    if not early:
                        dve.wait_ge(gu, q - 1)
                    dve.tensor_copy(xgT[:, u % 2, 4:8, :], t1b[:].rearrange("p (c n) -> p c n", c=4)).then_inc(ev1, 1)

                def add_up(q):
                    for m in range(DC):
                        dve.wait_ge(cmm, q * DC + (m + 1))
                        if m == 0:
                            dve.wait_ge(addd, q * DC + 1)
                        dve.tensor_tensor(acc[:, m, :], acc[:, m, :], cb[m % 4][:, 0:T], ALU.add).then_inc(addd, 1)

                def pair(q, u, tail=0, early=False):
                    dve.wait_ge(sil, q + 1)
                    if not (isinstance(q, int) and q == 0):
                        dve.wait_ge(at, q)
                    dve.tensor_tensor(ac[:], sl[:], gub[:, FF:], ALU.mult).then_inc(mul, 1)
                    if tail < 3:
                        turned_in(q + 1, (u + 1) % 4, early)
                    if tail == 0:
                        select(q + AHEAD, (u + AHEAD) % 4)
                    if not (isinstance(q, int) and q == 0):
                        add_up(q - 1)
                    if tail == 0:
                        places(q + AHEAD, (u + AHEAD) % 4)
                    dve.wait_ge(dn, q + 1)
                    dve.tensor_copy(ys[:, BLOCK:], y1b[:]).then_inc(ye1, 1)

                dve.tensor_copy(basew[:], base[:]).then_inc(based, 1)
                dve.memset(hit[:, 0:1], 0.0).then_inc(addd, 1)
                dve.wait_ge(based, 1)
                for q in range(AHEAD):
                    select(q, q)
                    places(q, q)
                turned_in(0, 0, True)
                pair(0, 0, early=True)
                for m in range(FC):
                    dve.wait_ge(sh_up, m + 1)
                    dve.tensor_tensor(shared_act[:, m, :], shared_act[:, m, :], cb[m][:, 0:T],
                                      ALU.mult).then_inc(sh_mul, 1)
                for q in range(1, SHARED + 1):
                    pair(q, q % 4)
                    for m in (2 * q - 2, 2 * q - 1):
                        dve.wait_ge(sh_dn, m + 1)
                        dve.scalar_tensor_tensor(out=hT[:, m, :], in0=hT[:, m, :], scalar=ALPHA,
                                                 in1=cb[m % 2][:, 0:T], op0=ALU.mult, op1=ALU.add).then_inc(sh_out, 1)
                in_loop(dve, pair, first=SHARED + 1)
                for q in range(PAIRS - 3, PAIRS):
                    pair(q, q % 4, tail=q - (PAIRS - 4))
                add_up(PAIRS - 1)

        more_rounds(nc, k, mem, layer, dict(
            bank=bank, xg=xg, xgT=xgT, selw=selw, basew=basew, gsb=gsb, hit=hit, sg=sg, idf=idf, idx=idx, sl=sl, ac=ac,
            aT=aT, ys=ys, gu_w=gu_w, dn_w=dn_w, wg=wg, wu=wu, wd=wd))


def more_rounds(nc, k, mem, layer, buf):
    acc, ident, pg, base, slot_id, tok = (mem[n] for n in ("acc", "ident", "pg", "pair_base", "slot_id", "tok"))
    bank, xg, xgT, selw, basew, gsb, hit, sg, idf, idx, sl, ac, aT, ys, gu_w, dn_w = (buf[n] for n in (
        "bank", "xg", "xgT", "selw", "basew", "gsb", "hit", "sg", "idf", "idx", "sl", "ac", "aT", "ys", "gu_w", "dn_w"))
    t0b, t1b, gub, atb, y0b, y1b, c0b, c1b = bank
    wg, wu, wd = buf["wg"], buf["wu"], buf["wd"]
    with Signals(nc, f"m{layer}_") as sem:
        gu_ready, dn_ready, passed = sem("gate_up_ready"), sem("down_ready"), sem("passed")
        round_set, picked, rows_bc, gate_in, placed, indexed, going, gathered = (sem(n) for n in (
            "round_set", "picked", "rows_broadcast", "gates_in", "placed", "indexed", "gather_going", "gathered"))
        turned, in_a, in_b, gu, silu, mul, at, ate = (sem(n) for n in (
            "turned", "turned_in_a", "turned_in_b", "gate_up", "silu", "gated", "act_turned", "act_in"))
        dn, y_a, y_b, combined, added = (sem(n) for n in ("down", "y_in_a", "y_in_b", "combined", "added"))

        def over_items(eng, item, new_round=None):
            longest = eng.value_load(mem["count"][0:1, 0:1], min_val=0, max_val=T)
            with eng.If(longest > SLOTS):
                with eng.Fori(1, (longest + (SLOTS - 1)) // SLOTS) as r:
                    if new_round:
                        new_round(r)
                    with eng.Fori(0, PAIRS) as p:
                        n = r * PAIRS + p - (PAIRS - 1)
                        item(p, n)
                        eng.wait_ge(added, n * DC)
                        eng.sem_inc(passed, 1)

        with nc.Block(no_gpsimd_drain=True) as block:

            @block.sync
            def _(sp):
                def item(p, n):
                    for e in range(2):
                        w = gu_w(e)
                        sp.dma_start(w[:, :, 0:FF], wg[p * 2 + e]).then_inc(gu_ready, 16)
                        sp.dma_start(w[:, :, FF:], wu[p * 2 + e]).then_inc(gu_ready, 16)
                        sp.dma_start(dn_w(e), wd[p * 2 + e]).then_inc(dn_ready, 16)

                over_items(sp, item)

            @block.gpsimd
            def _(pool):
                def item(p, n):
                    pool.wait_ge(indexed, n)
                    pool.sem_inc(going, 1)
                    pool.indirect_dma_start(
                        out=xg[:, 0, :], out_offset=None, in_=mem["rows_dram"],
                        in_offset=bass.IndirectOffsetOnAxis(ap=idx[:, 0, :], axis=0)).then_inc(gathered, 16)

                over_items(pool, item)

            @block.tensor
            def _(pe):
                def item(p, n):
                    pe.wait_ge(picked, n)
                    pe.matmul(t0b[:, 0:T], selw[:, 0, :], pg[:, 0, :], start=True, stop=True)
                    pe.matmul(t1b[:, 0:T], selw[:, 0, :], pg[:, 1, :], start=True, stop=True).then_inc(rows_bc, 1)
                    pe.wait_ge(indexed, n)
                    pe.wait_ge(gathered, n * 16)
                    for c in range(DC):
                        mm = pe.transpose((t0b, t1b)[c // 4][:, (c % 4) * P:(c % 4 + 1) * P],
                                          xg[:, 0, c * P:(c + 1) * P], ident[:])
                    mm.then_inc(turned, 1)
                    pe.wait_ge(in_a, n)
                    pe.wait_ge(in_b, n)
                    pe.wait_ge(gu_ready, n * 64)
                    for c in range(DC):
                        for e in range(2):
                            half = slice(e * SLOTS, (e + 1) * SLOTS)
                            mm = pe.matmul(gub[half, :], xgT[:, 0, c, half], gu_w(e)[:, c, :],
                                           start=(c == 0), stop=(c == DC - 1))
                    mm.then_inc(gu, 1)
                    pe.wait_ge(mul, n)
                    for f in range(FC):
                        mm = pe.transpose(atb[:, f * P:(f + 1) * P], ac[:, f * P:(f + 1) * P], ident[:])
                    mm.then_inc(at, 1)
                    pe.wait_ge(ate, n)
                    pe.wait_ge(dn_ready, n * 32)
                    for h, yb in enumerate((y0b, y1b)):
                        for f in range(FC):
                            for e in range(2):
                                half = slice(e * SLOTS, (e + 1) * SLOTS)
                                mm = pe.matmul(yb[half, :], aT[:, f, half], dn_w(e)[:, f, h * BLOCK:(h + 1) * BLOCK],
                                               start=(f == 0), stop=(f == FC - 1))
                    mm.then_inc(dn, 1)
                    pe.wait_ge(y_a, n)
                    pe.wait_ge(y_b, n)
                    for m in range(DC):
                        if m >= 2:
                            pe.wait_ge(added, n * DC - DC + m - 1)
                        pe.matmul((c0b, c1b)[m % 2][:, 0:T], ys[:, m * P:(m + 1) * P], sg[:, 0, :],
                                  start=True, stop=True).then_inc(combined, 1)

                over_items(pe, item)

            @block.scalar
            def _(act):
                def item(p, n):
                    act.wait_ge(rows_bc, n)
                    act.copy(gsb[:], t1b[:, 0:T]).then_inc(gate_in, 1)
                    act.wait_ge(turned, n)
                    act.copy(xgT[:, 0, 0:4, :], t0b[:].rearrange("p (c n) -> p c n", c=4)).then_inc(in_a, 1)
                    act.wait_ge(gu, n)
                    act.activation(sl[:], gub[:, 0:FF], ACT.Silu).then_inc(silu, 1)
                    act.wait_ge(at, n)
                    act.copy(aT[:], atb[:, 0:FF].rearrange("p (f n) -> p f n", f=FC)).then_inc(ate, 1)
                    act.wait_ge(dn, n)
                    act.copy(ys[:, 0:BLOCK], y0b[:]).then_inc(y_a, 1)

                over_items(act, item)

            @block.vector
            def _(dve):
                def new_round(r):
                    dve.tensor_scalar_add(pg[:, 0, :], pg[:, 0, :], -float(SLOTS)).then_inc(round_set, 1)
                    dve.tensor_copy(basew[:], base[:]).then_inc(round_set, 1)
                    dve.wait_ge(round_set, r * 2)
                    dve.sem_inc(passed, 1)

                def item(p, n):
                    dve.tensor_scalar(selw[:, 0, :], basew[:], 0.0, None, ALU.is_equal).then_inc(picked, 1)
                    dve.wait_ge(gate_in, n)
                    dve.tensor_scalar_add(basew[:], basew[:], -2.0).then_inc(placed, 1)
                    dve.scalar_tensor_tensor(out=sg[:, 0, :], in0=t0b[:, 0:T], scalar=slot_id[:, 0:1], in1=gsb[:],
                                             op0=ALU.is_equal, op1=ALU.mult).then_inc(placed, 1)
                    dve.scalar_tensor_tensor(out=hit[:], in0=t0b[:, 0:T], scalar=slot_id[:, 0:1], in1=tok[:],
                                             op0=ALU.is_equal, op1=ALU.mult, accum_out=idf[:]).then_inc(placed, 1)
                    dve.wait_ge(placed, n * 3)
                    dve.tensor_copy(idx[:, 0, :], idf[:]).then_inc(indexed, 1)
                    dve.wait_ge(turned, n)
                    dve.tensor_copy(xgT[:, 0, 4:8, :], t1b[:].rearrange("p (c n) -> p c n", c=4)).then_inc(in_b, 1)
                    dve.wait_ge(silu, n)
                    dve.tensor_tensor(ac[:], sl[:], gub[:, FF:], ALU.mult).then_inc(mul, 1)
                    dve.wait_ge(dn, n)
                    dve.tensor_copy(ys[:, BLOCK:], y1b[:]).then_inc(y_b, 1)
                    for m in range(DC):
                        dve.wait_ge(combined, n * DC - DC + m + 1)
                        dve.tensor_tensor(acc[:, m, :], acc[:, m, :], (c0b, c1b)[m % 2][:, 0:T],
                                          ALU.add).then_inc(added, 1)

                over_items(dve, item, new_round)


def write_out(nc, k, mem, out):
    hT, ident = mem["hT"], mem["ident"]
    with ExitStack() as inner:
        sem = lambda name: inner.enter_context(nc.semaphore(name))
        bank = [inner.enter_context(nc.psum_tensor(f"wo{b}", [P, BLOCK], F32)) for b in range(4)]
        rows = inner.enter_context(nc.sbuf_tensor("out_rows", [P, 4, BLOCK], F32))
        turned, copied, stored = sem("out_turned"), sem("out_copied"), sem("out_stored")
        with nc.Block() as block:

            @block.tensor
            def _(pe):
                for i in range(4):
                    t0 = META + (i // 2) * P
                    for c in range(4):
                        mm = pe.transpose(bank[i][:, c * P:(c + 1) * P], hT[:, 4 * (i % 2) + c, t0:t0 + P], ident[:])
                    mm.then_inc(turned, 1)

            @block.vector
            def _(dve):
                for i in range(4):
                    dve.wait_ge(turned, i + 1)
                    dve.tensor_copy(rows[:, i, :], bank[i][:]).then_inc(copied, 1)

            @block.sync
            def _(sp):
                for i in range(4):
                    sp.wait_ge(copied, i + 1)
                    sp.dma_start(out[0, (i // 2) * P:(i // 2 + 1) * P, (i % 2) * BLOCK:(i % 2 + 1) * BLOCK],
                                 rows[:, i, :]).then_inc(stored, 16)
                sp.wait_ge(stored, 64)


def s5_discretise(dve, link, act_sem, phase_sem, mem):
    par, lam, ki = mem["s5_par"], mem["s5_lam"], mem["s5_int"]
    C1, C2 = 6.28125, 1.9350051879882812e-03
    C3 = 2.0 * math.pi - C1 - C2
    lr, li = lam[:, 0, :], lam[:, 1, :]
    dt, th, ku, r, cs, s_, h2, abr, abi, den, nr, q1, q2 = (par[:, i, :] for i in range(13))
    mag, cfr, cfi = (mem["s5_coef"][:, i, :] for i in range(3))
    link(dve.tensor_scalar(lr, lr, -1e-4, None, ALU.min))
    dve.wait_ge(act_sem, 1)
    link(dve.tensor_tensor(th, li, dt, ALU.mult))
    dve.tensor_tensor(mag, lr, dt, ALU.mult).then_inc(phase_sem, 1)
    link(dve.tensor_scalar(ku, th, 1.0 / (2.0 * math.pi), None, ALU.mult))
    link(dve.tensor_copy(ki[:], ku))
    link(dve.tensor_copy(ku, ki[:]))
    link(dve.scalar_tensor_tensor(out=r, in0=ku, scalar=-C1, in1=th, op0=ALU.mult, op1=ALU.add))
    link(dve.scalar_tensor_tensor(out=r, in0=ku, scalar=-C2, in1=r, op0=ALU.mult, op1=ALU.add))
    link(dve.scalar_tensor_tensor(out=r, in0=ku, scalar=-C3, in1=r, op0=ALU.mult, op1=ALU.add))
    dve.tensor_scalar(r, r, 3.1415925, -3.1415925, ALU.min, ALU.max).then_inc(phase_sem, 1)
    dve.wait_ge(act_sem, 4)
    link(dve.tensor_tensor(cs, h2, h2, ALU.mult))
    dve.tensor_scalar(cs, cs, -2.0, 1.0, ALU.mult, ALU.add).then_inc(phase_sem, 1)
    dve.wait_ge(phase_sem, 3)
    link(dve.tensor_tensor(abr, mag, cs, ALU.mult))
    link(dve.tensor_tensor(abi, mag, s_, ALU.mult))
    link(dve.tensor_tensor(den, lr, lr, ALU.mult))
    link(dve.tensor_tensor(q1, li, li, ALU.mult))
    link(dve.tensor_tensor(den, den, q1, ALU.add))
    link(dve.reciprocal(den, den))
    link(dve.tensor_scalar_add(nr, abr, -1.0))
    link(dve.tensor_tensor(q1, nr, lr, ALU.mult))
    link(dve.tensor_tensor(q2, abi, li, ALU.mult))
    link(dve.tensor_tensor(q1, q1, q2, ALU.add))
    link(dve.tensor_tensor(cfr, q1, den, ALU.mult))
    link(dve.tensor_tensor(q1, abi, lr, ALU.mult))
    link(dve.tensor_tensor(q2, nr, li, ALU.mult))
    link(dve.tensor_tensor(q1, q1, q2, ALU.subtract))
    link(dve.tensor_tensor(cfi, q1, den, ALU.mult))
    link(dve.tensor_scalar(mem["s5_coef"][:, 3, :], cfi, -1.0, None, ALU.mult))


def s5_sines(act, act_sem, phase_sem, mem):
    par = mem["s5_par"]
    act.activation(par[:, 0, :], mem["s5_lam"][:, 2, :], ACT.Exp).then_inc(act_sem, 1)
    act.wait_ge(phase_sem, 1)
    mag = mem["s5_coef"][:, 0, :]
    act.activation(mag, mag, ACT.Exp).then_inc(act_sem, 1)
    act.wait_ge(phase_sem, 2)
    act.activation(par[:, 5, :], par[:, 3, :], ACT.Sin).then_inc(act_sem, 1)
    act.activation(par[:, 6, :], par[:, 3, :], ACT.Sin, scale=0.5).then_inc(act_sem, 1)


def s5_tables(pool, link, mem, slice_done):
    J, par, table, a_full = S5_TILES, mem["s5_par"], mem["s5_table"], mem["s5_scratch"]
    q1, q2 = par[:, 13, :], par[:, 14, :]
    cosT, sinT = table[:, :, 0, :], table[:, :, 1, :]
    link(pool.memset(cosT[:, :, 0:1], 1.0))
    link(pool.memset(sinT[:, :, 0:1], 0.0))
    link(pool.tensor_copy(cosT[:, :, 1], par[:, 4, :]))
    link(pool.tensor_copy(sinT[:, :, 1], par[:, 5, :]))
    levels = []
    m = 1
    while 2 * m < T:
        cm, sm = cosT[:, :, m], sinT[:, :, m]
        link(pool.tensor_tensor(q1, cm, cm, ALU.mult))
        link(pool.tensor_tensor(q2, sm, sm, ALU.mult))
        link(pool.tensor_tensor(cosT[:, :, 2 * m], q1, q2, ALU.subtract))
        link(pool.tensor_tensor(q1, cm, sm, ALU.mult))
        link(pool.tensor_tensor(sinT[:, :, 2 * m], q1, q1, ALU.add))
        m *= 2
        levels.append((m, min(m, T - m) - 1))
        if m < 64:
            double(pool, link, table, a_full, slice(0, J), *levels.pop())
    for j0 in range(0, J, S5_SLICE):
        for m, n in levels:
            ins = double(pool, link, table, a_full, slice(j0, j0 + S5_SLICE), m, n, last=(m, n) == levels[-1])
        ins.then_inc(slice_done, 1)
        pool.wait_ge(slice_done, j0 // S5_SLICE + 1)


def double(pool, link, table, scratch, js, m, n, last=False):
    k = js.stop - js.start
    ca, sa = (table[:, js, q, m].unsqueeze(2).broadcast_to([P, k, n]) for q in range(2))
    ci, si = (table[:, js, q, 1:1 + n] for q in range(2))
    co, so = (table[:, js, q, m + 1:m + 1 + n] for q in range(2))
    a = scratch[:, 0:k * n].rearrange("p (j n) -> p j n", j=k)
    link(pool.tensor_tensor(a, si, sa, ALU.mult))
    link(pool.tensor_tensor(co, ci, ca, ALU.mult))
    link(pool.tensor_tensor(co, co, a, ALU.subtract))
    link(pool.tensor_tensor(a, ci, sa, ALU.mult))
    link(pool.tensor_tensor(so, si, ca, ALU.mult))
    ins = pool.tensor_tensor(so, so, a, ALU.add)
    if not last:
        link(ins)
    return ins


def s5_buffers(ctx, nc, mem):
    sb = lambda name, shape: ctx.enter_context(nc.sbuf_tensor(f"s5_{name}", shape, F32))
    J = S5_TILES
    mem["s5"] = {n: sb(n, [P, J, 32]) for n in ("c_re", "c_im", "w_re", "w_nre", "w_nim")}
    mem["s5"] |= {"b_re": sb("b_re", [P, DC, P]), "b_im": sb("b_im", [P, DC, P]), "turns": sb("turns", [P, J, 2, T])}
    mem["s5"] |= {n: ctx.enter_context(nc.semaphore(f"s5_{n}")) for n in ("b_loaded", "c_loaded", "c_weighted")}
    mem["s5"]["tables"] = [ctx.enter_context(nc.semaphore(f"s5_table{i}_loaded")) for i in range(J // S5_SLICE)]


def load_s5(sp, k, mem):
    s5 = mem["s5"]
    for name in ("c_re", "c_im"):
        sp.dma_start(s5[name][:], k[f"s5_{name}"]).then_inc(s5["c_loaded"], 16)
    for name in ("b_re", "b_im"):
        sp.dma_start(s5[name][:], k[f"s5_{name}"]).then_inc(s5["b_loaded"], 16)
    sp.dma_start(mem["s5_d"][:], k["s5_d"]).then_inc(s5["b_loaded"], 16)
    sp.wait_ge(mem["tables_stored"], 16 * (S5_TILES // S5_SLICE))
    for i, loaded in enumerate(s5["tables"]):
        js = slice(i * S5_SLICE, (i + 1) * S5_SLICE)
        sp.dma_start(s5["turns"][:, js], k["s5_table_dram"][:, js]).then_inc(loaded, 16)


def weight_s5_outputs(pool, mem):
    s5 = mem["s5"]
    c_re, c_im, w_re, w_nre, w_nim = (s5[n][:] for n in ("c_re", "c_im", "w_re", "w_nre", "w_nim"))
    cfr, cfi, ncfi = (mem["s5_coef"][:, i, :].unsqueeze(2).broadcast_to([P, S5_TILES, 32]) for i in (1, 2, 3))
    link = Chain(pool, s5["c_weighted"]).done
    pool.wait_ge(s5["c_loaded"], 32)
    link(pool.tensor_tensor(w_nim, c_re, cfr, ALU.mult))
    link(pool.tensor_tensor(w_nre, c_im, cfi, ALU.mult))
    link(pool.tensor_tensor(w_re, w_nim, w_nre, ALU.subtract))
    link(pool.tensor_tensor(w_nre, w_nre, w_nim, ALU.subtract))
    link(pool.tensor_tensor(w_nim, c_re, ncfi, ALU.mult))
    link(pool.tensor_tensor(c_im, c_im, cfr, ALU.mult))
    link(pool.tensor_tensor(w_nim, w_nim, c_im, ALU.subtract))


def s5_mixer(nc, k, mem, ex, buffers):
    hT, ring = mem["hT"], mem["dense"]
    J = S5_TILES
    with ExitStack() as outer:
        yT = mem["acc"]
        glu = outer.enter_context(Signals(nc, "glu_"))
        w_ready = [glu("w_even"), glu("w_odd")]
        w_out = k["s5_w_out"].rearrange("(c p) n -> p c n", p=P)
        with ExitStack() as inner:
            sem = inner.enter_context(Signals(nc, "s5_"))
            sb = lambda name, shape, dt=F32: inner.enter_context(nc.sbuf_tensor(f"s5_{name}", shape, dt))
            bank = [inner.enter_context(nc.psum_tensor(f"s5_b{b}", [P, BLOCK], F32)) for b in range(8)]
            s5 = mem["s5"]
            table, w_re, w_nre, w_nim, b_re, b_im = (s5[n] for n in ("turns", "w_re", "w_nre", "w_nim", "b_re", "b_im"))
            b_loaded, tables, weighted = s5["b_loaded"], s5["tables"], s5["c_weighted"]
            mag = mem["s5_coef"][:, 0, :]
            R = 3
            in_bank = bank[0:4] + bank[6:8]
            b_sb = sb("b_sb", [P, R, 3, T])
            z = sb("z", [P, R, 2, T])
            by_cos, by_sin = sb("in_by_cos", [P, R, 2, T]), sb("in_by_sin", [P, R, 2, T])
            z_cos, z_sin = sb("z_by_cos", [P, R, 2, T]), sb("z_by_sin", [P, R, 2, T])
            bu, cp, cos_in, sin_in, turned = sem("bu"), sem("bu_in"), sem("in_by_cos"), sem("in_by_sin"), sem("turned")
            scanned, cos_out, sin_out, yy, fin, gel = (sem("scanned"), sem("z_by_cos"), sem("z_by_sin"), sem("y"),
                                                       sem("y_skip"), sem("gelu"))
            both = lambda x: x.unsqueeze(1).broadcast_to([P, 2, T])
            with nc.Block(no_gpsimd_drain=True) as block:

                @block.sync
                def _(sp):
                    for b in range(2):
                        sp.dma_start(ring[:, b], w_out[:, :, b * BLOCK:(b + 1) * BLOCK]).then_inc(w_ready[b], 16)

                @block.tensor
                def _(pe):
                    pe.wait_ge(b_loaded, 48)

                    def inputs(j):
                        a, b = j // 4, j % 4
                        rows = slice(32 * b, 32 * b + 32)
                        if j >= R:
                            pe.wait_ge(cp, 3 * (j - (R - 1)))
                        for q, w in enumerate((b_re, b_im)):
                            pe.matmul(in_bank[2 * (j % R) + q][:, 0:T], w[rows, a, :], hT[rows, a, :],
                                      start=True, stop=True).then_inc(bu, 1)

                    def outputs(j):
                        a, b = j // 4, j % 4
                        if b == 0 and a >= 2:
                            pe.wait_ge(fin, a - 1)
                        pe.wait_ge(cos_out, j + 1)
                        pe.wait_ge(sin_out, j + 1)
                        for q, (w, zz) in enumerate(((w_re, z_cos[:, j % R, 0]), (w_nim, z_cos[:, j % R, 1]),
                                                     (w_nim, z_sin[:, j % R, 0]), (w_nre, z_sin[:, j % R, 1]))):
                            mm = pe.matmul(bank[4 + a % 2][32 * b:32 * b + 32, 0:T], w[:, j, :], zz,
                                           start=(q == 0), stop=(q == 3))
                        mm.then_inc(yy, 1)

                    for j in range(J + R):
                        if j < J:
                            inputs(j)
                        if j == R:
                            pe.wait_ge(weighted, 7)
                        if j >= R:
                            outputs(j - R)

                @block.scalar
                def _(act):
                    for j in range(J):
                        for q, (bk, scale) in enumerate(((0, 1.0), (1, 1.0), (0, -1.0))):
                            act.wait_ge(bu, 2 * j + bk + 1)
                            if j >= R:
                                act.wait_ge(cos_in, j - (R - 1))
                                act.wait_ge(sin_in, j - (R - 1))
                            act.activation(b_sb[:, j % R, q, :], in_bank[2 * (j % R) + bk][:, 0:T], ACT.Copy,
                                           scale=scale).then_inc(cp, 1)
                    for a in range(DC):
                        act.wait_ge(fin, a + 1)
                        act.activation(yT[:, a, :], yT[:, a, :], ACT.Gelu_apprx_tanh).then_inc(gel, 1)

                @block.gpsimd
                def _(pool):
                    def forward(j):
                        if j % S5_SLICE == 0:
                            pool.wait_ge(tables[j // S5_SLICE], 16)
                        pool.wait_ge(cp, 3 * j + 3)
                        if j >= R:
                            pool.wait_ge(turned, j - (R - 1))
                        pool.tensor_tensor(by_sin[:, j % R], b_sb[:, j % R, 1:3, :], both(table[:, j, 1, :]),
                                           ALU.mult).then_inc(sin_in, 1)

                    def back(j):
                        pool.wait_ge(scanned, 2 * j + 2)
                        if j >= R:
                            pool.wait_ge(yy, j - (R - 1))
                        pool.tensor_tensor(z_sin[:, j % R], z[:, j % R], both(table[:, j, 1, :]),
                                           ALU.mult).then_inc(sin_out, 1)

                    for j in range(J + 1):
                        if j < J:
                            forward(j)
                        if j >= 1:
                            back(j - 1)

                @block.vector
                def _(dve):
                    dve.wait_ge(b_loaded, 48)

                    def forward(j):
                        if j % S5_SLICE == 0:
                            dve.wait_ge(tables[j // S5_SLICE], 16)
                        dve.wait_ge(cp, 3 * j + 3)
                        dve.tensor_tensor(by_cos[:, j % R], b_sb[:, j % R, 0:2, :], both(table[:, j, 0, :]),
                                          ALU.mult).then_inc(cos_in, 1)

                    def scans(j):
                        dve.wait_ge(cos_in, j + 1)
                        dve.wait_ge(sin_in, j + 1)
                        dve.tensor_tensor(by_cos[:, j % R], by_cos[:, j % R], by_sin[:, j % R],
                                          ALU.add).then_inc(turned, 1)
                        dve.wait_ge(turned, j + 1)
                        if j >= R:
                            dve.wait_ge(cos_out, j - (R - 1))
                            dve.wait_ge(sin_out, j - (R - 1))
                        rho = mag[:, j:j + 1].broadcast_to([P, T])
                        for q in range(2):
                            dve.tensor_tensor_scan(z[:, j % R, q, :], rho, by_cos[:, j % R, q, :], 0.0, ALU.mult,
                                                   ALU.add).then_inc(scanned, 1)

                    def back(j):
                        dve.wait_ge(scanned, 2 * j + 2)
                        if j >= R:
                            dve.wait_ge(yy, j - (R - 1))
                        dve.tensor_tensor(z_cos[:, j % R], z[:, j % R], both(table[:, j, 0, :]),
                                          ALU.mult).then_inc(cos_out, 1)

                    def skip(a):
                        dve.wait_ge(yy, 4 * (a + 1))
                        dve.scalar_tensor_tensor(out=yT[:, a, :], in0=hT[:, a, :], scalar=mem["s5_d"][:, a:a + 1],
                                                 in1=bank[4 + a % 2][:, 0:T], op0=ALU.mult, op1=ALU.add).then_inc(fin, 1)

                    forward(0)
                    for j in range(J + 1):
                        if j >= 1:
                            back(j - 1)
                        if j < J:
                            scans(j)
                            if j + 1 < J:
                                forward(j + 1)
                        if j >= 5 and j % 4 == 1:
                            skip(j // 4 - 1)
                    skip(DC - 1)

        buffers.close()
        with ExitStack() as inner:
            sem = glu
            mem["experts"] = ex.enter_context(nc.sbuf_tensor("experts1", [P, 4, 3 * D * FF // P], F32))
            ps = [inner.enter_context(nc.psum_tensor(f"glu{b}", [P, BLOCK], F32)) for b in range(4)]
            val = inner.enter_context(nc.sbuf_tensor("glu_val", [P, DC, T], F32))
            sig = inner.enter_context(nc.sbuf_tensor("glu_sig", [P, 2, T], F32))
            ready, w = w_ready, w_out
            proj, taken, mul, added = sem("proj"), sem("taken"), sem("mul"), sem("added")
            with nc.Block(no_gpsimd_drain=True) as block:

                @block.sync
                def _(sp):
                    for b in range(2, 4):
                        sp.wait_ge(proj, 4 * (b - 1))
                        sp.dma_start(ring[:, b % 2], w[:, :, b * BLOCK:(b + 1) * BLOCK]).then_inc(ready[b % 2], 16)
                    load_first_experts(sp, k, mem, 1)

                @block.tensor
                def _(pe):
                    for m in range(2 * DC):
                        b = m // 4
                        if m % 4 == 0:
                            pe.wait_ge(ready[b % 2], 16 * (b // 2 + 1))
                        if m >= 4:
                            pe.wait_ge(taken, m - 3)
                        for c in range(DC):
                            mm = pe.matmul(ps[m % 4][:, 0:T], ring[:, b % 2, c, (m % 4) * P:(m % 4 + 1) * P],
                                           yT[:, c, :], start=(c == 0), stop=(c == DC - 1))
                        mm.then_inc(proj, 1)

                @block.scalar
                def _(act):
                    for m in range(2 * DC):
                        act.wait_ge(proj, m + 1)
                        if m < DC:
                            act.copy(val[:, m, :], ps[m % 4][:, 0:T]).then_inc(taken, 1)
                        else:
                            if m >= DC + 2:
                                act.wait_ge(mul, m - DC - 1)
                            act.activation(sig[:, m % 2, :], ps[m % 4][:, 0:T], ACT.Sigmoid).then_inc(taken, 1)

                @block.vector
                def _(dve):
                    for m in range(DC):
                        dve.wait_ge(taken, DC + m + 1)
                        dve.tensor_tensor(val[:, m, :], val[:, m, :], sig[:, m % 2, :], ALU.mult).then_inc(mul, 1)
                        dve.wait_ge(mul, m + 1)
                        dve.scalar_tensor_tensor(out=hT[:, m, :], in0=hT[:, m, :], scalar=ALPHA, in1=val[:, m, :],
                                                 op0=ALU.mult, op1=ALU.add).then_inc(added, 1)


def trunk(nc, k, out, phases=4):
    with ExitStack() as ctx:
        sb = lambda name, shape, dt=F32: ctx.enter_context(nc.sbuf_tensor(name, shape, dt))
        sem = lambda name: ctx.enter_context(nc.semaphore(name))
        mem = {
            "hT": sb("hT", [P, DC, T]), "dense": sb("dense_ring", [P, 2, DC, BLOCK]),
            "ident": sb("ident", [P, P]), "ones": sb("ones", [P, P]), "eps": sb("eps", [P, 3]),
            "ln_par": sb("ln_par", [P, 8 * DC]), "s5_d": sb("s5_d", [P, DC]),
            "pair_base": sb("pair_base", [E, P]), "slot_id": sb("slot_id", [P, 1]), "tok": sb("tok", [P, T]),
            "count": sb("count", [1, 1], I32), "s5_coef": sb("s5_coef", [P, 4, S5_TILES]),
            "consts_loaded": sem("consts_loaded"), "rows_stored": sem("rows_stored"), "count_ready": sem("count_ready"),
            "router_loaded": sem("router_loaded"), "shared_gate_up_ready": sem("shared_gate_up_ready"),
            "shared_down_ready": sem("shared_down_ready"),
            "tables_stored": sem("tables_stored"), "rows_dram": k["rows_dram"],
            "gate_up_ready": [[sem(f"gate_up{la}_{half}_ready") for half in "ab"] for la in range(DEPTH)],
            "down_ready": [[sem(f"down{la}_{half}_ready") for half in "ab"] for la in range(DEPTH)],
        }
        ones_set, consts2 = sem("ones_set"), sem("expert_consts_loaded")
        with nc.Block(no_gpsimd_drain=True) as block:

            @block.vector
            def _(dve):
                dve.memset(mem["ones"][:], 1.0).then_inc(ones_set, 1)

            @block.sync
            def _(sp):
                for name in ("pair_base", "slot_id", "tok"):
                    sp.dma_start(mem[name][:], k[name]).then_inc(consts2, 16)

        with ExitStack() as mix:
            msb = lambda name, shape, dt=F32: mix.enter_context(nc.sbuf_tensor(name, shape, dt))
            mem |= {
                "qkv": msb("qkv", [P, 24, T]), "xa": msb("xa", [P, DC, T]), "y": msb("y", [P, 2 * DC, T]),
                "bd": msb("bd", [HEADS, 2, T]), "conv_w": msb("conv_w", [P, 32, CONV]), "conv_b": msb("conv_b", [P, DC]),
                "w_bd": msb("w_bd", [P, DC, DECAY_ROW + HEADS]), "offmask": msb("offmask", [P, LEVELS, P]),
                "causal": msb("causal", [P, P]), "sel8": msb("sel8", [HEADS, HEADS, P]), "lru_b": msb("lru_b", [P, 16]),
                "lru_lam": msb("lru_lam", [P, DC]), "head_par": msb("head_par", [HEADS, 2]),
                "norm_w": msb("norm_w", [P, 1]), "beta_G": msb("beta_G", [HEADS, 2, T]), "c8": msb("c8", [P, DC]),
                "lru_w_ready": mix.enter_context(nc.semaphore("lru_w_ready")),
            }
            in_projection(nc, k, mix, mem)
            with nc.Block(no_gpsimd_drain=True) as block:
                for start in (block.tensor, block.scalar, block.vector, block.gpsimd):

                    @start
                    def _(eng):
                        eng.wait_ge(mem["consts_loaded"], 16 * 10)

            group_mixers(nc, k, mix, mem)
        mem |= {
            "acc": sb("acc", [P, DC, T]), "pg": sb("places_gates", [E, 2, T]),
            "router_w": sb("router_w", [P, DC, E]), "router_b": sb("router_b", [P, E]),
            "after": sb("after", [P, 3, T]), "lower": sb("lower", [P, GROUPS, GROUPS]),
            "shared_act": sb("shared_act", [P, FC, T]),
        }
        ex = ctx.enter_context(ExitStack())
        mem["experts"] = ex.enter_context(nc.sbuf_tensor("experts0", [P, 4, 3 * D * FF // P], F32))

        def load_moe0(sp):
            load_router(sp, k, mem, 0)
            load_first_experts(sp, k, mem, 0)

        layer_norm(nc, k, mem, 0, "hT", loads=load_moe0)
        with nc.Block(no_gpsimd_drain=True) as block:
            for start in (block.tensor, block.vector):

                @start
                def _(eng):
                    eng.wait_ge(consts2, 48)

        def moe(layer, **preparing):
            router_and_shared(nc, k, mem, layer)
            experts(nc, k, mem, layer)
            ex.close()
            if layer == 0:
                s5_buffers(buffers, nc, mem)
            layer_norm(nc, k, mem, 2 * layer + 1, "acc", **preparing)

        buffers = ctx.enter_context(ExitStack())
        if phases >= 2:
            moe(0, loads=lambda sp: load_s5(sp, k, mem), pool_work=lambda pool: weight_s5_outputs(pool, mem))
        if phases >= 3:
            s5_mixer(nc, k, mem, ex, buffers)
            layer_norm(nc, k, mem, 2, "hT", loads=lambda sp: load_router(sp, k, mem, 1))
        if phases >= 4:
            moe(1)
        write_out(nc, k, mem, out)


def constants():
    i = np.arange(P)
    f = np.float32
    offmask = np.zeros((P, LEVELS, P), f)
    for lv in range(LEVELS):
        b = 2 ** lv
        same = i[:, None] // (2 * b) == i[None, :] // (2 * b)
        offmask[:, lv, :] = same & (i[:, None] // b % 2 == 0) & (i[None, :] // b % 2 == 1)
    sel8 = np.zeros((HEADS, HEADS, P), f)
    for h in range(HEADS):
        sel8[h, h, :] = 1.0
    t = np.arange(T)
    tile_tok = i[:, None] + P * np.arange(3)[None, :]
    return {
        "ident": np.eye(P, dtype=f), "offmask": offmask,
        "causal": (i[None, :] >= i[:, None]).astype(f), "sel8": sel8,
        "eps": np.tile(np.array([[NORM_EPS, NORM_EPS * P, LN_EPS]], f), (P, 1)),
        "after": (t[None, None, :] > tile_tok[:, :, None]).astype(f),
        "lower": np.broadcast_to(np.tril(np.ones((GROUPS, GROUPS), f), -1), (P, GROUPS, GROUPS)).copy(),
        "pair_base": (np.arange(E)[:, None] - (i[None, :] >= SLOTS)).astype(f),
        "slot_id": (i % SLOTS).astype(f)[:, None],
        "tok": np.tile(t.astype(f)[None, :], (P, 1)),
    }


def layout(a):
    tile = lambda v: np.ascontiguousarray(np.asarray(v).reshape(-1, P).T)
    a = {n: np.asarray(v) for n, v in a.items()}
    r = {}
    h0 = np.concatenate([a["meta_tokens"], a["x"][0]], axis=0)
    r["h0T"] = h0.T.reshape(DC, P, T).transpose(1, 0, 2)
    r["w_in"] = a["ab_w_in"][0]
    bd = np.zeros((D, DECAY_ROW + HEADS), r["w_in"].dtype)
    bd[:, 0:HEADS], bd[:, DECAY_ROW:] = r["w_in"][:, 6 * D:6 * D + HEADS], r["w_in"][:, 6 * D + HEADS:]
    r["w_bd"] = bd.reshape(DC, P, -1).transpose(1, 0, 2)
    g = a["gdn_conv_w"][0]
    conv = np.concatenate([g[:, D:2 * D], g[:, 0:D], g[:, 2 * D:], a["ab_conv_w"][0]], axis=1)
    r["conv_w"] = conv.reshape(CONV, 32, P).transpose(2, 1, 0)
    r["conv_b"] = tile(a["ab_conv_b"][0])
    w = np.stack([a["lru_w_r"][0], a["lru_w_i"][0]])
    r["lru_w"] = w.reshape(2, 4, 2, P, 2 * P).transpose(3, 0, 1, 2, 4).reshape(P, DC, BLOCK)
    r["lru_b"] = np.concatenate([tile(a["lru_b_r"][0]), tile(a["lru_b_i"][0])], axis=1)
    r["lru_lam"] = tile(a["lru_lambda"][0])
    r["head_par"] = np.stack([a["gdn_a_log"][0], a["gdn_dt_bias"][0]], axis=1)
    r["norm_w"] = a["gdn_norm_w"][0][:, None]
    r["w_out"] = a["ab_w_out"][0]
    ln = []
    for layer in range(DEPTH):
        for kind in ("mix", "ffn"):
            ln += [tile(a[f"ln_{kind}_g"][layer]), tile(a[f"ln_{kind}_b"][layer])]
    r["ln_par"] = np.concatenate(ln, axis=1)
    r["router_w"] = a["moe_w_router"].reshape(DEPTH, DC, P, E).transpose(0, 2, 1, 3)
    r["router_b"] = a["moe_router_bias"]
    r["moe_gate"], r["moe_up"], r["moe_down"] = a["moe_w_gate"], a["moe_w_up"], a["moe_w_down"]
    r["sh_gate"], r["sh_up"], r["sh_down"] = a["moe_shared_w_gate"], a["moe_shared_w_up"], a["moe_shared_w_down"]
    st = lambda v: v.reshape(S5_TILES, P).T
    dt = np.repeat(a["s5_log_dt"][0][:, None], STATES, axis=1)
    r["s5_lam"] = np.stack([st(a["s5_lambda_re"][0]), st(a["s5_lambda_im"][0]), st(dt)], axis=1)
    for name in ("re", "im"):
        b = a[f"s5_b_{name}"][0].reshape(DC, 4, 2, STATES, 16)
        wide = np.zeros((4, 2, 16, DC, 2, STATES), b.dtype)
        c = a[f"s5_c_{name}"][0].reshape(S5_TILES, 2, 16, STATES)
        cw = np.zeros((2, STATES, S5_TILES, 2, 16), c.dtype)
        for g2 in range(2):
            wide[:, g2, :, :, g2, :] = b[:, :, g2].transpose(1, 3, 0, 2)
            cw[g2, :, :, g2, :] = c[:, g2].transpose(2, 0, 1)
        r[f"s5_b_{name}"] = wide.reshape(P, DC, P)
        r[f"s5_c_{name}"] = cw.reshape(P, S5_TILES, 32)
    r["s5_d"] = tile(a["s5_d"][0])
    r["s5_w_out"] = a["s5_w_out"][0]
    return {n: np.ascontiguousarray(v) for n, v in r.items()}


def kernel(**inputs):
    import concourse.bacc as _bacc
    from concourse.bass_utils import run_bass_kernel_spmd as _run

    arrays = layout(inputs) | constants()
    nc = _bacc.Bacc("TRN2", target_bir_lowering=False, num_devices=1)
    k = {n: nc.dram_tensor(f"in_{n}", v.shape, mybir.dt.from_np(v.dtype), kind="ExternalInput").ap()
         for n, v in arrays.items()}
    k["rows_dram"] = nc.dram_tensor("rows_dram", (T, D), F32, kind="Internal").ap()
    k["s5_table_dram"] = nc.dram_tensor("s5_table_dram", (P, S5_TILES, 2, T), F32, kind="Internal").ap()
    out = nc.dram_tensor("out", (1, SEQ, D), F32, kind="ExternalOutput").ap()
    trunk(nc, k, out)
    r = _run(nc, [{f"in_{n}": v for n, v in arrays.items()}], core_ids=[0])
    return r.results[0]["out"]
```
